# Optimizing a Trainium2 kernel written in Bass

```python
import functools
import jax, jax.numpy as jnp
from jax import lax
import numpy as np

D_MODEL = 1024
BATCH = 1
SEQ = 2048
DEPTH = 2
DEC_BATCH = 8
DEC_SEQ = 1
PAST_LEN = 8192
PAGE_SIZE = 128

N_A = DEPTH // 2
N_B = DEPTH - N_A
HEAD_DIM = 128
D_CONV = D_MODEL
CONV_W = 3
DIL_CONFIGS = ((128, 1), (512, 4), (2048, 16))
N_GROUPS = len(DIL_CONFIGS)
DIL_HEADS = 4
D_DIL = DIL_HEADS * HEAD_DIM
MEM_LEN = 256
MEM_HEADS = 4
D_MEM = MEM_HEADS * HEAD_DIM
BAND_BLOCK = 128
EPS = 1e-6
NEG = -1e30
D_IN_A = 4 * D_CONV + 2 * D_MEM
D_IN_B = N_GROUPS * D_DIL + D_DIL + 2 * D_MEM
D_KV = N_GROUPS * 2 * D_DIL

kernel_name = "yoco_shortconv_dilated_swa_memxattn_step"

def rms_norm(x, g):
    xf = x.astype(jnp.float32)
    y = xf * lax.rsqrt(jnp.mean(xf * xf, axis=-1, keepdims=True) + EPS) * g.astype(jnp.float32)
    return y.astype(x.dtype)

def mem_kv_proj(mem, norm_g, w, k_norm_g):
    b, m, _ = mem.shape
    kv = (rms_norm(mem, norm_g) @ w).reshape(b, m, 2, MEM_HEADS, HEAD_DIM)
    k = rms_norm(kv[:, :, 0], k_norm_g)
    return jnp.stack([k, kv[:, :, 1]], axis=2)

def mem_attend(q, mem_kv):
    s = jnp.einsum('bthe,bmhe->bhtm', q, mem_kv[:, :, 0], preferred_element_type=jnp.float32)
    p = jax.nn.softmax(s, axis=-1)
    return jnp.einsum('bhtm,bmhe->bthe', p, mem_kv[:, :, 1].astype(jnp.float32)).astype(q.dtype)

def shared_kv(x, kv_norm_g, w_kv, k_norm_g):
    b, t, _ = x.shape
    kv = (rms_norm(x, kv_norm_g) @ w_kv).reshape(b, t, N_GROUPS, 2, DIL_HEADS, HEAD_DIM)
    k = rms_norm(kv[:, :, :, 0], k_norm_g[:, None, :])
    return k, kv[:, :, :, 1]

def band_attend(q, k, v, d, nw):
    b, s_len, h, e = q.shape
    span = d * BAND_BLOCK
    s_pad = -(-s_len // span) * span
    n = s_pad // d
    nb = n // BAND_BLOCK

    def to_res(a):
        a = jnp.pad(a, ((0, 0), (0, s_pad - s_len), (0, 0), (0, 0)))
        a = a.reshape(b, n, d, h, e).transpose(0, 2, 1, 3, 4)
        return a.reshape(b, d, nb, BAND_BLOCK, h, e)

    def with_prev(a):
        prev = jnp.pad(a, ((0, 0), (0, 0), (1, 0), (0, 0), (0, 0), (0, 0)))[:, :, :-1]
        return jnp.concatenate([prev, a], axis=3)

    qb = to_res(q)
    kk = with_prev(to_res(k))
    vv = with_prev(to_res(v))
    s = jnp.einsum('brnqhe,brnkhe->brnhqk', qb, kk, preferred_element_type=jnp.float32)
    qi = jnp.arange(BAND_BLOCK)[:, None]
    kj = jnp.arange(2 * BAND_BLOCK)[None, :]
    rel = qi + BAND_BLOCK - kj
    valid = (rel >= 0) & (rel <= nw)
    has_prev = (jnp.arange(nb)[:, None, None] > 0) | (kj >= BAND_BLOCK)[None]
    valid = valid[None] & has_prev
    s = jnp.where(valid[None, None, :, None], s, NEG)
    m = jnp.max(s, axis=-1, keepdims=True)
    p = jnp.exp(s - m)
    l = jnp.sum(p, axis=-1, keepdims=True)
    o = jnp.einsum('brnhqk,brnkhe->brnqhe', p / l, vv.astype(jnp.float32)).astype(q.dtype)
    lse = (m + jnp.log(l))[..., 0]
    o = o.reshape(b, d, n, h, e).transpose(0, 2, 1, 3, 4).reshape(b, s_pad, h, e)[:, :s_len]
    lse = lse.transpose(0, 1, 2, 4, 3).reshape(b, d, n, h).transpose(0, 2, 1, 3)
    lse = lse.reshape(b, s_pad, h)[:, :s_len]
    return o, lse

def strided_gather_attend(q, kk, vv, d, nw):
    t_len = q.shape[1]
    l_len = kk.shape[1] - t_len
    rows = l_len + jnp.arange(t_len)[:, None] - d * jnp.arange(nw + 1)[None, :]
    valid = rows >= 0
    idx = jnp.maximum(rows, 0)
    kg = kk[:, idx]
    vg = vv[:, idx]
    s = jnp.einsum('bthe,btshe->bhts', q, kg, preferred_element_type=jnp.float32)
    s = jnp.where(valid[None, None], s, NEG)
    m = jnp.max(s, axis=-1, keepdims=True)
    p = jnp.exp(s - m)
    l = jnp.sum(p, axis=-1, keepdims=True)
    o = jnp.einsum('bhts,btshe->bthe', p / l, vg.astype(jnp.float32)).astype(q.dtype)
    lse = (m + jnp.log(l))[..., 0].transpose(0, 2, 1)
    return o, lse

def combine_groups(outs, lses):
    o = jnp.stack(outs, axis=2).astype(jnp.float32)
    w = jax.nn.softmax(jnp.stack(lses, axis=2), axis=2)
    return jnp.sum(o * w[..., None], axis=2).astype(outs[0].dtype)

def dilated_prompt(q, k, v):
    outs, lses = [], []
    for g, (win, d) in enumerate(DIL_CONFIGS):
        o, lse = band_attend(q[:, :, g], k[:, :, g], v[:, :, g], d, win // d)
        outs.append(o)
        lses.append(lse)
    return combine_groups(outs, lses)

def dilated_sample(q, k_new, v_new, bufs):
    outs, lses = [], []
    for g, (win, d) in enumerate(DIL_CONFIGS):
        kk = jnp.concatenate([bufs[g][:, :, 0], k_new[:, :, g]], axis=1)
        vv = jnp.concatenate([bufs[g][:, :, 1], v_new[:, :, g]], axis=1)
        o, lse = strided_gather_attend(q[:, :, g], kk, vv, d, win // d)
        outs.append(o)
        lses.append(lse)
    return combine_groups(outs, lses)

def conv_layer(x, conv_state, mem_kv, norm_g, w_in, conv_w, mem_q_g, w_out):
    b, t, _ = x.shape
    z = rms_norm(x, norm_g) @ w_in
    hh, c, bg, g, mq, mg = jnp.split(
        z, [D_CONV, 2 * D_CONV, 3 * D_CONV, 4 * D_CONV, 4 * D_CONV + D_MEM], axis=-1)
    u = c * hh
    ext = jnp.concatenate([conv_state, u], axis=1)
    y = sum(conv_w[j] * ext[:, j:j + t] for j in range(CONV_W))
    conv_out = jax.nn.silu(g) * bg * y
    q = rms_norm(mq.reshape(b, t, MEM_HEADS, HEAD_DIM), mem_q_g) * (HEAD_DIM ** -0.5)
    mem_out = mem_attend(q, mem_kv).reshape(b, t, D_MEM) * jax.nn.silu(mg)
    out = jnp.concatenate([conv_out, mem_out], axis=-1) @ w_out
    return x + out, ext[:, -(CONV_W - 1):]

def dil_layer(x, dil_fn, mem_kv, norm_g, w_in, q_norm_g, mem_q_g, w_out):
    b, t, _ = x.shape
    z = rms_norm(x, norm_g) @ w_in
    qd, gd, mq, mg = jnp.split(
        z, [N_GROUPS * D_DIL, (N_GROUPS + 1) * D_DIL, (N_GROUPS + 1) * D_DIL + D_MEM], axis=-1)
    qd = rms_norm(qd.reshape(b, t, N_GROUPS, DIL_HEADS, HEAD_DIM), q_norm_g[:, None, :]) * (HEAD_DIM ** -0.5)
    dil_out = dil_fn(qd).reshape(b, t, D_DIL) * jax.nn.silu(gd)
    q = rms_norm(mq.reshape(b, t, MEM_HEADS, HEAD_DIM), mem_q_g) * (HEAD_DIM ** -0.5)
    mem_out = mem_attend(q, mem_kv).reshape(b, t, D_MEM) * jax.nn.silu(mg)
    out = jnp.concatenate([dil_out, mem_out], axis=-1) @ w_out
    return x + out

def setup_inputs(seed: int = 0) -> dict:
    key = jax.random.key(seed)
    ks = jax.random.split(key, 24)
    f32 = jnp.float32

    def nrm(k, shape, scale=1.0):
        return jax.random.normal(k, shape, f32) * scale

    def gain(k, shape):
        return 1.0 + 0.1 * jax.random.normal(k, shape, f32)

    win = [min(w, PAST_LEN) for w, _ in DIL_CONFIGS]
    return {
        "x_prompt": nrm(ks[0], (BATCH, SEQ, D_MODEL)),
        "x_sample": nrm(ks[1], (DEC_BATCH, DEC_SEQ, D_MODEL)),
        "cache_mem_kv": nrm(ks[2], (DEPTH, DEC_BATCH, MEM_LEN, 2, MEM_HEADS, HEAD_DIM)),
        "state_conv": nrm(ks[3], (N_A, DEC_BATCH, CONV_W - 1, D_CONV)),
        "cache_dil0_kv": nrm(ks[4], (DEC_BATCH, win[0], 2, DIL_HEADS, HEAD_DIM)),
        "cache_dil1_kv": nrm(ks[5], (DEC_BATCH, win[1], 2, DIL_HEADS, HEAD_DIM)),
        "cache_dil2_kv": nrm(ks[6], (DEC_BATCH, win[2], 2, DIL_HEADS, HEAD_DIM)),
        "mem_prompt": nrm(ks[7], (BATCH, MEM_LEN, D_MODEL)),
        "norm_a": gain(ks[8], (N_A, D_MODEL)),
        "w_in_a": nrm(ks[9], (N_A, D_MODEL, D_IN_A), D_MODEL ** -0.5),
        "conv_w_a": nrm(ks[10], (N_A, CONV_W, D_CONV), CONV_W ** -0.5),
        "w_out_a": nrm(ks[11], (N_A, D_CONV + D_MEM, D_MODEL), (D_CONV + D_MEM) ** -0.5),
        "norm_b": gain(ks[12], (N_B, D_MODEL)),
        "w_in_b": nrm(ks[13], (N_B, D_MODEL, D_IN_B), D_MODEL ** -0.5),
        "q_norm_b": gain(ks[14], (N_B, N_GROUPS, HEAD_DIM)),
        "w_out_b": nrm(ks[15], (N_B, D_DIL + D_MEM, D_MODEL), (D_DIL + D_MEM) ** -0.5),
        "kv_norm": gain(ks[16], (D_MODEL,)),
        "w_kv": nrm(ks[17], (D_MODEL, D_KV), D_MODEL ** -0.5),
        "k_norm_dil": gain(ks[18], (N_GROUPS, HEAD_DIM)),
        "mem_norm": gain(ks[19], (DEPTH, D_MODEL)),
        "w_mem_kv": nrm(ks[20], (DEPTH, D_MODEL, 2 * D_MEM), D_MODEL ** -0.5),
        "mem_k_norm": gain(ks[21], (DEPTH, HEAD_DIM)),
        "mem_q_norm": gain(ks[22], (DEPTH, HEAD_DIM)),
    }

def reference(x_prompt, x_sample, cache_mem_kv, state_conv, cache_dil0_kv, cache_dil1_kv,
              cache_dil2_kv, mem_prompt, norm_a, w_in_a, conv_w_a, w_out_a, norm_b, w_in_b,
              q_norm_b, w_out_b, kv_norm, w_kv, k_norm_dil, mem_norm, w_mem_kv, mem_k_norm,
              mem_q_norm):
    mem_kv_p = jnp.stack([mem_kv_proj(mem_prompt, mem_norm[l], w_mem_kv[l], mem_k_norm[l])
                          for l in range(DEPTH)])
    xp, xs = x_prompt, x_sample
    s_len = x_prompt.shape[1]
    conv_p, conv_s = [], []
    dil_p_state, dil_s_state = [], []
    dil_p_fn = dil_s_fn = None
    for l in range(DEPTH):
        if l < N_A:
            a = l
            zero_state = jnp.zeros((xp.shape[0], CONV_W - 1, D_CONV), xp.dtype)
            xp, cp = conv_layer(xp, zero_state, mem_kv_p[l], norm_a[a], w_in_a[a], conv_w_a[a],
                                mem_q_norm[l], w_out_a[a])
            xs, cs = conv_layer(xs, state_conv[a], cache_mem_kv[l], norm_a[a], w_in_a[a],
                                conv_w_a[a], mem_q_norm[l], w_out_a[a])
            conv_p.append(cp)
            conv_s.append(cs)
        else:
            if l == N_A:
                kp, vp = shared_kv(xp, kv_norm, w_kv, k_norm_dil)
                ks_, vs_ = shared_kv(xs, kv_norm, w_kv, k_norm_dil)
                dil_p_fn = functools.partial(dilated_prompt, k=kp, v=vp)
                dil_s_fn = functools.partial(dilated_sample, k_new=ks_, v_new=vs_,
                                             bufs=(cache_dil0_kv, cache_dil1_kv, cache_dil2_kv))
                for g, (win, _) in enumerate(DIL_CONFIGS):
                    keep = min(win, s_len)
                    dil_p_state.append(jnp.stack([kp[:, -keep:, g], vp[:, -keep:, g]], axis=2))
                    dil_s_state.append(jnp.stack([ks_[:, :, g], vs_[:, :, g]], axis=2))
            bl = l - N_A
            xp = dil_layer(xp, dil_p_fn, mem_kv_p[l], norm_b[bl], w_in_b[bl], q_norm_b[bl],
                           mem_q_norm[l], w_out_b[bl])
            xs = dil_layer(xs, dil_s_fn, cache_mem_kv[l], norm_b[bl], w_in_b[bl], q_norm_b[bl],
                           mem_q_norm[l], w_out_b[bl])
    conv_prompt = jnp.stack(conv_p)
    conv_sample = jnp.stack(conv_s)
    return (xp, xs, mem_kv_p, conv_prompt, conv_sample,
            dil_p_state[0], dil_p_state[1], dil_p_state[2],
            dil_s_state[0], dil_s_state[1], dil_s_state[2])


_drawn_inputs = setup_inputs


def setup_inputs(seed=0):
    import zlib

    import numpy as np

    out = dict(_drawn_inputs(seed))
    spreads = {}
    factors = {'cache_dil0_kv': 3.062,
     'cache_dil1_kv': 2.984,
     'cache_dil2_kv': 3.062,
     'norm_b': 7.015,
     'q_norm_b': 8.0,
     'mem_q_norm': 8.0}
    for name, (base, spread) in spreads.items():
        noise = np.random.default_rng([zlib.crc32(name.encode()), seed]).standard_normal(out[name].shape)
        drawn = base * np.exp(spread * noise) if base else spread * noise
        out[name] = __import__('jax').numpy.asarray(drawn.astype(out[name].dtype))
    for name, factor in factors.items():
        out[name] = (out[name] * factor).astype(out[name].dtype)
    return out
```

```python
from contextlib import ExitStack

import concourse.bass as bass
import numpy as np
from concourse import mybir

F32 = mybir.dt.float32
F32R = mybir.dt.float32r
ACT = mybir.ActivationFunctionType
ALU = mybir.AluOpType
AX = mybir.AxisListType

P = 128
D = 1024
KD = D // P
T = 2048
NT = T // P
S = 8
TS = T + S
HD = 128
H = 4
C = H * HD
MEM = 256
MT = MEM // P
TB = 4
NW = TB * C // T * 512
EPS = 1e-6
NEG = -1e30
SCALE = HD ** -0.5
DIL = ((128, 1), (512, 4), (2048, 16))
OW = C + 2 * H
NCONV = KD


def ds(start, n):
    return bass.ds(start, n)


def pairs(eng, n, body):
    for u in range(2):
        body(0, u, True)
    if n > 2:
        with eng.Fori(1, n // 2) as q:
            for u in range(2):
                body(q, u, False)


class Core:

    def __init__(self, nc, ctx, io):
        self.nc, self.ctx, self.io = nc, ctx, io
        self.ps = ctx.enter_context(nc.psum_tensor("ps", [P, 8, 512], F32))
        self.ident = ctx.enter_context(nc.sbuf_tensor("ident", [P, P], F32))

    def sems(self, stack, tag, names):
        sems = [self.nc.alloc_semaphore(f"{tag}_{n}") for n in names.split()]
        stack.callback(self.nc.all_engine_barrier)
        stack.callback(self.nc.clear_and_free_semaphores, sems)
        return sems

    def sb(self, stack, name, shape, dt=F32):
        return stack.enter_context(self.nc.sbuf_tensor(name, shape, dt))


def setup_stage(core, gains):
    nc = core.nc
    with ExitStack() as st:
        zeroed, made, loaded = core.sems(st, "setup", "zeroed made loaded")
        block = st.enter_context(nc.Block())

        @block.gpsimd
        def _(pool):
            pool.memset(core.ident[:, :], 0.0).then_inc(zeroed, 1)
            pool.wait_ge(zeroed, 1)
            pool.affine_select(out=core.ident[:, :], in_=core.ident[:, :], compare_op=ALU.not_equal,
                               fill=1.0, base=0, pattern=[[-1, P]], channel_multiplier=1).then_inc(made, 1)
            pool.wait_ge(made, 1)

        @block.sync
        def _(sp):
            sp.dma_start(gains[:, :], core.io["gain_cols"]).then_inc(loaded, 16)
            sp.wait_ge(loaded, 16)


def split_weight_chunk_act(act, raw, w_hi, gain):
    return act.activation(w_hi, raw, ACT.Copy, scale=gain)


def split_weight_chunk_dve(dve, raw, w_hi, w_lo, gain):
    return dve.scalar_tensor_tensor(out=w_lo, in0=raw, scalar=gain, in1=w_hi,
                                    op0=ALU.mult, op1=ALU.subtract)


def prep_stage(core, tag, x, x_s, xt_hi, xt_lo, w_src, w_hi, w_lo, gain):
    nc, ps, ident = core.nc, core.ps, core.ident
    with ExitStack() as st:
        xb = core.sb(st, f"{tag}_x", [P, 2, D])
        xn = core.sb(st, f"{tag}_xn", [P, 2, D])
        raw = core.sb(st, f"{tag}_raw", [P, 2, C])
        stat = core.sb(st, f"{tag}_stat", [P, 2, 4])
        (x_in0, x_in1, raw_in0, raw_in1, squared, rooted, inverted, scaled, turned, hi_done, lo_done,
         w_hi_done, w_lo_done) = core.sems(
            st, tag, "x_in0 x_in1 raw_in0 raw_in1 squared rooted inverted scaled turned hi_done lo_done "
                     "w_hi_done w_lo_done")
        x_in, raw_in = (x_in0, x_in1), (raw_in0, raw_in1)
        block = st.enter_context(nc.Block())
        N = NT + 1
        rows = lambda i: S if i == NT else P

        @block.sync
        def _(sp):
            def load(q, u, first):
                if not first:
                    sp.wait_ge(scaled, q * 2 + (u - 1))
                sp.dma_start(xb[:, u, :], x[ds(q * (2 * P) + u * P, P), :]).then_inc(x_in[u], 16)
            pairs(sp, NT, load)
            sp.wait_ge(scaled, NT - 1)
            sp.dma_start(xb[0:S, 0, :], x_s).then_inc(x_in[0], 16)
            for k in range(KD):
                if k >= 2:
                    sp.wait_ge(w_lo_done, k - 1)
                sp.dma_start(raw[:, k % 2, :], w_src[k * P:(k + 1) * P, :]).then_inc(raw_in[k % 2], 16)

        @block.scalar
        def _(act):
            def square(q, u, first, n=P):
                act.wait_ge(x_in[u], q * 16 + 16)
                if not first:
                    act.wait_ge(turned, q * 2 + (u - 1))
                act.activation(xn[0:n, u, :], xb[0:n, u, :], ACT.Square,
                               accum_out=stat[0:n, u, 0:1]).then_inc(squared, 1)
                act.wait_ge(squared, q * 2 + (u + 1))
                act.activation(stat[0:n, u, 1:2], stat[0:n, u, 0:1], ACT.Sqrt, scale=1.0 / D,
                               bias=EPS).then_inc(rooted, 1)

            def high(q, u, at, n=P):
                act.wait_ge(turned, q * 2 + (u + 1))
                act.activation(xt_hi[:, :, ds(at, n)],
                               ps[:, 2 * u:2 * u + 2, :].rearrange("p a (b t) -> p (a b) t", t=P)[:, :, 0:n],
                               ACT.Copy).then_inc(hi_done, 1)

            def step(q, u, first):
                square(q, u, first)
                if u:
                    high(q, 0, q * (2 * P))
                elif not first:
                    high(q - 1, 1, q * (2 * P) - P)
            pairs(act, NT, step)
            square(NT // 2, 0, False, S)
            high(NT // 2 - 1, 1, T - P)
            high(NT // 2, 0, T, S)
            for k in range(KD):
                act.wait_ge(raw_in[k % 2], 16 * (k // 2 + 1))
                split_weight_chunk_act(act, raw[:, k % 2, :], w_hi[:, k, :], gain[:, k:k + 1]).then_inc(w_hi_done, 1)

        @block.vector
        def _(dve):
            def scale(q, u, first, n=P):
                dve.wait_ge(rooted, q * 2 + (u + 1))
                dve.reciprocal(stat[0:n, u, 2:3], stat[0:n, u, 1:2]).then_inc(inverted, 1)
                dve.wait_ge(inverted, q * 2 + (u + 1))
                dve.tensor_scalar(xn[0:n, u, :], xb[0:n, u, :], stat[0:n, u, 2:3], None,
                                  ALU.mult).then_inc(scaled, 1)

            def low(q, u, at, n=P):
                dve.wait_ge(hi_done, q * 2 + (u + 1))
                dve.tensor_tensor(xt_lo[:, :, ds(at, n)],
                                  ps[:, 2 * u:2 * u + 2, :].rearrange("p a (b t) -> p (a b) t", t=P)[:, :, 0:n],
                                  xt_hi[:, :, ds(at, n)], ALU.subtract).then_inc(lo_done, 1)

            def step(q, u, first):
                scale(q, u, first)
                if u:
                    low(q, 0, q * (2 * P))
                elif not first:
                    low(q - 1, 1, q * (2 * P) - P)
            pairs(dve, NT, step)
            scale(NT // 2, 0, False, S)
            low(NT // 2 - 1, 1, T - P)
            low(NT // 2, 0, T, S)
            for k in range(KD):
                dve.wait_ge(w_hi_done, k + 1)
                split_weight_chunk_dve(dve, raw[:, k % 2, :], w_hi[:, k, :], w_lo[:, k, :],
                                       gain[:, k:k + 1]).then_inc(w_lo_done, 1)
            dve.wait_ge(w_lo_done, KD)

        @block.tensor
        def _(pe):
            def step(q, u, first, n=P):
                pe.wait_ge(scaled, q * 2 + (u + 1))
                if not first:
                    pe.wait_ge(lo_done, q * 2 + (u - 1))
                for k in range(KD):
                    at = (k % 4) * P
                    t = pe.transpose(ps[:, 2 * u + k // 4, at:at + n], xn[0:n, u, k * P:(k + 1) * P],
                                     ident[0:n, 0:n])
                t.then_inc(turned, 1)
            pairs(pe, NT, step)
            step(NT // 2, 0, False, S)


def conv_stage(core, w_all, xt_hi, xt_lo, wh, wl, gain):
    nc, ps, io = core.nc, core.ps, core.io
    conv_t, tail, tail_s = io["conv_t"], io["tail"], io["tail_s"]
    tag = "conv"
    NSTEP = TB + 1
    OPS = 7
    with ExitStack() as st:
        raw = core.sb(st, "conv_raw", [P, 2, C])
        u = core.sb(st, "conv_u", [P, 2, 2 + 512])
        us = core.sb(st, "conv_us", [P, 3, S])
        t = core.sb(st, "conv_gate", [P, 512])
        o = core.sb(st, "conv_o", [P, 512])
        small = core.sb(st, "conv_small", [P, 2, 3 + 2 * S])
        (raw_in0, raw_in1, small_in0, small_in1, w_hi_done, w_lo_done, multiplied, c_copied, tapped,
         gated, ops, o_out, tails_out) = core.sems(
            st, tag, "raw_in0 raw_in1 small_in0 small_in1 w_hi_done w_lo_done multiplied c_copied "
                     "tapped gated ops o_out tails_out")
        raw_in, small_in = (raw_in0, raw_in1), (small_in0, small_in1)
        block = st.enter_context(nc.Block())

        def loop(eng, body):
            body(0, True)
            with eng.Fori(1, NCONV // 2) as q:
                body(q, False)

        @block.sync
        def _(sp):
            def body(q, first):
                for j in range(2):
                    if not first:
                        sp.wait_ge(ops, (q * 2 + (j - 1)) * (NSTEP * OPS))
                    sp.dma_start(small[:, j, :], io["conv_small"][ds((q * 2 + j) * P, P), :]).then_inc(small_in[j], 16)
                    for k in range(KD):
                        if not (first and j == 0 and k < 2):
                            sp.wait_ge(w_lo_done, q * (2 * KD) + (j * KD + k - 1))
                        sp.dma_start(raw[:, k % 2, :],
                                     w_all[ds((q * 2 + (j + 1)) * D + k * P, P), :]).then_inc(raw_in[k % 2], 16)
            loop(sp, body)

        @block.gpsimd
        def _(pool):
            def body(q, first):
                for j in range(2):
                    for b in range(NSTEP):
                        step = q * (2 * NSTEP) + (j * NSTEP + b)
                        n = 512 if b < TB else S
                        pool.wait_ge(ops, (step + 1) * OPS)
                        pool.dma_start(conv_t[ds((q * 2 + j) * P, P), b * 512:b * 512 + n],
                                       o[:, 0:n]).then_inc(o_out, 16)
                        if b == TB - 1:
                            pool.dma_start(tail[ds((q * 2 + j) * P, P), :],
                                           u[:, (j * NSTEP + b) % 2, 512:514]).then_inc(tails_out, 16)
                        if b == TB:
                            pool.dma_start(tail_s[ds((q * 2 + j) * P, P), :],
                                           us[:, 1:3, :].rearrange("p a s -> p (a s)")).then_inc(tails_out, 16)
            loop(pool, body)
            pool.wait_ge(o_out, 16 * NCONV * NSTEP)
            pool.wait_ge(tails_out, 32 * NCONV)

        @block.scalar
        def _(act):
            def body(q, first):
                for j in range(2):
                    for b in range(NSTEP):
                        step = q * (2 * NSTEP) + (j * NSTEP + b)
                        slot = (j * NSTEP + b) % 2
                        sample = b == TB
                        n = S if sample else 512
                        u_new = us[:, 2, :] if sample else u[:, slot, 2:514]
                        very_first = first and j == 0 and b == 0
                        act.wait_ge(multiplied, step * 4 + 1)
                        if not very_first:
                            act.wait_ge(ops, step * OPS)
                        if b in (0, TB) and not (first and j == 0):
                            act.wait_ge(tails_out, (q * 2 + j) * 32)
                        act.activation(u_new, ps[:, slot * 4, 0:n], ACT.Copy).then_inc(c_copied, 1)
                        act.wait_ge(ops, step * OPS + 2)
                        if not very_first:
                            act.wait_ge(o_out, step * 16)
                        if b == 0:
                            act.wait_ge(small_in[j], q * 16 + 16)
                        act.activation(o[:, 0:n], u_new, ACT.Copy, scale=small[:, j, 2:3]).then_inc(tapped, 1)
                        act.wait_ge(multiplied, step * 4 + 3)
                        act.activation(t[:, 0:n], ps[:, slot * 4 + 2, 0:n], ACT.Sigmoid).then_inc(gated, 1)
                        for k in range(2 * b, min(2 * b + 2, KD)):
                            chunk = q * (2 * KD) + (j * KD + k)
                            act.wait_ge(raw_in[k % 2], q * (KD * 16) + (j * (KD // 2) + k // 2 + 1) * 16)
                            split_weight_chunk_act(act, raw[:, k % 2, :], wh[1 - j][:, k, :],
                                                   gain[:, k:k + 1]).then_inc(w_hi_done, 1)
            loop(act, body)

        @block.vector
        def _(dve):
            def body(q, first):
                for j in range(2):
                    for b in range(NSTEP):
                        step = q * (2 * NSTEP) + (j * NSTEP + b)
                        slot = (j * NSTEP + b) % 2
                        sample = b == TB
                        n = S if sample else 512
                        u_new = us[:, 2, :] if sample else u[:, slot, 2:514]
                        u_one = us[:, 1, :] if sample else u[:, slot, 1:513]
                        u_two = us[:, 0, :] if sample else u[:, slot, 0:512]
                        if b == 0:
                            dve.wait_ge(small_in[j], q * 16 + 16)
                        if sample:
                            if not (first and j == 0):
                                dve.wait_ge(tails_out, (q * 2 + j) * 32)
                            dve.tensor_copy(us[:, 0:2, :].rearrange("p a s -> p (a s)"),
                                            small[:, j, 3:3 + 2 * S]).then_inc(ops, 1)
                        elif b == 0:
                            dve.memset(u[:, slot, 0:2], 0.0).then_inc(ops, 1)
                        else:
                            dve.tensor_copy(u[:, slot, 0:2], u[:, 1 - slot, 512:514]).then_inc(ops, 1)
                        dve.wait_ge(c_copied, step + 1)
                        dve.wait_ge(multiplied, step * 4 + 2)
                        dve.tensor_tensor(u_new, ps[:, slot * 4 + 1, 0:n], u_new, ALU.mult).then_inc(ops, 1)
                        dve.wait_ge(tapped, step + 1)
                        dve.wait_ge(ops, step * OPS + 2)
                        dve.scalar_tensor_tensor(out=o[:, 0:n], in0=u_one, scalar=small[:, j, 1:2],
                                                 in1=o[:, 0:n], op0=ALU.mult, op1=ALU.add).then_inc(ops, 1)
                        dve.wait_ge(ops, step * OPS + 3)
                        dve.scalar_tensor_tensor(out=o[:, 0:n], in0=u_two, scalar=small[:, j, 0:1],
                                                 in1=o[:, 0:n], op0=ALU.mult, op1=ALU.add).then_inc(ops, 1)
                        dve.wait_ge(gated, step + 1)
                        dve.tensor_tensor(t[:, 0:n], ps[:, slot * 4 + 2, 0:n], t[:, 0:n], ALU.mult).then_inc(ops, 1)
                        dve.wait_ge(multiplied, step * 4 + 4)
                        dve.wait_ge(ops, step * OPS + 5)
                        dve.tensor_tensor(t[:, 0:n], ps[:, slot * 4 + 3, 0:n], t[:, 0:n], ALU.mult).then_inc(ops, 1)
                        dve.wait_ge(ops, step * OPS + 6)
                        dve.tensor_tensor(o[:, 0:n], o[:, 0:n], t[:, 0:n], ALU.mult).then_inc(ops, 1)
                        for k in range(2 * b, min(2 * b + 2, KD)):
                            dve.wait_ge(w_hi_done, q * (2 * KD) + (j * KD + k + 1))
                            split_weight_chunk_dve(dve, raw[:, k % 2, :], wh[1 - j][:, k, :], wl[1 - j][:, k, :],
                                                   gain[:, k:k + 1]).then_inc(w_lo_done, 1)
            loop(dve, body)
            dve.wait_ge(w_lo_done, NCONV * KD)

        @block.tensor
        def _(pe):
            def body(q, first):
                for j in range(2):
                    if not (first and j == 0):
                        pe.wait_ge(w_lo_done, (q * 2 + j) * KD)
                    for b in range(NSTEP):
                        slot = (j * NSTEP + b) % 2
                        step = q * (2 * NSTEP) + (j * NSTEP + b)
                        if not (first and j == 0 and b < 2):
                            pe.wait_ge(ops, (step - 1) * OPS)
                        n = 512 if b < TB else S
                        for part in range(4):
                            acc = ps[:, slot * 4 + part, 0:n]
                            for k in range(KD):
                                a_hi = wh[j][:, k, part * P:(part + 1) * P]
                                a_lo = wl[j][:, k, part * P:(part + 1) * P]
                                x_hi = xt_hi[:, k, b * 512:b * 512 + n]
                                x_lo = xt_lo[:, k, b * 512:b * 512 + n]
                                pe.matmul(acc, a_hi, x_hi, start=(k == 0), stop=False)
                                pe.matmul(acc, a_hi, x_lo, start=False, stop=False)
                                m = pe.matmul(acc, a_lo, x_hi, start=False, stop=(k == KD - 1))
                            m.then_inc(multiplied, 1)
            loop(pe, body)


def tokens_stage(core, tag, w_all, blocks, xt_hi, xt_lo, wh, wl):
    nc, ps, io = core.nc, core.ps, core.io
    N = NT + 1
    count = lambda b, kind: sum(blk[0] == kind for blk in blocks[:b])
    with ExitStack() as st:
        raw = core.sb(st, f"{tag}_raw", [P, 2, C])
        o = core.sb(st, f"{tag}_o", [P, 2, C])
        grow = core.sb(st, f"{tag}_grow", [P, C])
        stat = core.sb(st, f"{tag}_stat", [P, 2, 3, H])
        (raw_in0, raw_in1, grow_in, w_hi_done, w_lo_done, multiplied, squared, acted, inverted, o_done,
         o_out0, o_out1) = core.sems(
            st, tag, "raw_in0 raw_in1 grow_in w_hi_done w_lo_done multiplied squared acted inverted "
                     "o_done o_out0 o_out1")
        raw_in, o_out = (raw_in0, raw_in1), (o_out0, o_out1)
        block = st.enter_context(nc.Block())
        rows = lambda i: P if i < NT else S

        @block.sync
        def _(sp):
            for b, (kind, dst, gain, g) in enumerate(blocks):
                if kind == "norm":
                    if b:
                        sp.wait_ge(o_done, b * N)
                    sp.dma_start(grow[:, :], io["gain_rows"][g:g + 1, :].to_broadcast([P, C])).then_inc(grow_in, 16)
                if gain is not None:
                    for k in range(KD):
                        if b * KD + k >= 2:
                            sp.wait_ge(w_lo_done, b * KD + k - 1)
                        sp.dma_start(raw[:, k % 2, :], w_all[b * D + k * P:b * D + (k + 1) * P, :]
                                     ).then_inc(raw_in[k % 2], 16)

        @block.gpsimd
        def _(pool):
            for b, (kind, dst, gain, g) in enumerate(blocks):
                for i in range(N):
                    n, tile = rows(i), b * N + i
                    pool.wait_ge(o_done, tile + 1)
                    pool.dma_start(dst[i * P:i * P + n, :], o[0:n, tile % 2, :]).then_inc(o_out[tile % 2], 16)
            for slot in range(2):
                pool.wait_ge(o_out[slot], 16 * ((len(blocks) * N + 1 - slot) // 2))

        @block.scalar
        def _(act):
            for b, (kind, dst, gain, g) in enumerate(blocks):
                for i in range(N):
                    n, tile = rows(i), b * N + i
                    slot = tile % 2
                    act.wait_ge(multiplied, tile + 1)
                    if kind != "copy" and tile >= 2:
                        act.wait_ge(o_out[slot], 16 * (tile // 2))
                    if kind == "norm":
                        for h in range(H):
                            cols = slice(h * HD, (h + 1) * HD)
                            sq = act.activation(o[0:n, slot, cols], ps[0:n, slot, cols], ACT.Square,
                                                accum_out=stat[0:n, slot, 0, h:h + 1])
                        sq.then_inc(squared, 1)
                        act.wait_ge(squared, count(b, "norm") * N + i + 1)
                        act.activation(stat[0:n, slot, 1, :], stat[0:n, slot, 0, :], ACT.Sqrt, scale=1.0 / HD,
                                       bias=EPS).then_inc(acted, 1)
                    if kind == "silu":
                        act.activation(o[0:n, slot, :], ps[0:n, slot, :], ACT.Sigmoid).then_inc(acted, 1)
                    if gain is not None and i % 2 == 1:
                        k = i // 2
                        act.wait_ge(raw_in[k % 2], 16 * (b * KD // 2 + k // 2 + 1))
                        split_weight_chunk_act(act, raw[:, k % 2, :], wh[1 - b % 2][:, k, :],
                                               gain[:, k:k + 1]).then_inc(w_hi_done, 1)

        @block.vector
        def _(dve):
            for b, (kind, dst, gain, g) in enumerate(blocks):
                if kind == "norm":
                    dve.wait_ge(grow_in, 16 * (count(b, "norm") + 1))
                for i in range(N):
                    n, tile = rows(i), b * N + i
                    slot = tile % 2
                    if kind == "copy":
                        dve.wait_ge(multiplied, tile + 1)
                        if tile >= 2:
                            dve.wait_ge(o_out[slot], 16 * (tile // 2))
                        dve.tensor_copy(o[0:n, slot, :], ps[0:n, slot, :]).then_inc(o_done, 1)
                    else:
                        dve.wait_ge(acted, (b - count(b, "copy")) * N + i + 1)
                    if kind == "silu":
                        dve.tensor_tensor(o[0:n, slot, :], ps[0:n, slot, :], o[0:n, slot, :],
                                          ALU.mult).then_inc(o_done, 1)
                    if kind == "norm":
                        dve.reciprocal(stat[0:n, slot, 2, :], stat[0:n, slot, 1, :]).then_inc(inverted, 1)
                        dve.wait_ge(inverted, count(b, "norm") * N + i + 1)
                        for h in range(H):
                            cols = slice(h * HD, (h + 1) * HD)
                            m = dve.scalar_tensor_tensor(out=o[0:n, slot, cols], in0=ps[0:n, slot, cols],
                                                         scalar=stat[0:n, slot, 2, h:h + 1], in1=grow[0:n, cols],
                                                         op0=ALU.mult, op1=ALU.mult)
                        m.then_inc(o_done, 1)
                    if gain is not None and i % 2 == 1:
                        k = i // 2
                        dve.wait_ge(w_hi_done, b * KD + k + 1)
                        split_weight_chunk_dve(dve, raw[:, k % 2, :], wh[1 - b % 2][:, k, :],
                                               wl[1 - b % 2][:, k, :], gain[:, k:k + 1]).then_inc(w_lo_done, 1)

        @block.tensor
        def _(pe):
            for b in range(len(blocks)):
                if b:
                    pe.wait_ge(w_lo_done, b * KD)
                for i in range(N):
                    n, tile = rows(i), b * N + i
                    if tile >= 2:
                        pe.wait_ge(o_done, tile - 1)
                    acc = ps[0:n, tile % 2, :]
                    for k in range(KD):
                        x_hi = xt_hi[:, k, i * P:i * P + n]
                        x_lo = xt_lo[:, k, i * P:i * P + n]
                        pe.matmul(acc, x_hi, wh[b % 2][:, k, :], start=(k == 0), stop=False)
                        pe.matmul(acc, x_hi, wl[b % 2][:, k, :], start=False, stop=False)
                        m = pe.matmul(acc, x_lo, wh[b % 2][:, k, :], start=False, stop=(k == KD - 1))
                    m.then_inc(multiplied, 1)


def memkv_stage(core, layer, w_mem, out_kv, wo_src, wo_chunks, wo_hi, wo_lo, kt_hi, kt_lo, v_hi, v_lo,
                mem_gain, norm_row):
    nc, ps, io, ident = core.nc, core.ps, core.io, core.ident
    tag = f"memkv{layer}"
    NB = 2
    with ExitStack() as st:
        mem = core.sb(st, f"{tag}_mem", [P, MT, D])
        mn = core.sb(st, f"{tag}_mn", [P, MT, D])
        mt_hi = core.sb(st, f"{tag}_mthi", [P, KD, MEM], F32R)
        mt_lo = core.sb(st, f"{tag}_mtlo", [P, KD, MEM], F32R)
        raw = core.sb(st, f"{tag}_raw", [P, 4, C])
        mw_hi = core.sb(st, f"{tag}_mwhi", [P, 4, C], F32R)
        mw_lo = core.sb(st, f"{tag}_mwlo", [P, 4, C], F32R)
        kv = core.sb(st, f"{tag}_kv", [P, NB, MT, C])
        grow = core.sb(st, f"{tag}_grow", [P, C])
        stat = core.sb(st, f"{tag}_stat", [P, MT, 3, H + 1])
        names = ("mem_in grow_in raw_in0 raw_in1 raw_in2 raw_in3 squared rooted inverted scaled turned "
                 "hi_done lo_done w_hi_done w_lo_done multiplied ksquared krooted kinverted kv_done v_hi_done "
                 "kturned khi_done klo_done v_lo_done kv_out")
        (mem_in, grow_in, raw_in0, raw_in1, raw_in2, raw_in3, squared, rooted, inverted, scaled, turned,
         hi_done, lo_done, w_hi_done, w_lo_done, multiplied, ksquared, krooted, kinverted, kv_done, v_hi_done,
         kturned, khi_done, klo_done, v_lo_done, kv_out) = core.sems(st, tag, names)
        raw_in = (raw_in0, raw_in1, raw_in2, raw_in3)
        block = st.enter_context(nc.Block())
        MEMC = KD * NB
        TOTAL = MEMC + 2 * wo_chunks

        def chunk_source(c):
            if c < MEMC:
                k, b = c // NB, c % NB
                return w_mem[k * P:(k + 1) * P, b * C:(b + 1) * C]
            k, half = (c - MEMC) // 2, (c - MEMC) % 2
            return wo_src[k * P:(k + 1) * P, half * C:(half + 1) * C]

        def chunk_split(c):
            if c < MEMC:
                return mw_hi[:, c % 4, :], mw_lo[:, c % 4, :]
            k, half = (c - MEMC) // 2, (c - MEMC) % 2
            cols = slice(half * C, (half + 1) * C)
            return wo_hi[:, k, cols], wo_lo[:, k, cols]

        @block.sync
        def _(sp):
            sp.dma_start(mem[:, :, :], io["mem_prompt"].rearrange("(m p) d -> p m d", p=P)).then_inc(mem_in, 16)
            sp.dma_start(grow[:, :], io["gain_rows"][norm_row:norm_row + 1, :].to_broadcast([P, C])
                         ).then_inc(grow_in, 16)
            for c in range(TOTAL):
                if c >= 4:
                    sp.wait_ge(w_lo_done, c - 3)
                sp.dma_start(raw[:, c % 4, :], chunk_source(c)).then_inc(raw_in[c % 4], 16)

        @block.gpsimd
        def _(pool):
            for b in range(NB):
                for m in range(MT):
                    pool.wait_ge(kv_done, b * MT + m + 1)
                    pool.dma_start(out_kv[m * P:(m + 1) * P, b * C:(b + 1) * C], kv[:, b, m, :]
                                   ).then_inc(kv_out, 16)
            pool.wait_ge(kv_out, 16 * NB * MT)

        @block.scalar
        def _(act):
            act.wait_ge(mem_in, 16)
            for m in range(MT):
                act.activation(mn[:, m, :], mem[:, m, :], ACT.Square,
                               accum_out=stat[:, m, 0, H:H + 1]).then_inc(squared, 1)
            for m in range(MT):
                act.wait_ge(squared, m + 1)
                act.activation(stat[:, m, 1, H:H + 1], stat[:, m, 0, H:H + 1], ACT.Sqrt, scale=1.0 / D,
                               bias=EPS).then_inc(rooted, 1)
            for m in range(MT):
                act.wait_ge(turned, m + 1)
                act.activation(mt_hi[:, :, m * P:(m + 1) * P],
                               ps[:, 2 * m:2 * m + 2, :].rearrange("p a (b t) -> p (a b) t", t=P),
                               ACT.Copy).then_inc(hi_done, 1)

            def split(c):
                act.wait_ge(raw_in[c % 4], 16 * (c // 4 + 1))
                if 4 <= c < MEMC:
                    act.wait_ge(multiplied, c - 3)
                scale = mem_gain[:, c // NB:c // NB + 1] if c < MEMC else 1.0
                split_weight_chunk_act(act, raw[:, c % 4, :], chunk_split(c)[0], scale).then_inc(w_hi_done, 1)
            for c in range(MEMC):
                split(c)
            act.wait_ge(multiplied, MEMC)
            for m in range(MT):
                for h in range(H):
                    sq = act.activation(kv[:, 0, m, h * HD:(h + 1) * HD], ps[:, 4 + m, h * HD:(h + 1) * HD],
                                        ACT.Square, accum_out=stat[:, m, 0, h:h + 1])
                sq.then_inc(ksquared, 1)
            for m in range(MT):
                act.wait_ge(ksquared, m + 1)
                act.activation(stat[:, m, 1, 0:H], stat[:, m, 0, 0:H], ACT.Sqrt, scale=1.0 / HD,
                               bias=EPS).then_inc(krooted, 1)
            for m in range(MT):
                act.activation(v_hi[:, m, :], ps[:, 6 + m, :], ACT.Copy).then_inc(v_hi_done, 1)
            act.wait_ge(kturned, 1)
            act.activation(kt_hi[:, :, :].rearrange("p h m -> p (h m)"),
                           ps[:, 0:2, :].rearrange("p a b -> p (a b)"), ACT.Copy).then_inc(khi_done, 1)
            for c in range(MEMC, TOTAL):
                split(c)

        @block.vector
        def _(dve):
            for m in range(MT):
                dve.wait_ge(rooted, m + 1)
                dve.reciprocal(stat[:, m, 2, H:H + 1], stat[:, m, 1, H:H + 1]).then_inc(inverted, 1)
                dve.wait_ge(inverted, m + 1)
                dve.tensor_scalar(mn[:, m, :], mem[:, m, :], stat[:, m, 2, H:H + 1], None, ALU.mult
                                  ).then_inc(scaled, 1)
            for m in range(MT):
                dve.wait_ge(hi_done, m + 1)
                dve.tensor_tensor(mt_lo[:, :, m * P:(m + 1) * P],
                                  ps[:, 2 * m:2 * m + 2, :].rearrange("p a (b t) -> p (a b) t", t=P),
                                  mt_hi[:, :, m * P:(m + 1) * P], ALU.subtract).then_inc(lo_done, 1)

            def split(c):
                dve.wait_ge(w_hi_done, c + 1)
                scale = mem_gain[:, c // NB:c // NB + 1] if c < MEMC else 1.0
                split_weight_chunk_dve(dve, raw[:, c % 4, :], *chunk_split(c), scale).then_inc(w_lo_done, 1)
            for c in range(MEMC):
                split(c)
            dve.wait_ge(grow_in, 16)
            for m in range(MT):
                dve.wait_ge(krooted, m + 1)
                dve.reciprocal(stat[:, m, 2, 0:H], stat[:, m, 1, 0:H]).then_inc(kinverted, 1)
                dve.wait_ge(kinverted, m + 1)
                for h in range(H):
                    cols = slice(h * HD, (h + 1) * HD)
                    k = dve.scalar_tensor_tensor(out=kv[:, 0, m, cols], in0=ps[:, 4 + m, cols],
                                                 scalar=stat[:, m, 2, h:h + 1], in1=grow[:, cols],
                                                 op0=ALU.mult, op1=ALU.mult)
                k.then_inc(kv_done, 1)
            for m in range(MT):
                dve.wait_ge(v_hi_done, m + 1)
                dve.tensor_copy(kv[:, 1, m, :], ps[:, 6 + m, :]).then_inc(kv_done, 1)
                dve.tensor_tensor(v_lo[:, m, :], ps[:, 6 + m, :], v_hi[:, m, :], ALU.subtract).then_inc(v_lo_done, 1)
            dve.wait_ge(khi_done, 1)
            dve.tensor_tensor(kt_lo[:, :, :].rearrange("p h m -> p (h m)"),
                              ps[:, 0:2, :].rearrange("p a b -> p (a b)"),
                              kt_hi[:, :, :].rearrange("p h m -> p (h m)"), ALU.subtract).then_inc(klo_done, 1)
            for c in range(MEMC, TOTAL):
                split(c)
            dve.wait_ge(w_lo_done, TOTAL)

        @block.tensor
        def _(pe):
            for m in range(MT):
                pe.wait_ge(scaled, m + 1)
                for k in range(KD):
                    at = (k % 4) * P
                    t = pe.transpose(ps[:, 2 * m + k // 4, at:at + P], mn[:, m, k * P:(k + 1) * P], ident[:, :])
                t.then_inc(turned, 1)
            pe.wait_ge(lo_done, MT)
            for c in range(MEMC):
                k, b = c // NB, c % NB
                pe.wait_ge(w_lo_done, c + 1)
                for m in range(MT):
                    acc = ps[:, 4 + 2 * b + m, :]
                    x_hi, x_lo = mt_hi[:, k, m * P:(m + 1) * P], mt_lo[:, k, m * P:(m + 1) * P]
                    pe.matmul(acc, x_hi, mw_hi[:, c % 4, :], start=(k == 0), stop=False)
                    pe.matmul(acc, x_hi, mw_lo[:, c % 4, :], start=False, stop=False)
                    mm = pe.matmul(acc, x_lo, mw_hi[:, c % 4, :], start=False, stop=(k == KD - 1))
                mm.then_inc(multiplied, 1)
            pe.wait_ge(kv_done, MT)
            for h in range(H):
                for m in range(MT):
                    at = (h % 2) * MEM + m * P
                    t = pe.transpose(ps[:, h // 2, at:at + P], kv[:, 0, m, h * HD:(h + 1) * HD], ident[:, :])
            t.then_inc(kturned, 1)


def split3(pe, acc, a_hi, a_lo, b_hi, b_lo, first, last):
    pe.matmul(acc, a_hi, b_hi, start=first, stop=False)
    pe.matmul(acc, a_hi, b_lo, start=False, stop=False)
    return pe.matmul(acc, a_lo, b_hi, start=False, stop=last)


def out_stage(core, layer, src, x, y, wo_hi, wo_lo, kt_hi, kt_lo, v_hi, v_lo):
    nc, ps, ident = core.nc, core.ps, core.ident
    tag = f"out{layer}"
    conv = layer == 0
    MIX = KD if conv else H
    KO = MIX + H
    with ExitStack() as st:
        q_in_b = core.sb(st, f"{tag}_q", [P, 2, C])
        g_b = core.sb(st, f"{tag}_g", [P, 2, C])
        x_b = core.sb(st, f"{tag}_x", [P, 2, D])
        qt_hi = core.sb(st, f"{tag}_qthi", [P, C], F32R)
        qt_lo = core.sb(st, f"{tag}_qtlo", [P, C], F32R)
        prob = core.sb(st, f"{tag}_prob", [P, H, MEM])
        pt_hi = core.sb(st, f"{tag}_pthi", [P, H * MT, P], F32R)
        pt_lo = core.sb(st, f"{tag}_ptlo", [P, H * MT, P], F32R)
        og = core.sb(st, f"{tag}_og", [P, C])
        cat_hi = core.sb(st, f"{tag}_cathi", [P, 2, KO, P], F32R)
        cat_lo = core.sb(st, f"{tag}_catlo", [P, 2, KO, P], F32R)
        y_b = core.sb(st, f"{tag}_y", [P, D])
        stat = core.sb(st, f"{tag}_stat", [P, 4, H])
        if conv:
            c_b = core.sb(st, f"{tag}_c", [P, 2, KD, P])
        else:
            grp = core.sb(st, f"{tag}_grp", [P, 2, 3, OW])
            gd_b = core.sb(st, f"{tag}_gd", [P, 2, C])
            od = core.sb(st, f"{tag}_od", [P, C])
            cstat = core.sb(st, f"{tag}_cstat", [P, 6, 3 * H])
        names = ("in0 in1 qturned qhi_done qlo_done scored maxed biased exped inverted pturned phi_done plo_done "
                 "summed og_done oturned ohi_done olo_done mhi_done mlo_done projected y_done y_out "
                 "mturned ops cexp")
        (in0, in1, qturned, qhi_done, qlo_done, scored, maxed, biased, exped, inverted, pturned, phi_done, plo_done,
         summed, og_done, oturned, ohi_done, olo_done, mhi_done, mlo_done, projected, y_done, y_out,
         mturned, ops, cexp) = core.sems(st, tag, names)
        tile_in = (in0, in1)
        LOADS = 4 if conv else 7
        COPS = 10
        block = st.enter_context(nc.Block())

        @block.sync
        def _(sp):
            def load(q, u, first):
                at = q * (2 * P) + u * P
                if not first:
                    sp.wait_ge(y_done, q * 4 + (2 * u - 2))
                for dst, s in ((q_in_b[:, u, :], src["q"][ds(at, P), :]), (g_b[:, u, :], src["mg"][ds(at, P), :]),
                               (x_b[:, u, :], x[ds(at, P), :])):
                    sp.dma_start(dst, s).then_inc(tile_in[u], 16)
                if conv:
                    sp.dma_start(c_b[:, u, :, :], src["conv_t"].rearrange("(k p) t -> p k t", p=P)[:, :, ds(at, P)]
                                 ).then_inc(tile_in[u], 16)
                else:
                    sp.dma_start(gd_b[:, u, :], src["gd"][ds(at, P), :]).then_inc(tile_in[u], 16)
                    for g in range(3):
                        sp.dma_start(grp[:, u, g, :], src["grp"][ds(at + g * T, P), :]).then_inc(tile_in[u], 16)
            pairs(sp, NT, load)

        @block.gpsimd
        def _(pool):
            def store(q, u, first):
                pool.wait_ge(y_done, q * 4 + (2 * u + 2))
                pool.dma_start(y[ds(q * (2 * P) + u * P, P), :], y_b[:, :]).then_inc(y_out, 16)
            pairs(pool, NT, store)
            pool.wait_ge(y_out, 16 * NT)

        def n_of(q, u, extra):
            return q * 2 + (u + extra)

        @block.scalar
        def _(act):
            def step(q, u, first):
                act.wait_ge(qturned, n_of(q, u, 1))
                act.activation(qt_hi[:, :], ps[:, 0, :], ACT.Copy).then_inc(qhi_done, 1)
                if conv:
                    act.activation(cat_hi[:, u, 0:KD, :], c_b[:, u, :, :], ACT.Copy).then_inc(mhi_done, 1)
                act.wait_ge(biased, n_of(q, u, 1))
                for h in range(H):
                    e = act.activation(prob[:, h, :], ps[:, 1 + h // 2, (h % 2) * MEM:(h % 2 + 1) * MEM], ACT.Exp,
                                       scale=SCALE, bias=stat[:, 1, h:h + 1], accum_out=stat[:, 2, h:h + 1])
                e.then_inc(exped, 1)
                if not conv:
                    act.wait_ge(ops, q * (2 * COPS) + (u * COPS + 2))
                    act.activation(cstat[:, 2, :], cstat[:, 1, :], ACT.Exp, scale=SCALE).then_inc(cexp, 1)
                    act.wait_ge(mturned, n_of(q, u, 1))
                    act.activation(cat_hi[:, u, 0:H, :].rearrange("p a b -> p (a b)"), ps[:, 5, :], ACT.Copy
                                   ).then_inc(mhi_done, 1)
                act.wait_ge(pturned, n_of(q, u, 1))
                act.activation(pt_hi[:, :, :].rearrange("p a b -> p (a b)"),
                               ps[:, 3:5, :].rearrange("p a b -> p (a b)"), ACT.Copy).then_inc(phi_done, 1)
                act.wait_ge(oturned, n_of(q, u, 1))
                act.activation(cat_hi[:, u, MIX:KO, :].rearrange("p a b -> p (a b)"), ps[:, 0, :], ACT.Copy
                               ).then_inc(ohi_done, 1)

            def whole(q, u, first):
                act.wait_ge(tile_in[u], q * (16 * LOADS) + 16 * LOADS)
                step(q, u, first)
            pairs(act, NT, whole)

        @block.vector
        def _(dve):
            def combine(q, u, first):
                at = q * (2 * COPS) + u * COPS

                def sync_to(k):
                    dve.wait_ge(ops, at + k)
                mx = grp[:, u, :, C:C + H]
                sums = grp[:, u, :, C + H:C + 2 * H]
                dve.tensor_reduce(cstat[:, 0, 0:H], mx.rearrange("p g h -> p h g"), AX.X, ALU.max).then_inc(ops, 1)
                sync_to(1)
                dve.tensor_tensor(cstat[:, 1, :].rearrange("p (g h) -> p g h", h=H), mx,
                                  cstat[:, 0:1, 0:H].to_broadcast([P, 3, H]), ALU.subtract).then_inc(ops, 1)
                dve.wait_ge(cexp, n_of(q, u, 1))
                dve.tensor_tensor(cstat[:, 3, :].rearrange("p (g h) -> p g h", h=H), sums,
                                  cstat[:, 2, :].rearrange("p (g h) -> p g h", h=H), ALU.mult).then_inc(ops, 1)
                sync_to(3)
                dve.tensor_reduce(cstat[:, 0, H:2 * H], cstat[:, 3, :].rearrange("p (g h) -> p h g", h=H), AX.X,
                                  ALU.add).then_inc(ops, 1)
                sync_to(4)
                dve.reciprocal(cstat[:, 4, 0:H], cstat[:, 0, H:2 * H]).then_inc(ops, 1)
                sync_to(5)
                dve.tensor_tensor(cstat[:, 5, :].rearrange("p (g h) -> p g h", h=H),
                                  cstat[:, 2, :].rearrange("p (g h) -> p g h", h=H),
                                  cstat[:, 4:5, 0:H].to_broadcast([P, 3, H]), ALU.mult).then_inc(ops, 1)
                sync_to(6)
                for g in range(3):
                    for h in range(H):
                        cols = slice(h * HD, (h + 1) * HD)
                        w = cstat[:, 5, g * H + h:g * H + h + 1]
                        if g == 0:
                            m = dve.tensor_scalar(od[:, cols], grp[:, u, g, cols], w, None, ALU.mult)
                        else:
                            m = dve.scalar_tensor_tensor(out=od[:, cols], in0=grp[:, u, g, cols], scalar=w,
                                                         in1=od[:, cols], op0=ALU.mult, op1=ALU.add)
                    m.then_inc(ops, 1)
                    sync_to(7 + g)
                dve.tensor_tensor(od[:, :], od[:, :], gd_b[:, u, :], ALU.mult).then_inc(ops, 1)

            def add(q, u, half):
                dve.wait_ge(projected, q * 4 + (2 * u + half + 1))
                if half == 0:
                    if not (isinstance(q, int) and q == 0 and u == 0):
                        dve.wait_ge(y_out, q * 32 + u * 16)
                cols = slice(half * C, (half + 1) * C)
                dve.tensor_tensor(y_b[:, cols], ps[:, 6 + half, :], x_b[:, u, cols], ALU.add).then_inc(y_done, 1)

            def step(q, u, first):
                before = (q, 0) if u else (q - 1, 1)
                dve.wait_ge(tile_in[u], q * (16 * LOADS) + 16 * LOADS)
                dve.wait_ge(qhi_done, n_of(q, u, 1))
                dve.tensor_tensor(qt_lo[:, :], ps[:, 0, :], qt_hi[:, :], ALU.subtract).then_inc(qlo_done, 1)
                dve.wait_ge(scored, n_of(q, u, 1))
                dve.tensor_reduce(stat[:, 0, :], ps[:, 1:3, :].rearrange("p a (b m) -> p (a b) m", m=MEM), AX.X,
                                  ALU.max).then_inc(maxed, 1)
                dve.wait_ge(maxed, n_of(q, u, 1))
                dve.tensor_scalar(stat[:, 1, :], stat[:, 0, :], -SCALE, None, ALU.mult).then_inc(biased, 1)
                if conv:
                    dve.wait_ge(mhi_done, n_of(q, u, 1))
                    dve.tensor_tensor(cat_lo[:, u, 0:KD, :], c_b[:, u, :, :], cat_hi[:, u, 0:KD, :], ALU.subtract
                                      ).then_inc(mlo_done, 1)
                else:
                    combine(q, u, first)
                if not (first and u == 0):
                    add(*before, 0)
                dve.wait_ge(exped, n_of(q, u, 1))
                dve.reciprocal(stat[:, 3, :], stat[:, 2, :]).then_inc(inverted, 1)
                if not conv:
                    dve.wait_ge(mhi_done, n_of(q, u, 1))
                    dve.tensor_tensor(cat_lo[:, u, 0:H, :].rearrange("p a b -> p (a b)"), ps[:, 5, :],
                                      cat_hi[:, u, 0:H, :].rearrange("p a b -> p (a b)"), ALU.subtract
                                      ).then_inc(mlo_done, 1)
                dve.wait_ge(phi_done, n_of(q, u, 1))
                dve.tensor_tensor(pt_lo[:, :, :].rearrange("p a b -> p (a b)"),
                                  ps[:, 3:5, :].rearrange("p a b -> p (a b)"),
                                  pt_hi[:, :, :].rearrange("p a b -> p (a b)"), ALU.subtract).then_inc(plo_done, 1)
                if not (first and u == 0):
                    add(*before, 1)
                dve.wait_ge(inverted, n_of(q, u, 1))
                dve.wait_ge(summed, n_of(q, u, 1))
                for h in range(H):
                    cols = slice(h * HD, (h + 1) * HD)
                    m = dve.scalar_tensor_tensor(out=og[:, cols], in0=ps[:, 5, cols], scalar=stat[:, 3, h:h + 1],
                                                 in1=g_b[:, u, cols], op0=ALU.mult, op1=ALU.mult)
                m.then_inc(og_done, 1)
                dve.wait_ge(ohi_done, n_of(q, u, 1))
                dve.tensor_tensor(cat_lo[:, u, MIX:KO, :].rearrange("p a b -> p (a b)"), ps[:, 0, :],
                                  cat_hi[:, u, MIX:KO, :].rearrange("p a b -> p (a b)"), ALU.subtract
                                  ).then_inc(olo_done, 1)
            pairs(dve, NT, step)
            add(NT // 2 - 1, 1, 0)
            add(NT // 2 - 1, 1, 1)

        @block.tensor
        def _(pe):
            def project(q, u, half):
                if half == 0:
                    pe.wait_ge(olo_done, n_of(q, u, 1))
                    pe.wait_ge(mlo_done, n_of(q, u, 1))
                if not (isinstance(q, int) and q == 0 and u == 0):
                    pe.wait_ge(y_done, q * 4 + (2 * u + half - 1))
                cols = slice(half * C, (half + 1) * C)
                for k in range(KO):
                    m = split3(pe, ps[:, 6 + half, :], cat_hi[:, u, k, :], cat_lo[:, u, k, :],
                               wo_hi[:, k, cols], wo_lo[:, k, cols], k == 0, k == KO - 1)
                m.then_inc(projected, 1)

            def step(q, u, first):
                before = (q, 0) if u else (q - 1, 1)
                pe.wait_ge(tile_in[u], q * (16 * LOADS) + 16 * LOADS)
                if not (first and u == 0):
                    pe.wait_ge(olo_done, n_of(q, u, 0))
                for h in range(H):
                    t = pe.transpose(ps[:, 0, h * HD:(h + 1) * HD], q_in_b[:, u, h * HD:(h + 1) * HD], ident[:, :])
                t.then_inc(qturned, 1)
                pe.wait_ge(qlo_done, n_of(q, u, 1))
                if not (first and u == 0):
                    pe.wait_ge(exped, n_of(q, u, 0))
                for h in range(H):
                    at = (h % 2) * MEM
                    cols = slice(h * HD, (h + 1) * HD)
                    m = split3(pe, ps[:, 1 + h // 2, at:at + MEM], qt_hi[:, cols], qt_lo[:, cols],
                               kt_hi[:, h, :], kt_lo[:, h, :], True, True)
                m.then_inc(scored, 1)
                if not (first and u == 0):
                    project(*before, 0)
                if not conv:
                    pe.wait_ge(ops, q * (2 * COPS) + (u + 1) * COPS)
                    if not (first and u == 0):
                        pe.wait_ge(og_done, n_of(q, u, 0))
                    for h in range(H):
                        t = pe.transpose(ps[:, 5, h * HD:(h + 1) * HD], od[:, h * HD:(h + 1) * HD], ident[:, :])
                    t.then_inc(mturned, 1)
                pe.wait_ge(exped, n_of(q, u, 1))
                if not (first and u == 0):
                    pe.wait_ge(plo_done, n_of(q, u, 0))
                for h in range(H):
                    for mt in range(MT):
                        at = ((h * MT + mt) % 4) * P
                        t = pe.transpose(ps[:, 3 + h // 2, at:at + P], prob[:, h, mt * P:(mt + 1) * P], ident[:, :])
                t.then_inc(pturned, 1)
                if not (first and u == 0):
                    project(*before, 1)
                pe.wait_ge(plo_done, n_of(q, u, 1))
                if conv:
                    if not (first and u == 0):
                        pe.wait_ge(og_done, n_of(q, u, 0))
                else:
                    pe.wait_ge(mlo_done, n_of(q, u, 1))
                for h in range(H):
                    cols = slice(h * HD, (h + 1) * HD)
                    for mt in range(MT):
                        m = split3(pe, ps[:, 5, cols], pt_hi[:, h * MT + mt, :], pt_lo[:, h * MT + mt, :],
                                   v_hi[:, mt, cols], v_lo[:, mt, cols], mt == 0, mt == MT - 1)
                m.then_inc(summed, 1)
                pe.wait_ge(og_done, n_of(q, u, 1))
                for h in range(H):
                    t = pe.transpose(ps[:, 0, h * HD:(h + 1) * HD], og[:, h * HD:(h + 1) * HD], ident[:, :])
                t.then_inc(oturned, 1)
            pairs(pe, NT, step)
            for half in range(2):
                project(NT // 2 - 1, 1, half)


def dil_stage(core, g, q_src, kv_src, dst, masks_r, ident_r, zeros):
    nc, ps, ident = core.nc, core.ps, core.ident
    d = DIL[g][1]
    per_stream = NT // d
    U = 4
    TURNS = NT // U
    tag = f"dil{g}"

    def has_prev(q, u):
        if per_stream == 1:
            return False
        if d > 1:
            return u > 0
        return not (isinstance(q, int) and q == 0 and u == 0)

    def rows(ap, q, u):
        view = ap.rearrange("(m d) c -> d m c", d=d)
        if per_stream == 1:
            return view[ds(q * U + u, 1), :, :].rearrange("o m c -> (o m) c")
        if d > 1:
            return view[ds(q, 1), u * P:(u + 1) * P, :].rearrange("o m c -> (o m) c")
        return view[:, ds(q * (U * P) + u * P, P), :].rearrange("o m c -> (o m) c")

    def turns(eng, body, tail=()):
        for u in range(U):
            body(0, u)
        with eng.Fori(1, TURNS) as q:
            for u in range(U):
                body(q, u)

    def back(q, u, k):
        if u >= k:
            return q, u - k
        if isinstance(q, int) and q == 0:
            return None
        return q - 1, u - k + U

    def cnt(s, extra=1):
        return s[0] * U + (s[1] + extra)

    def use(s, per=16):
        return s[0] * (U // 2 * per) + (s[1] // 2 + 1) * per

    with ExitStack() as st:
        q_b = core.sb(st, f"{tag}_q", [P, 2, C])
        k_b = core.sb(st, f"{tag}_k", [P, 2, C])
        v_b = core.sb(st, f"{tag}_v", [P, 2, C])
        qt_hi = core.sb(st, f"{tag}_qthi", [P, C], F32R)
        qt_lo = core.sb(st, f"{tag}_qtlo", [P, C], F32R)
        kt_hi = core.sb(st, f"{tag}_kthi", [P, H, 2, P], F32R)
        kt_lo = core.sb(st, f"{tag}_ktlo", [P, H, 2, P], F32R)
        v_hi = core.sb(st, f"{tag}_vhi", [P, 2, C], F32R)
        v_lo = core.sb(st, f"{tag}_vlo", [P, 2, C], F32R)
        prob = core.sb(st, f"{tag}_prob", [P, H, 2, P])
        pt_hi = core.sb(st, f"{tag}_pthi", [P, H, 2, P], F32R)
        pt_lo = core.sb(st, f"{tag}_ptlo", [P, H, 2, P], F32R)
        o_b = core.sb(st, f"{tag}_o", [P, 2, OW])
        bias = core.sb(st, f"{tag}_bias", [P, H])
        names = ("qk_in0 qk_in1 v_in0 v_in1 o_out0 o_out1 turned qhi_done khi_done qlo_done klo_done vhi_done "
                 "vlo_done scored maxed biased exped pturned phi_done plo_done summed o_done")
        (qk_in0, qk_in1, v_in0, v_in1, o_out0, o_out1, turned, qhi_done, khi_done, qlo_done, klo_done, vhi_done,
         vlo_done, scored, maxed, biased, exped, pturned, phi_done, plo_done, summed, o_done) = core.sems(
            st, tag, names)
        qk_in, v_in, o_out = (qk_in0, qk_in1), (v_in0, v_in1), (o_out0, o_out1)
        block = st.enter_context(nc.Block())

        def keys(s):
            return (1 - s[1] % 2, s[1] % 2) if has_prev(*s) else (s[1] % 2,)

        def span(s):
            ks = sorted(keys(s))
            return ks[0], ks[-1] + 1

        scores = ps[:, 1:3, :].rearrange("p a (b s k) -> p (a b) s k", b=2, s=2)
        turned_p = ps[:, 3:5, :].rearrange("p a (b s k) -> p (a b) s k", b=2, s=2)

        @block.sync
        def _(sp):
            def store(s):
                sp.wait_ge(o_done, cnt(s))
                sp.dma_start(rows(dst, *s), o_b[:, s[1] % 2, :]).then_inc(o_out[s[1] % 2], 16)

            def body(q, u):
                slot = u % 2
                if back(q, u, 2):
                    sp.wait_ge(turned, cnt(back(q, u, 2)))
                sp.dma_start(q_b[:, slot, :], rows(q_src, q, u)).then_inc(qk_in[slot], 16)
                sp.dma_start(k_b[:, slot, :], rows(kv_src[:, 0:C], q, u)).then_inc(qk_in[slot], 16)
                if back(q, u, 2):
                    sp.wait_ge(vlo_done, cnt(back(q, u, 2)))
                sp.dma_start(v_b[:, slot, :], rows(kv_src[:, C:2 * C], q, u)).then_inc(v_in[slot], 16)
                if back(q, u, 3):
                    store(back(q, u, 3))
            turns(sp, body)
            for u in (U - 3, U - 2, U - 1):
                store(back(TURNS, 0, U - u))
            for s in o_out:
                sp.wait_ge(s, 16 * NT // 2)

        @block.gpsimd
        def _(pool):
            def body(q, u):
                slot = u % 2
                pool.wait_ge(v_in[slot], use((q, u)))
                if back(q, u, 1):
                    pool.wait_ge(summed, cnt(back(q, u, 1)))
                pool.tensor_tensor(v_hi[:, slot, :], v_b[:, slot, :], zeros[:, :], ALU.add).then_inc(vhi_done, 1)
                pool.wait_ge(vhi_done, cnt((q, u)))
                pool.tensor_tensor(v_lo[:, slot, :], v_b[:, slot, :], v_hi[:, slot, :], ALU.subtract
                                   ).then_inc(vlo_done, 1)
            turns(pool, body)

        @block.scalar
        def _(act):
            def exps(s):
                a, b = span(s)
                act.wait_ge(biased, cnt(s))
                for h in range(H):
                    e = act.activation(prob[:, h, a:b, :], scores[:, h, a:b, :], ACT.Exp, scale=SCALE,
                                       bias=bias[:, h:h + 1],
                                       accum_out=o_b[:, s[1] % 2, C + H + h:C + H + h + 1])
                e.then_inc(exped, 1)

            def copy_sums(s):
                act.wait_ge(summed, cnt(s))
                act.activation(o_b[:, s[1] % 2, 0:C], ps[:, 5, :], ACT.Copy).then_inc(o_done, 1)

            def probs_high(s):
                a, b = span(s)
                act.wait_ge(pturned, cnt(s))
                act.activation(pt_hi[:, :, a:b, :], turned_p[:, :, a:b, :], ACT.Copy).then_inc(phi_done, 1)

            def body(q, u):
                act.wait_ge(turned, cnt((q, u)))
                act.activation(qt_hi[:, :], ps[:, 0, :], ACT.Copy).then_inc(qhi_done, 1)
                act.activation(kt_hi[:, :, u % 2, :], ps[:, 6, :].rearrange("p (h k) -> p h k", h=H), ACT.Copy
                               ).then_inc(khi_done, 1)
                if back(q, u, 1):
                    exps(back(q, u, 1))
                if back(q, u, 2):
                    copy_sums(back(q, u, 2))
                if back(q, u, 1):
                    probs_high(back(q, u, 1))
            turns(act, body)
            last, before = back(TURNS, 0, 1), back(TURNS, 0, 2)
            exps(last)
            copy_sums(before)
            probs_high(last)
            copy_sums(last)

        @block.vector
        def _(dve):
            def maxima(s):
                a, b = span(s)
                slot = s[1] % 2
                dve.wait_ge(scored, cnt(s))
                if back(*s, 2):
                    dve.wait_ge(o_out[slot], use(back(*s, 2)))
                dve.tensor_reduce(o_b[:, slot, C:C + H], scores[:, :, a:b, :].rearrange("p h s k -> p h (s k)"),
                                  AX.X, ALU.max).then_inc(maxed, 1)
                dve.wait_ge(maxed, cnt(s))
                dve.tensor_scalar(bias[:, :], o_b[:, slot, C:C + H], -SCALE, None, ALU.mult).then_inc(biased, 1)

            def probs_low(s):
                a, b = span(s)
                dve.wait_ge(phi_done, cnt(s))
                dve.tensor_tensor(pt_lo[:, :, a:b, :].rearrange("p h s k -> p h (s k)"),
                                  turned_p[:, :, a:b, :].rearrange("p h s k -> p h (s k)"),
                                  pt_hi[:, :, a:b, :].rearrange("p h s k -> p h (s k)"), ALU.subtract
                                  ).then_inc(plo_done, 1)

            def body(q, u):
                if back(q, u, 1):
                    maxima(back(q, u, 1))
                dve.wait_ge(qhi_done, cnt((q, u)))
                dve.tensor_tensor(qt_lo[:, :], ps[:, 0, :], qt_hi[:, :], ALU.subtract).then_inc(qlo_done, 1)
                dve.wait_ge(khi_done, cnt((q, u)))
                dve.tensor_tensor(kt_lo[:, :, u % 2, :], ps[:, 6, :].rearrange("p (h k) -> p h k", h=H),
                                  kt_hi[:, :, u % 2, :], ALU.subtract).then_inc(klo_done, 1)
                if back(q, u, 1):
                    probs_low(back(q, u, 1))
            turns(dve, body)
            last = back(TURNS, 0, 1)
            maxima(last)
            probs_low(last)

        @block.tensor
        def _(pe):
            def score(s):
                a, b = span(s)
                own = s[1] % 2
                if has_prev(*s):
                    mask = masks_r[:, 0:2 * P] if own else masks_r[:, P:3 * P]
                else:
                    mask = masks_r[:, P:2 * P]
                pe.wait_ge(qlo_done, cnt(s))
                pe.wait_ge(klo_done, cnt(s))
                for h in range(H):
                    cols = slice(h * HD, (h + 1) * HD)
                    acc = scores[:, h, a:b, :].rearrange("p s k -> p (s k)")
                    pe.matmul(acc, ident_r[:, :], mask, start=True, stop=False)
                    m = split3(pe, acc, qt_hi[:, cols], qt_lo[:, cols],
                               kt_hi[:, h, a:b, :].rearrange("p s k -> p (s k)"),
                               kt_lo[:, h, a:b, :].rearrange("p s k -> p (s k)"), False, True)
                m.then_inc(scored, 1)

            def turn(q, u):
                pe.wait_ge(qk_in[u % 2], use((q, u), 32))
                for h in range(H):
                    cols = slice(h * HD, (h + 1) * HD)
                    pe.transpose(ps[:, 0, cols], q_b[:, u % 2, cols], ident[:, :])
                for h in range(H):
                    cols = slice(h * HD, (h + 1) * HD)
                    t = pe.transpose(ps[:, 6, cols], k_b[:, u % 2, cols], ident[:, :])
                t.then_inc(turned, 1)

            def sums(s):
                pe.wait_ge(plo_done, cnt(s))
                pe.wait_ge(vlo_done, cnt(s))
                if back(*s, 1):
                    pe.wait_ge(o_done, cnt(back(*s, 1)))
                ks = keys(s)
                for h in range(H):
                    cols = slice(h * HD, (h + 1) * HD)
                    for j, key in enumerate(ks):
                        m = split3(pe, ps[:, 5, cols], pt_hi[:, h, key, :], pt_lo[:, h, key, :],
                                   v_hi[:, key, cols], v_lo[:, key, cols], j == 0, j == len(ks) - 1)
                m.then_inc(summed, 1)

            def turn_probs(s):
                pe.wait_ge(exped, cnt(s))
                for h in range(H):
                    for key in keys(s):
                        t = pe.transpose(turned_p[:, h, key, :], prob[:, h, key, :], ident[:, :])
                t.then_inc(pturned, 1)

            def body(q, u):
                if back(q, u, 1):
                    score(back(q, u, 1))
                turn(q, u)
                if back(q, u, 2):
                    sums(back(q, u, 2))
                if back(q, u, 1):
                    turn_probs(back(q, u, 1))
            turns(pe, body)
            last, before = back(TURNS, 0, 1), back(TURNS, 0, 2)
            score(last)
            sums(before)
            turn_probs(last)
            sums(last)


def masks_stage(core, masks, masks_r, ident_r, zeros):
    nc, ident = core.nc, core.ident
    with ExitStack() as st:
        zeroed, made, = core.sems(st, "masks", "zeroed made")
        block = st.enter_context(nc.Block())

        @block.gpsimd
        def _(pool):
            pool.memset(masks[:, :], 0.0).then_inc(zeroed, 1)
            pool.wait_ge(zeroed, 1)
            for at, sign in ((0, -1), (1, 1), (2, -1)):
                cols = masks[:, at * P:(at + 1) * P]
                pool.affine_select(out=cols, in_=cols, compare_op=ALU.is_ge, fill=NEG, base=0,
                                   pattern=[[-sign, P]], channel_multiplier=sign).then_inc(made, 1)

        @block.vector
        def _(dve):
            dve.wait_ge(made, 3)
            dve.tensor_copy(masks_r[:, :], masks[:, :])
            dve.tensor_copy(ident_r[:, :], ident[:, :])
            dve.memset(zeros[:, :], 0.0)


def dec_stage(core, layer, src, x_s, y_s, wo_hi, wo_lo):
    nc, ps, ident, io = core.nc, core.ps, core.ident, core.io
    tag = f"dec{layer}"
    conv = layer == 0
    MIX = KD if conv else H
    KO = MIX + H
    HS = H * S
    NG = len(DIL)
    GW = P + S
    n_att = 1 if conv else 2
    with ExitStack() as st:
        rows_in = core.sb(st, f"{tag}_rows", [S, 4, C])
        kc = core.sb(st, f"{tag}_kc", [P, 3, H, MEM])
        vc = core.sb(st, f"{tag}_vc", [P, 3, MT, C])
        cols_t = core.sb(st, f"{tag}_cols", [P, 3, HS])
        scr = core.sb(st, f"{tag}_scr", [P, MT, HS])
        sc = core.sb(st, f"{tag}_sc", [HS, MEM])
        pr = core.sb(st, f"{tag}_pr", [HS, MEM])
        pt = core.sb(st, f"{tag}_pt", [P, MT, HS])
        stat = core.sb(st, f"{tag}_stat", [HS, 8])
        cat = core.sb(st, f"{tag}_cat", [P, KO, S])
        cat_hi = core.sb(st, f"{tag}_cathi", [P, KO, S], F32R)
        cat_lo = core.sb(st, f"{tag}_catlo", [P, KO, S], F32R)
        xs = core.sb(st, f"{tag}_xs", [S, D])
        ys = core.sb(st, f"{tag}_ys", [S, D])
        if not conv:
            qd = core.sb(st, f"{tag}_qd", [S, NG, C])
            kvn = core.sb(st, f"{tag}_kvn", [S, NG, 2, C])
            kd = core.sb(st, f"{tag}_kd", [P, 3, H, P])
            vd = core.sb(st, f"{tag}_vd", [P, 3, C])
            qdt = core.sb(st, f"{tag}_qdt", [P, NG, HS])
            knt = core.sb(st, f"{tag}_knt", [P, NG, HS])
            dscr = core.sb(st, f"{tag}_dscr", [P, NG, HS])
            nscr = core.sb(st, f"{tag}_nscr", [S, NG, HS])
            other = core.sb(st, f"{tag}_other", [S, NG * H, S])
            dsc = core.sb(st, f"{tag}_dsc", [HS, NG * GW])
            dpt = core.sb(st, f"{tag}_dpt", [P, NG, HS])
            npt = core.sb(st, f"{tag}_npt", [S, NG, HS])
        names = ("in_done kc_in0 kc_in1 kc_in2 vc_in0 vc_in1 vc_in2 kd_in0 kd_in1 kd_in2 vd_in0 vd_in1 vd_in2 "
                 "act_done dve_done pe_done k_used v_used kd_used vd_used y_out other_made")
        (in_done, kc_in0, kc_in1, kc_in2, vc_in0, vc_in1, vc_in2, kd_in0, kd_in1, kd_in2, vd_in0, vd_in1, vd_in2,
         act_done, dve_done, pe_done, k_used, v_used, kd_used, vd_used, y_out, other_made) = core.sems(st, tag, names)
        kc_in, vc_in = (kc_in0, kc_in1, kc_in2), (vc_in0, vc_in1, vc_in2)
        kd_in, vd_in = (kd_in0, kd_in1, kd_in2), (vd_in0, vd_in1, vd_in2)
        LOADS = 4 if conv else 6
        FINAL = 12 if conv else 23
        block = st.enter_context(nc.Block())

        @block.sync
        def _(sp):
            sp.dma_start(rows_in[:, 0, :], src["q"][T:TS, :]).then_inc(in_done, 16)
            sp.dma_start(rows_in[:, 1, :], src["mg"][T:TS, :]).then_inc(in_done, 16)
            sp.dma_start(xs[:, :], x_s).then_inc(in_done, 16)
            if conv:
                sp.dma_start(cat[:, 0:KD, :], src["conv_t"].rearrange("(k p) t -> p k t", p=P)[:, :, T:TS]
                             ).then_inc(in_done, 16)
            else:
                sp.dma_start(rows_in[:, 2, :], src["gd"][T:TS, :]).then_inc(in_done, 16)
                sp.dma_start(qd[:, :, :], src["qd"].rearrange("g t c -> t g c")[T:TS, :, :]).then_inc(in_done, 16)
                sp.dma_start(kvn[:, :, :, :].rearrange("s g a c -> s g (a c)"),
                             src["kv"].rearrange("g t c -> t g c")[T:TS, :, :]).then_inc(in_done, 16)
            for b in range(S):
                if b >= 3:
                    sp.wait_ge(k_used, b - 2)
                sp.dma_start(kc[:, b % 3, :, :].rearrange("p h m -> p (h m)"),
                             io["cache_kt"][(layer * S + b) * P:(layer * S + b + 1) * P, :]).then_inc(kc_in[b % 3], 16)
            for b in range(S):
                if b >= 3:
                    sp.wait_ge(v_used, b - 2)
                sp.dma_start(vc[:, b % 3, :, :],
                             io["cache_v"][layer, b].rearrange("(m p) c -> p m c", p=P)).then_inc(vc_in[b % 3], 16)

        @block.gpsimd
        def _(pool):
            if not conv:
                pool.memset(other[:, :, :], NEG).then_inc(other_made, 1)
                pool.wait_ge(other_made, 1)
                pool.affine_select(out=other[:, :, :], in_=other[:, :, :], compare_op=ALU.not_equal, fill=0.0,
                                   base=0, pattern=[[0, NG * H], [-1, S]], channel_multiplier=1
                                   ).then_inc(other_made, 1)
                for n in range(NG * S):
                    g, b = n // S, n % S
                    if n >= 3:
                        pool.wait_ge(kd_used, n - 2)
                    pool.dma_start(kd[:, n % 3, :, :].rearrange("p h m -> p (h m)"),
                                   io["dil_kt"][n * P:(n + 1) * P, :]).then_inc(kd_in[n % 3], 16)
                for n in range(NG * S):
                    if n >= 3:
                        pool.wait_ge(vd_used, n - 2)
                    pool.dma_start(vd[:, n % 3, :], io["dil_v"][((n % NG) * S + n // NG) * P:
                                                               ((n % NG) * S + n // NG + 1) * P, :]
                                   ).then_inc(vd_in[n % 3], 16)
            pool.wait_ge(dve_done, FINAL)
            pool.dma_start(y_s, ys[:, :]).then_inc(y_out, 16)
            pool.wait_ge(y_out, 16)

        @block.tensor
        def _(pe):
            id_s = ident[0:S, 0:S]
            pe.wait_ge(in_done, 16 * LOADS)
            for r in range(2 if conv else 3):
                for h in range(H):
                    at = r * HS + h * S
                    t = pe.transpose(ps[:, 0, at:at + S], rows_in[:, r, h * HD:(h + 1) * HD], id_s)
            t.then_inc(pe_done, 1)
            pe.wait_ge(dve_done, 1)
            for b in range(S):
                pe.wait_ge(kc_in[b % 3], 16 * (b // 3 + 1))
                for h in range(H):
                    for m in range(MT):
                        c = h * S + b
                        mm = pe.matmul(ps[:, 1, m * HS + c:m * HS + c + 1], kc[:, b % 3, h, m * P:(m + 1) * P],
                                       cols_t[:, 0, c:c + 1], start=True, stop=True)
                mm.then_inc(k_used, 1)
            pe.wait_ge(dve_done, 2)
            for m in range(MT):
                t = pe.transpose(ps[0:HS, 2, m * P:(m + 1) * P], scr[:, m, :], ident[:, :])
            t.then_inc(pe_done, 1)
            pe.wait_ge(dve_done, 7)
            for m in range(MT):
                t = pe.transpose(ps[:, 3, m * HS:(m + 1) * HS], pr[:, m * P:(m + 1) * P], ident[0:HS, 0:HS])
            t.then_inc(pe_done, 1)
            pe.wait_ge(dve_done, 8)
            for b in range(S):
                pe.wait_ge(vc_in[b % 3], 16 * (b // 3 + 1))
                for h in range(H):
                    c = h * S + b
                    for m in range(MT):
                        mm = pe.matmul(ps[:, 4, c:c + 1], vc[:, b % 3, m, h * HD:(h + 1) * HD], pt[:, m, c:c + 1],
                                       start=(m == 0), stop=(m == MT - 1))
                mm.then_inc(v_used, 1)
            if not conv:
                for g in range(NG):
                    for h in range(H):
                        at = g * HS + h * S
                        pe.transpose(ps[:, 5, at:at + S], qd[:, g, h * HD:(h + 1) * HD], id_s)
                        t = pe.transpose(ps[:, 6, at:at + S], kvn[:, g, 0, h * HD:(h + 1) * HD], id_s)
                t.then_inc(pe_done, 1)
                pe.wait_ge(dve_done, 10)
                for n in range(NG * S):
                    g, b = n // S, n % S
                    pe.wait_ge(kd_in[n % 3], 16 * (n // 3 + 1))
                    for h in range(H):
                        c = h * S + b
                        mm = pe.matmul(ps[:, 7, g * HS + c:g * HS + c + 1], kd[:, n % 3, h, :], qdt[:, g, c:c + 1],
                                       start=True, stop=True)
                    mm.then_inc(kd_used, 1)
                for g in range(NG):
                    for h in range(H):
                        hs = slice(h * S, (h + 1) * S)
                        mm = pe.matmul(ps[0:S, 0, g * HS + h * S:g * HS + (h + 1) * S], knt[:, g, hs], qdt[:, g, hs],
                                       start=True, stop=True)
                mm.then_inc(pe_done, 1)
                pe.wait_ge(dve_done, 12)
                for g in range(NG):
                    pe.transpose(ps[0:HS, 1, g * GW:g * GW + P], dscr[:, g, :], ident[:, :])
                    t = pe.transpose(ps[0:HS, 1, g * GW + P:(g + 1) * GW], nscr[:, g, :], id_s)
                t.then_inc(pe_done, 1)
                pe.wait_ge(dve_done, 17)
                for g in range(NG):
                    pe.transpose(ps[:, 2, g * HS:(g + 1) * HS], dsc[:, g * GW:g * GW + P], ident[0:HS, 0:HS])
                    t = pe.transpose(ps[0:S, 3, g * HS:(g + 1) * HS], dsc[:, g * GW + P:(g + 1) * GW],
                                     ident[0:HS, 0:HS])
                t.then_inc(pe_done, 1)
                pe.wait_ge(dve_done, 19)
                for b in range(S):
                    for g in range(NG):
                        pe.wait_ge(vd_in[g], 16 * (b + 1))
                    for h in range(H):
                        c = h * S + b
                        cols = slice(h * HD, (h + 1) * HD)
                        for g in range(NG):
                            pe.matmul(ps[:, 5, c:c + 1], vd[:, g, cols], dpt[:, g, c:c + 1],
                                      start=(g == 0), stop=False)
                            mm = pe.matmul(ps[:, 5, c:c + 1], kvn[:, g, 1, cols], npt[:, g, c:c + 1],
                                           start=False, stop=(g == NG - 1))
                    mm.then_inc(vd_used, NG)
            pe.wait_ge(dve_done, FINAL - 1)
            for half in range(2):
                cols = slice(half * C, (half + 1) * C)
                for k in range(KO):
                    mm = split3(pe, ps[0:S, 6 + half, :], cat_hi[:, k, :], cat_lo[:, k, :], wo_hi[:, k, cols],
                                wo_lo[:, k, cols], k == 0, k == KO - 1)
            mm.then_inc(pe_done, 1)

        @block.vector
        def _(dve):
            done = [0]

            def op(ins):
                done[0] += 1
                ins.then_inc(dve_done, 1)

            def after(n=None):
                dve.wait_ge(dve_done, done[0] if n is None else n)
            R = 2 if conv else 3
            dve.wait_ge(pe_done, 1)
            op(dve.tensor_copy(cols_t[:, 0:R, :].rearrange("p r c -> p (r c)"), ps[:, 0, 0:R * HS]))
            dve.wait_ge(k_used, S)
            op(dve.tensor_copy(scr[:, :, :].rearrange("p m c -> p (m c)"), ps[:, 1, 0:MT * HS]))
            dve.wait_ge(pe_done, 2)
            op(dve.tensor_copy(sc[:, :], ps[0:HS, 2, 0:MEM]))
            after()
            op(dve.tensor_reduce(stat[:, 0:1], sc[:, :], AX.X, ALU.max))
            after()
            op(dve.tensor_scalar(stat[:, 1:2], stat[:, 0:1], -SCALE, None, ALU.mult))
            dve.wait_ge(act_done, 1)
            op(dve.reciprocal(stat[:, 3:4], stat[:, 2:3]))
            after()
            op(dve.tensor_scalar(pr[:, :], pr[:, :], stat[:, 3:4], None, ALU.mult))
            dve.wait_ge(pe_done, 3)
            op(dve.tensor_copy(pt[:, :, :].rearrange("p m c -> p (m c)"), ps[:, 3, 0:MT * HS]))
            dve.wait_ge(v_used, S)
            op(dve.tensor_tensor(cat[:, MIX:KO, :].rearrange("p h b -> p (h b)"), ps[:, 4, 0:HS],
                                 cols_t[:, 1, :], ALU.mult))
            if not conv:
                dve.wait_ge(pe_done, 4)
                dve.tensor_copy(qdt[:, :, :].rearrange("p g c -> p (g c)"), ps[:, 5, 0:NG * HS])
                op(dve.tensor_copy(knt[:, :, :].rearrange("p g c -> p (g c)"), ps[:, 6, 0:NG * HS]))
                dve.wait_ge(pe_done, 5)
                dve.wait_ge(other_made, 2)
                op(dve.tensor_copy(dscr[:, :, :].rearrange("p g c -> p (g c)"), ps[:, 7, 0:NG * HS]))
                op(dve.tensor_tensor(nscr[:, :, :].rearrange("p g c -> p (g c)"), ps[0:S, 0, 0:NG * HS],
                                     other[:, :, :].rearrange("p a b -> p (a b)"), ALU.add))
                dve.wait_ge(pe_done, 6)
                op(dve.tensor_copy(dsc[:, :], ps[0:HS, 1, 0:NG * GW]))
                after()
                op(dve.tensor_reduce(stat[:, 4:5], dsc[:, :], AX.X, ALU.max))
                after()
                op(dve.tensor_scalar(stat[:, 5:6], stat[:, 4:5], -SCALE, None, ALU.mult))
                dve.wait_ge(act_done, 2)
                op(dve.reciprocal(stat[:, 7:8], stat[:, 6:7]))
                after()
                op(dve.tensor_scalar(dsc[:, :], dsc[:, :], stat[:, 7:8], None, ALU.mult))
                dve.wait_ge(pe_done, 7)
                op(dve.tensor_copy(dpt[:, :, :].rearrange("p g c -> p (g c)"), ps[:, 2, 0:NG * HS]))
                op(dve.tensor_copy(npt[:, :, :].rearrange("p g c -> p (g c)"), ps[0:S, 3, 0:NG * HS]))
                dve.wait_ge(vd_used, NG * S)
                op(dve.tensor_tensor(cat[:, 0:H, :].rearrange("p h b -> p (h b)"), ps[:, 5, 0:HS],
                                     cols_t[:, 2, :], ALU.mult))
            else:
                dve.wait_ge(in_done, 16 * LOADS)
            after()
            op(dve.tensor_copy(cat_hi[:, :, :], cat[:, :, :]))
            after()
            op(dve.tensor_tensor(cat_lo[:, :, :], cat[:, :, :], cat_hi[:, :, :], ALU.subtract))
            dve.wait_ge(pe_done, 4 if conv else 8)
            dve.wait_ge(in_done, 16 * LOADS)
            dve.tensor_tensor(ys[:, 0:C], ps[0:S, 6, :], xs[:, 0:C], ALU.add)
            op(dve.tensor_tensor(ys[:, C:D], ps[0:S, 7, :], xs[:, C:D], ALU.add))
            assert done[0] == FINAL

        @block.scalar
        def _(act):
            act.wait_ge(dve_done, 5)
            act.activation(pr[:, :], sc[:, :], ACT.Exp, scale=SCALE, bias=stat[:, 1:2], accum_out=stat[:, 2:3]
                           ).then_inc(act_done, 1)
            if not conv:
                act.wait_ge(dve_done, 15)
                act.activation(dsc[:, :], dsc[:, :], ACT.Exp, scale=SCALE, bias=stat[:, 5:6],
                               accum_out=stat[:, 6:7]).then_inc(act_done, 1)


def build(nc, io):
    with ExitStack() as ctx:
        core = Core(nc, ctx, io)
        gains = core.sb(ctx, "gains", [P, 5 * KD])
        norm_a, kv_norm, norm_b, mem_norm_0, mem_norm_1 = (gains[:, n * KD:(n + 1) * KD] for n in range(5))
        setup_stage(core, gains)

        def wide(stack, name):
            return [core.sb(stack, f"{name}_{n}", shape, F32R)
                    for n, shape in (("xthi", [P, KD, TS]), ("xtlo", [P, KD, TS]),
                                     ("wh0", [P, KD, C]), ("wl0", [P, KD, C]))]

        def output_side(layer, w_mem, w_out, chunks, mem_norm, src, x, x_s, y, y_s):
            with ExitStack() as st:
                wo_hi = core.sb(st, f"wohi{layer}", [P, chunks, D], F32R)
                wo_lo = core.sb(st, f"wolo{layer}", [P, chunks, D], F32R)
                with ExitStack() as kvs:
                    kt_hi, kt_lo = (core.sb(kvs, f"mk{n}{layer}", [P, H, MEM], F32R) for n in ("hi", "lo"))
                    v_hi, v_lo = (core.sb(kvs, f"mv{n}{layer}", [P, MT, C], F32R) for n in ("hi", "lo"))
                    memkv_stage(core, layer, w_mem, io["mem_kv"][layer * MEM:(layer + 1) * MEM, :], w_out, chunks,
                                wo_hi, wo_lo, kt_hi, kt_lo, v_hi, v_lo, mem_norm, 8 + layer)
                    out_stage(core, layer, src, x, y, wo_hi, wo_lo, kt_hi, kt_lo, v_hi, v_lo)
                dec_stage(core, layer, src, x_s, y_s, wo_hi, wo_lo)

        with ExitStack() as st:
            xt_hi, xt_lo, wh0, wl0 = wide(st, "a")
            prep_stage(core, "prepa", io["x_prompt"], io["x_sample"], xt_hi, xt_lo, io["w_a"], wh0, wl0, norm_a)
            wh, wl = (wh0, core.sb(st, "a_wh1", [P, KD, C], F32R)), (wl0, core.sb(st, "a_wl1", [P, KD, C], F32R))
            conv_stage(core, io["w_a"], xt_hi, xt_lo, wh, wl, norm_a)
            tokens_stage(core, "toka", io["w_a"][(NCONV + 1) * D:, :],
                         [("norm", io["tok_a"][0], norm_a, 6), ("silu", io["tok_a"][1], None, None)],
                         xt_hi, xt_lo, wh, wl)
        src = {"q": io["tok_a"][0], "mg": io["tok_a"][1], "conv_t": io["conv_t"]}
        output_side(0, io["w_mem"][0:D, :], io["w_out_a"], KD + H, mem_norm_0, src, io["x_prompt"],
                    io["x_sample"], io["x1"][0:T, :], io["x1"][T:TS, :])
        with ExitStack() as st:
            xt_hi, xt_lo, wh0, wl0 = wide(st, "b")
            prep_stage(core, "prepb", io["x1"][0:T, :], io["x1"][T:TS, :], xt_hi, xt_lo, io["w_b"], wh0, wl0,
                       kv_norm)
            wh, wl = (wh0, core.sb(st, "b_wh1", [P, KD, C], F32R)), (wl0, core.sb(st, "b_wl1", [P, KD, C], F32R))
            kv = lambda g, part: io["kv"][g][:, part * C:(part + 1) * C]
            blocks = []
            for g in range(len(DIL)):
                blocks.append(("norm", kv(g, 0), kv_norm, g))
                blocks.append(("copy", kv(g, 1), kv_norm if g < 2 else norm_b, None))
            for g in range(len(DIL)):
                blocks.append(("norm", io["tok_b"][g], norm_b, 3 + g))
            blocks.append(("norm", io["tok_b"][3], norm_b, 7))
            blocks.append(("silu", io["tok_b"][4], norm_b, None))
            blocks.append(("silu", io["tok_b"][5], None, None))
            tokens_stage(core, "tokb", io["w_b"][D:, :], blocks, xt_hi, xt_lo, wh, wl)
        with ExitStack() as st:
            masks = core.sb(st, "masks", [P, 3 * P])
            masks_r = core.sb(st, "masks_r", [P, 3 * P], F32R)
            ident_r = core.sb(st, "ident_r", [P, P], F32R)
            zeros = core.sb(st, "zeros", [P, C])
            masks_stage(core, masks, masks_r, ident_r, zeros)
            for g in range(len(DIL)):
                dil_stage(core, g, io["tok_b"][g][0:T, :], io["kv"][g][0:T, :], io["grp"][g * T:(g + 1) * T, :],
                          masks_r, ident_r, zeros)
        src = {"q": io["tok_b"][3], "mg": io["tok_b"][5], "gd": io["tok_b"][4], "grp": io["grp"],
               "qd": io["tok_b"][0:3], "kv": io["kv"]}
        output_side(1, io["w_mem"][D:2 * D, :], io["w_out_b"], 2 * H, mem_norm_1, src, io["x1"][0:T, :],
                    io["x1"][T:TS, :], io["y"][0:T, :], io["y"][T:TS, :])


def kernel(**inputs):
    import concourse.bacc as bacc
    from concourse.bass_utils import run_bass_kernel_spmd

    a = {k: np.asarray(v) for k, v in inputs.items()}
    layout = np.ascontiguousarray
    w_in_a, w_in_b = a["w_in_a"][0], a["w_in_b"][0]
    part = lambda w, n: w[:, n * D:(n + 1) * D].reshape(D, NCONV, P)
    conv_w = np.stack([part(w_in_a, n) for n in (1, 0, 3, 2)], axis=2)
    w_a = np.concatenate([conv_w.transpose(1, 0, 2, 3).reshape(NCONV * D, C),
                          w_in_a[:, 4 * D:].reshape(D, 2, C).transpose(1, 0, 2).reshape(2 * D, C)])
    b_cols = w_in_b.reshape(D, 6, C)[:, [0, 1, 2, 4, 3, 5], :]
    w_b = np.concatenate([a["w_kv"].reshape(D, 6, C).transpose(1, 0, 2).reshape(6 * D, C),
                          b_cols.transpose(1, 0, 2).reshape(6 * D, C)])
    columns = np.stack([a["norm_a"][0], a["kv_norm"], a["norm_b"][0], a["mem_norm"][0], a["mem_norm"][1]])
    rows = np.concatenate([a["k_norm_dil"], a["q_norm_b"][0], a["mem_q_norm"], a["mem_k_norm"]])
    caches = [a["cache_dil0_kv"], a["cache_dil1_kv"], a["cache_dil2_kv"]]
    dil = np.stack([c[:, ::d] for c, (_, d) in zip(caches, DIL)])
    mem = a["cache_mem_kv"]
    arrays = {
        "x_prompt": a["x_prompt"][0],
        "x_sample": a["x_sample"][:, 0],
        "mem_prompt": a["mem_prompt"][0],
        "w_a": w_a,
        "w_b": w_b,
        "w_mem": a["w_mem_kv"].reshape(2 * D, 2 * C),
        "w_out_a": a["w_out_a"][0],
        "w_out_b": a["w_out_b"][0],
        "gain_cols": columns.reshape(5, KD, P).transpose(2, 0, 1).reshape(P, 5 * KD),
        "gain_rows": np.tile(rows, (1, H)),
        "conv_small": np.concatenate([a["conv_w_a"][0].T, a["state_conv"][0].transpose(2, 1, 0).reshape(D, 2 * S)],
                                     axis=1),
        "cache_kt": mem[:, :, :, 0].transpose(0, 1, 4, 3, 2).reshape(2 * S * P, H * MEM),
        "cache_v": mem[:, :, :, 1].reshape(2, S, MEM, C),
        "dil_kt": dil[:, :, :, 0].transpose(0, 1, 4, 3, 2).reshape(3 * S * P, H * P),
        "dil_v": dil[:, :, :, 1].reshape(3 * S * P, C),
    }
    arrays = {k: layout(v) for k, v in arrays.items()}
    outs = {"y": (TS, D), "mem_kv": (2 * MEM, 2 * C), "tail": (D, 2), "tail_s": (D, 2 * S), "kv": (3, TS, 2 * C)}
    scratch = {"conv_t": (D, TS), "tok_a": (2, TS, C), "tok_b": (6, TS, C), "grp": (3 * T, OW), "x1": (TS, D)}
    nc = bacc.Bacc("TRN2", target_bir_lowering=False, num_devices=1)
    io = {}
    for name, v in arrays.items():
        io[name] = nc.dram_tensor(f"{name}_dram", v.shape, F32, kind="ExternalInput").ap()
    for name, shape in outs.items():
        io[name] = nc.dram_tensor(f"{name}_dram", shape, F32, kind="ExternalOutput").ap()
    for name, shape in scratch.items():
        io[name] = nc.dram_tensor(f"{name}_dram", shape, F32, kind="Internal").ap()
    build(nc, io)
    r = run_bass_kernel_spmd(nc, [{f"{k}_dram": v for k, v in arrays.items()}], core_ids=[0]).results[0]
    y, kv = r["y_dram"], r["kv_dram"].reshape(3, TS, 2, H, HD)
    heads = (2, H, HD)
    prompt = [kv[g, T - w:T][None] for g, (w, _) in enumerate(DIL)]
    sample = [kv[g, T:TS][:, None] for g in range(3)]
    return (
        y[0:T][None],
        y[T:TS][:, None],
        r["mem_kv_dram"].reshape(2, 1, MEM, *heads),
        layout(r["tail_dram"].T)[None, None],
        layout(r["tail_s_dram"].reshape(D, 2, S).transpose(2, 1, 0))[None],
        *(layout(p) for p in prompt),
        *(layout(s) for s in sample),
    )
```

```python
from contextlib import ExitStack

import concourse.bass as bass
import numpy as np
from concourse import mybir

F32 = mybir.dt.float32
F32R = mybir.dt.float32r
ACT = mybir.ActivationFunctionType
ALU = mybir.AluOpType
AX = mybir.AxisListType

P = 128
D = 1024
KD = D // P
T = 2048
NT = T // P
S = 8
TS = T + S
HD = 128
H = 4
C = H * HD
MEM = 256
MT = MEM // P
TB = 4
NW = TB * C // T * 512
EPS = 1e-6
NEG = -1e30
SCALE = HD ** -0.5
DIL = ((128, 1), (512, 4), (2048, 16))
OW = C + 2 * H
NCONV = KD


def ds(start, n):
    return bass.ds(start, n)


def pairs(eng, n, body):
    for u in range(2):
        body(0, u, True)
    if n > 2:
        with eng.Fori(1, n // 2) as q:
            for u in range(2):
                body(q, u, False)


class Core:

    def __init__(self, nc, ctx, io):
        self.nc, self.ctx, self.io = nc, ctx, io
        self.ps = ctx.enter_context(nc.psum_tensor("ps", [P, 8, 512], F32))
        self.ident = ctx.enter_context(nc.sbuf_tensor("ident", [P, P], F32))

    def sems(self, stack, tag, names):
        sems = [self.nc.alloc_semaphore(f"{tag}_{n}") for n in names.split()]
        stack.callback(self.nc.all_engine_barrier)
        stack.callback(self.nc.clear_and_free_semaphores, sems)
        return sems

    def sb(self, stack, name, shape, dt=F32):
        return stack.enter_context(self.nc.sbuf_tensor(name, shape, dt))


def setup_stage(core, gains):
    nc = core.nc
    with ExitStack() as st:
        zeroed, made, loaded = core.sems(st, "setup", "zeroed made loaded")
        block = st.enter_context(nc.Block())

        @block.gpsimd
        def _(pool):
            pool.memset(core.ident[:, :], 0.0).then_inc(zeroed, 1)
            pool.wait_ge(zeroed, 1)
            pool.affine_select(out=core.ident[:, :], in_=core.ident[:, :], compare_op=ALU.not_equal,
                               fill=1.0, base=0, pattern=[[-1, P]], channel_multiplier=1).then_inc(made, 1)
            pool.wait_ge(made, 1)

        @block.sync
        def _(sp):
            sp.dma_start(gains[:, :], core.io["gain_cols"]).then_inc(loaded, 16)
            sp.wait_ge(loaded, 16)


def split_weight_chunk_act(act, raw, w_hi, gain):
    return act.activation(w_hi, raw, ACT.Copy, scale=gain)


def split_weight_chunk_dve(dve, raw, w_hi, w_lo, gain):
    return dve.scalar_tensor_tensor(out=w_lo, in0=raw, scalar=gain, in1=w_hi,
                                    op0=ALU.mult, op1=ALU.subtract)


def split3(pe, acc, a_hi, a_lo, b_hi, b_lo, first, last):
    pe.matmul(acc, a_hi, b_hi, start=first, stop=False)
    pe.matmul(acc, a_hi, b_lo, start=False, stop=False)
    return pe.matmul(acc, a_lo, b_hi, start=False, stop=last)


def prep_stage(core, tag, x, x_s, xt_hi, xt_lo, w_src, w_hi, w_lo, gain):
    nc, ps, ident = core.nc, core.ps, core.ident
    U = 4
    with ExitStack() as st:
        xb = core.sb(st, f"{tag}_x", [P, U, D])
        xn = core.sb(st, f"{tag}_xn", [P, 2, D])
        raw = core.sb(st, f"{tag}_raw", [P, 4, C])
        stat = core.sb(st, f"{tag}_stat", [P, 2, 4])
        sems = core.sems(st, tag, "x_in0 x_in1 x_in2 x_in3 raw_in0 raw_in1 raw_in2 raw_in3 squared rooted inverted "
                                  "scaled turned hi_done lo_done w_hi_done w_lo_done")
        x_in, raw_in = sems[0:4], sems[4:8]
        squared, rooted, inverted, scaled, turned, hi_done, lo_done, w_hi_done, w_lo_done = sems[8:]
        block = st.enter_context(nc.Block())

        def turns(eng, body):
            for u in range(U):
                body(0, u, True)
            with eng.Fori(1, NT // U) as q:
                for u in range(U):
                    body(q, u, False)

        @block.sync
        def _(sp):
            for k in range(4):
                sp.dma_start(raw[:, k, :], w_src[k * P:(k + 1) * P, :]).then_inc(raw_in[k], 16)

            def load(q, u, first):
                if not first:
                    sp.wait_ge(scaled, q * U + (u - U + 1))
                sp.dma_start(xb[:, u, :], x[ds(q * (U * P) + u * P, P), :]).then_inc(x_in[u], 16)
                if first:
                    sp.wait_ge(w_lo_done, u + 1)
                    sp.dma_start(raw[:, u, :], w_src[(4 + u) * P:(5 + u) * P, :]).then_inc(raw_in[u], 16)
            turns(sp, load)
            sp.wait_ge(scaled, NT - U + 1)
            sp.dma_start(xb[0:S, 0, :], x_s).then_inc(x_in[0], 16)

        @block.scalar
        def _(act):
            def square(q, u, first, n=P):
                act.wait_ge(x_in[u], q * 16 + 16)
                if not first or u >= 2:
                    act.wait_ge(turned, q * U + (u - 1))
                act.activation(xn[0:n, u % 2, :], xb[0:n, u, :], ACT.Square,
                               accum_out=stat[0:n, u % 2, 0:1]).then_inc(squared, 1)
                act.wait_ge(squared, q * U + (u + 1))
                act.activation(stat[0:n, u % 2, 1:2], stat[0:n, u % 2, 0:1], ACT.Sqrt, scale=1.0 / D,
                               bias=EPS).then_inc(rooted, 1)

            def high(q, u, n=P):
                u2 = u % 2
                act.wait_ge(turned, q * U + (u + 1))
                act.activation(xt_hi[:, :, ds(q * (U * P) + u * P, n)],
                               ps[:, 2 * u2:2 * u2 + 2, :].rearrange("p a (b t) -> p (a b) t", t=P)[:, :, 0:n],
                               ACT.Copy).then_inc(hi_done, 1)

            def split(k):
                act.wait_ge(raw_in[k % 4], 16 * (k // 4 + 1))
                split_weight_chunk_act(act, raw[:, k % 4, :], w_hi[:, k, :], gain[:, k:k + 1]).then_inc(w_hi_done, 1)

            def step(q, u, first):
                square(q, u, first)
                if u:
                    high(q, u - 1)
                elif not first:
                    high(q - 1, U - 1)
                if first:
                    split(4 + u)
            for k in range(4):
                split(k)
            turns(act, step)
            square(NT // U, 0, False, S)
            high(NT // U - 1, U - 1)
            high(NT // U, 0, S)

        @block.vector
        def _(dve):
            def scale(q, u, first, n=P):
                u2 = u % 2
                dve.wait_ge(rooted, q * U + (u + 1))
                dve.reciprocal(stat[0:n, u2, 2:3], stat[0:n, u2, 1:2]).then_inc(inverted, 1)
                dve.wait_ge(inverted, q * U + (u + 1))
                dve.tensor_scalar(xn[0:n, u2, :], xb[0:n, u, :], stat[0:n, u2, 2:3], None,
                                  ALU.mult).then_inc(scaled, 1)

            def low(q, u, n=P):
                u2 = u % 2
                dve.wait_ge(hi_done, q * U + (u + 1))
                dve.tensor_tensor(xt_lo[:, :, ds(q * (U * P) + u * P, n)],
                                  ps[:, 2 * u2:2 * u2 + 2, :].rearrange("p a (b t) -> p (a b) t", t=P)[:, :, 0:n],
                                  xt_hi[:, :, ds(q * (U * P) + u * P, n)], ALU.subtract).then_inc(lo_done, 1)

            def split(k):
                dve.wait_ge(w_hi_done, k + 1)
                split_weight_chunk_dve(dve, raw[:, k % 4, :], w_hi[:, k, :], w_lo[:, k, :],
                                       gain[:, k:k + 1]).then_inc(w_lo_done, 1)

            def step(q, u, first):
                scale(q, u, first)
                if u:
                    low(q, u - 1)
                elif not first:
                    low(q - 1, U - 1)
                if first:
                    split(4 + u)
            for k in range(4):
                split(k)
            turns(dve, step)
            scale(NT // U, 0, False, S)
            low(NT // U - 1, U - 1)
            low(NT // U, 0, S)
            dve.wait_ge(w_lo_done, KD)

        @block.tensor
        def _(pe):
            def step(q, u, first, n=P):
                u2 = u % 2
                pe.wait_ge(scaled, q * U + (u + 1))
                if not first or u >= 2:
                    pe.wait_ge(lo_done, q * U + (u - 1))
                for k in range(KD):
                    at = (k % 4) * P
                    t = pe.transpose(ps[:, 2 * u2 + k // 4, at:at + n], xn[0:n, u2, k * P:(k + 1) * P],
                                     ident[0:n, 0:n])
                t.then_inc(turned, 1)
            turns(pe, step)
            step(NT // U, 0, False, S)


def conv_stage(core, w_all, xt_hi, xt_lo, wh, wl, gain):
    nc, ps, io = core.nc, core.ps, core.io
    tail_s = io["tail_s"].rearrange("s (a c) -> s a c", a=2)
    OPS = 7
    BOPS = TB * OPS + 9
    BMUL = TB * 4 + 1
    W0, W1, W2, S0, S1 = range(5)
    with ExitStack() as st:
        raw = core.sb(st, "conv_raw", [P, 2, C])
        u = core.sb(st, "conv_u", [P, 2, 2 + 512])
        t = core.sb(st, "conv_gate", [P, 512])
        o = core.sb(st, "conv_o", [P, 512])
        taps = core.sb(st, "conv_taps", [P, 2, 3])
        rows = core.sb(st, "conv_rows", [S, 5, P])
        u_s = u[0:S, 0, 2:2 + P]
        (raw_in0, raw_in1, taps_in0, taps_in1, rows_in, w_hi_done, w_lo_done, multiplied, c_copied, tapped,
         gated, ops, o_out, block_out) = core.sems(
            st, "conv", "raw_in0 raw_in1 taps_in0 taps_in1 rows_in w_hi_done w_lo_done multiplied c_copied "
                        "tapped gated ops o_out block_out")
        raw_in, taps_in = (raw_in0, raw_in1), (taps_in0, taps_in1)
        block = st.enter_context(nc.Block())
        BOUT = 4 * 16

        def loop(eng, body):
            body(0, True)
            with eng.Fori(1, NCONV // 2) as q:
                body(q, False)

        @block.sync
        def _(sp):
            def body(q, first):
                for j in range(2):
                    if not first:
                        sp.wait_ge(ops, (q * 2 + (j - 1)) * BOPS)
                    sp.dma_start(taps[:, j, :], io["conv_taps"][ds((q * 2 + j) * P, P), :]).then_inc(taps_in[j], 16)
                    for k in range(KD):
                        if not (first and j == 0 and k < 2):
                            sp.wait_ge(w_lo_done, q * (2 * KD) + (j * KD + k - 1))
                        sp.dma_start(raw[:, k % 2, :],
                                     w_all[ds((q * 2 + (j + 1)) * D + k * P, P), :]).then_inc(raw_in[k % 2], 16)
                        if k == 3:
                            if not (first and j == 0):
                                sp.wait_ge(block_out, (q * 2 + j) * BOUT)
                            sp.dma_start(rows[:, :, :].rearrange("s a c -> s (a c)"),
                                         io["conv_rows"][ds((q * 2 + j) * S, S), :]).then_inc(rows_in, 16)
            loop(sp, body)

        @block.gpsimd
        def _(pool):
            def body(q, first):
                for j in range(2):
                    blk = q * 2 + j
                    for b in range(TB):
                        pool.wait_ge(ops, blk * BOPS + (b + 1) * OPS)
                        pool.dma_start(io["conv_t"][ds(blk * P, P), b * 512:(b + 1) * 512], o[:, :]
                                       ).then_inc(o_out, 16)
                    pool.dma_start(io["tail"][ds(blk * P, P), :], u[:, 1, 512:514]).then_inc(block_out, 16)
                    pool.wait_ge(ops, (blk + 1) * BOPS)
                    pool.dma_start(io["conv_s"][:, ds(blk * P, P)], rows[:, W0, :]).then_inc(block_out, 16)
                    pool.dma_start(tail_s[:, 0, ds(blk * P, P)], rows[:, S1, :]).then_inc(block_out, 16)
                    pool.dma_start(tail_s[:, 1, ds(blk * P, P)], u_s).then_inc(block_out, 16)
            loop(pool, body)
            pool.wait_ge(o_out, 16 * NCONV * TB)
            pool.wait_ge(block_out, BOUT * NCONV)

        @block.scalar
        def _(act):
            def split(q, j, k):
                act.wait_ge(raw_in[k % 2], q * (KD * 16) + (j * (KD // 2) + k // 2 + 1) * 16)
                split_weight_chunk_act(act, raw[:, k % 2, :], wh[1 - j][:, k, :], gain[:, k:k + 1]
                                       ).then_inc(w_hi_done, 1)

            def body(q, first):
                for j in range(2):
                    blk = q * 2 + j
                    begun = not (first and j == 0)
                    for b in range(TB):
                        slot = (j * (TB + 1) + b) % 2
                        step = blk * TB + b
                        u_new = u[:, b % 2, 2:514]
                        act.wait_ge(multiplied, blk * BMUL + b * 4 + 1)
                        if begun or b:
                            act.wait_ge(ops, blk * BOPS + b * OPS)
                        if b == 0 and begun:
                            act.wait_ge(block_out, blk * BOUT)
                        act.activation(u_new, ps[:, slot * 4, :], ACT.Copy).then_inc(c_copied, 1)
                        act.wait_ge(ops, blk * BOPS + (b * OPS + 2))
                        if begun or b:
                            act.wait_ge(o_out, step * 16)
                        if b == 0:
                            act.wait_ge(taps_in[j], q * 16 + 16)
                        act.activation(o[:, :], u_new, ACT.Copy, scale=taps[:, j, 2:3]).then_inc(tapped, 1)
                        act.wait_ge(multiplied, blk * BMUL + b * 4 + 3)
                        act.activation(t[:, :], ps[:, slot * 4 + 2, :], ACT.Sigmoid).then_inc(gated, 1)
                        split(q, j, 2 * b)
                        split(q, j, 2 * b + 1)
                    slot = (j * (TB + 1) + TB) % 2
                    act.wait_ge(multiplied, (blk + 1) * BMUL)
                    act.wait_ge(ops, blk * BOPS + TB * OPS)
                    act.activation(u_s, ps[0:S, slot * 4, 0:P], ACT.Copy).then_inc(c_copied, 1)
                    act.activation(t[0:S, 0:P], ps[0:S, slot * 4, 2 * P:3 * P], ACT.Sigmoid).then_inc(gated, 1)
            loop(act, body)

        @block.vector
        def _(dve):
            def split(q, j, k):
                dve.wait_ge(w_hi_done, q * (2 * KD) + (j * KD + k + 1))
                split_weight_chunk_dve(dve, raw[:, k % 2, :], wh[1 - j][:, k, :], wl[1 - j][:, k, :],
                                       gain[:, k:k + 1]).then_inc(w_lo_done, 1)

            def body(q, first):
                for j in range(2):
                    blk = q * 2 + j
                    for b in range(TB):
                        slot = (j * (TB + 1) + b) % 2
                        at = blk * BOPS + b * OPS
                        u_new, u_one, u_two = (u[:, b % 2, n:n + 512] for n in (2, 1, 0))
                        if b == 0:
                            dve.wait_ge(taps_in[j], q * 16 + 16)
                        if b == 0:
                            dve.memset(u[:, 0, 0:2], 0.0).then_inc(ops, 1)
                        else:
                            dve.tensor_copy(u[:, b % 2, 0:2], u[:, 1 - b % 2, 512:514]).then_inc(ops, 1)
                        dve.wait_ge(c_copied, blk * (TB + 1) + (b + 1))
                        dve.wait_ge(multiplied, blk * BMUL + b * 4 + 2)
                        dve.tensor_tensor(u_new, ps[:, slot * 4 + 1, :], u_new, ALU.mult).then_inc(ops, 1)
                        dve.wait_ge(tapped, blk * TB + (b + 1))
                        dve.wait_ge(ops, at + 2)
                        dve.scalar_tensor_tensor(out=o[:, :], in0=u_one, scalar=taps[:, j, 1:2], in1=o[:, :],
                                                 op0=ALU.mult, op1=ALU.add).then_inc(ops, 1)
                        dve.wait_ge(ops, at + 3)
                        dve.scalar_tensor_tensor(out=o[:, :], in0=u_two, scalar=taps[:, j, 0:1], in1=o[:, :],
                                                 op0=ALU.mult, op1=ALU.add).then_inc(ops, 1)
                        dve.wait_ge(gated, blk * (TB + 1) + (b + 1))
                        dve.tensor_tensor(t[:, :], ps[:, slot * 4 + 2, :], t[:, :], ALU.mult).then_inc(ops, 1)
                        dve.wait_ge(multiplied, blk * BMUL + b * 4 + 4)
                        dve.wait_ge(ops, at + 5)
                        dve.tensor_tensor(t[:, :], ps[:, slot * 4 + 3, :], t[:, :], ALU.mult).then_inc(ops, 1)
                        dve.wait_ge(ops, at + 6)
                        dve.tensor_tensor(o[:, :], o[:, :], t[:, :], ALU.mult).then_inc(ops, 1)
                        split(q, j, 2 * b)
                        split(q, j, 2 * b + 1)
                    slot = (j * (TB + 1) + TB) % 2
                    at = blk * BOPS + TB * OPS
                    row = lambda n: rows[:, n, :]
                    z = lambda n: ps[0:S, slot * 4, n * P:(n + 1) * P]
                    dve.wait_ge(rows_in, (blk + 1) * 16)
                    dve.tensor_tensor(row(W0), row(S0), row(W0), ALU.mult).then_inc(ops, 1)
                    dve.tensor_tensor(row(W1), row(S1), row(W1), ALU.mult).then_inc(ops, 1)
                    dve.wait_ge(c_copied, (blk + 1) * (TB + 1))
                    dve.wait_ge(gated, (blk + 1) * (TB + 1))
                    dve.wait_ge(ops, at + 2)
                    dve.tensor_tensor(row(W0), row(W0), row(W1), ALU.add).then_inc(ops, 1)
                    dve.tensor_tensor(u_s, z(1), u_s, ALU.mult).then_inc(ops, 1)
                    dve.wait_ge(ops, at + 4)
                    dve.tensor_tensor(row(W2), u_s, row(W2), ALU.mult).then_inc(ops, 1)
                    dve.tensor_tensor(t[0:S, 0:P], z(2), t[0:S, 0:P], ALU.mult).then_inc(ops, 1)
                    dve.wait_ge(ops, at + 6)
                    dve.tensor_tensor(row(W0), row(W0), row(W2), ALU.add).then_inc(ops, 1)
                    dve.tensor_tensor(t[0:S, 0:P], z(3), t[0:S, 0:P], ALU.mult).then_inc(ops, 1)
                    dve.wait_ge(ops, at + 8)
                    dve.tensor_tensor(row(W0), row(W0), t[0:S, 0:P], ALU.mult).then_inc(ops, 1)
            loop(dve, body)
            dve.wait_ge(w_lo_done, NCONV * KD)

        @block.tensor
        def _(pe):
            def body(q, first):
                for j in range(2):
                    blk = q * 2 + j
                    begun = not (first and j == 0)
                    if begun:
                        pe.wait_ge(w_lo_done, blk * KD)
                    for b in range(TB):
                        slot = (j * (TB + 1) + b) % 2
                        if b >= 1 and (begun or b >= 2):
                            pe.wait_ge(ops, blk * BOPS + (b - 1) * OPS)
                        elif b == 0 and begun:
                            pe.wait_ge(ops, (blk - 1) * BOPS + TB * OPS)
                        for part in range(4):
                            for k in range(KD):
                                cols, toks = slice(part * P, (part + 1) * P), slice(b * 512, (b + 1) * 512)
                                m = split3(pe, ps[:, slot * 4 + part, :], wh[j][:, k, cols], wl[j][:, k, cols],
                                           xt_hi[:, k, toks], xt_lo[:, k, toks], k == 0, k == KD - 1)
                            m.then_inc(multiplied, 1)
                    slot = (j * (TB + 1) + TB) % 2
                    pe.wait_ge(ops, blk * BOPS + (TB - 1) * OPS)
                    for k in range(KD):
                        m = split3(pe, ps[0:S, slot * 4, :], xt_hi[:, k, T:TS], xt_lo[:, k, T:TS],
                                   wh[j][:, k, :], wl[j][:, k, :], k == 0, k == KD - 1)
                    m.then_inc(multiplied, 1)
            loop(pe, body)


def tokens_stage(core, tag, w_all, blocks, xt_hi, xt_lo, wh, wl):
    nc, ps, io = core.nc, core.ps, core.io
    N = NT + 1
    count = lambda b, kind: sum(blk[0] == kind for blk in blocks[:b])
    with ExitStack() as st:
        raw = core.sb(st, f"{tag}_raw", [P, 2, C])
        o = core.sb(st, f"{tag}_o", [P, 2, C])
        grow = core.sb(st, f"{tag}_grow", [P, C])
        stat = core.sb(st, f"{tag}_stat", [P, 2, 3, H])
        (raw_in0, raw_in1, grow_in, w_hi_done, w_lo_done, multiplied, squared, acted, inverted, o_done,
         o_out0, o_out1) = core.sems(
            st, tag, "raw_in0 raw_in1 grow_in w_hi_done w_lo_done multiplied squared acted inverted "
                     "o_done o_out0 o_out1")
        raw_in, o_out = (raw_in0, raw_in1), (o_out0, o_out1)
        block = st.enter_context(nc.Block())
        rows = lambda i: P if i < NT else S

        @block.sync
        def _(sp):
            for b, (kind, dst, gain, g) in enumerate(blocks):
                if kind == "norm":
                    if b:
                        sp.wait_ge(o_done, b * N)
                    sp.dma_start(grow[:, :], io["gain_rows"][g:g + 1, :].to_broadcast([P, C])).then_inc(grow_in, 16)
                if gain is not None:
                    for k in range(KD):
                        if b * KD + k >= 2:
                            sp.wait_ge(w_lo_done, b * KD + k - 1)
                        sp.dma_start(raw[:, k % 2, :], w_all[b * D + k * P:b * D + (k + 1) * P, :]
                                     ).then_inc(raw_in[k % 2], 16)

        @block.gpsimd
        def _(pool):
            for b, (kind, dst, gain, g) in enumerate(blocks):
                for i in range(N):
                    n, tile = rows(i), b * N + i
                    pool.wait_ge(o_done, tile + 1)
                    pool.dma_start(dst[i * P:i * P + n, :], o[0:n, tile % 2, :]).then_inc(o_out[tile % 2], 16)
            for slot in range(2):
                pool.wait_ge(o_out[slot], 16 * ((len(blocks) * N + 1 - slot) // 2))

        @block.scalar
        def _(act):
            for b, (kind, dst, gain, g) in enumerate(blocks):
                for i in range(N):
                    n, tile = rows(i), b * N + i
                    slot = tile % 2
                    act.wait_ge(multiplied, tile + 1)
                    if kind != "copy" and tile >= 2:
                        act.wait_ge(o_out[slot], 16 * (tile // 2))
                    if kind == "norm":
                        for h in range(H):
                            cols = slice(h * HD, (h + 1) * HD)
                            sq = act.activation(o[0:n, slot, cols], ps[0:n, slot, cols], ACT.Square,
                                                accum_out=stat[0:n, slot, 0, h:h + 1])
                        sq.then_inc(squared, 1)
                        act.wait_ge(squared, count(b, "norm") * N + i + 1)
                        act.activation(stat[0:n, slot, 1, :], stat[0:n, slot, 0, :], ACT.Sqrt, scale=1.0 / HD,
                                       bias=EPS).then_inc(acted, 1)
                    if kind == "silu":
                        act.activation(o[0:n, slot, :], ps[0:n, slot, :], ACT.Sigmoid).then_inc(acted, 1)
                    if gain is not None and i % 2 == 1:
                        k = i // 2
                        act.wait_ge(raw_in[k % 2], 16 * (b * KD // 2 + k // 2 + 1))
                        split_weight_chunk_act(act, raw[:, k % 2, :], wh[1 - b % 2][:, k, :],
                                               gain[:, k:k + 1]).then_inc(w_hi_done, 1)

        @block.vector
        def _(dve):
            for b, (kind, dst, gain, g) in enumerate(blocks):
                if kind == "norm":
                    dve.wait_ge(grow_in, 16 * (count(b, "norm") + 1))
                for i in range(N):
                    n, tile = rows(i), b * N + i
                    slot = tile % 2
                    if kind == "copy":
                        dve.wait_ge(multiplied, tile + 1)
                        if tile >= 2:
                            dve.wait_ge(o_out[slot], 16 * (tile // 2))
                        dve.tensor_copy(o[0:n, slot, :], ps[0:n, slot, :]).then_inc(o_done, 1)
                    else:
                        dve.wait_ge(acted, (b - count(b, "copy")) * N + i + 1)
                    if kind == "silu":
                        dve.tensor_tensor(o[0:n, slot, :], ps[0:n, slot, :], o[0:n, slot, :],
                                          ALU.mult).then_inc(o_done, 1)
                    if kind == "norm":
                        dve.reciprocal(stat[0:n, slot, 2, :], stat[0:n, slot, 1, :]).then_inc(inverted, 1)
                        dve.wait_ge(inverted, count(b, "norm") * N + i + 1)
                        for h in range(H):
                            cols = slice(h * HD, (h + 1) * HD)
                            m = dve.scalar_tensor_tensor(out=o[0:n, slot, cols], in0=ps[0:n, slot, cols],
                                                         scalar=stat[0:n, slot, 2, h:h + 1], in1=grow[0:n, cols],
                                                         op0=ALU.mult, op1=ALU.mult)
                        m.then_inc(o_done, 1)
                    if gain is not None and i % 2 == 1:
                        k = i // 2
                        dve.wait_ge(w_hi_done, b * KD + k + 1)
                        split_weight_chunk_dve(dve, raw[:, k % 2, :], wh[1 - b % 2][:, k, :],
                                               wl[1 - b % 2][:, k, :], gain[:, k:k + 1]).then_inc(w_lo_done, 1)

        @block.tensor
        def _(pe):
            for b in range(len(blocks)):
                if b:
                    pe.wait_ge(w_lo_done, b * KD)
                for i in range(N):
                    n, tile = rows(i), b * N + i
                    if tile >= 2:
                        pe.wait_ge(o_done, tile - 1)
                    acc = ps[0:n, tile % 2, :]
                    for k in range(KD):
                        x_hi = xt_hi[:, k, i * P:i * P + n]
                        x_lo = xt_lo[:, k, i * P:i * P + n]
                        pe.matmul(acc, x_hi, wh[b % 2][:, k, :], start=(k == 0), stop=False)
                        pe.matmul(acc, x_hi, wl[b % 2][:, k, :], start=False, stop=False)
                        m = pe.matmul(acc, x_lo, wh[b % 2][:, k, :], start=False, stop=(k == KD - 1))
                    m.then_inc(multiplied, 1)


def memkv_stage(core, layer, w_mem, out_kv, wo_src, wo_chunks, wo_hi, wo_lo, kt_hi, kt_lo, v_hi, v_lo,
                mem_gain, norm_row):
    nc, ps, io, ident = core.nc, core.ps, core.io, core.ident
    tag = f"memkv{layer}"
    NB = 2
    with ExitStack() as st:
        mem = core.sb(st, f"{tag}_mem", [P, MT, D])
        mn = core.sb(st, f"{tag}_mn", [P, MT, D])
        mt_hi = core.sb(st, f"{tag}_mthi", [P, KD, MEM], F32R)
        mt_lo = core.sb(st, f"{tag}_mtlo", [P, KD, MEM], F32R)
        raw = core.sb(st, f"{tag}_raw", [P, 4, C])
        mw_hi = core.sb(st, f"{tag}_mwhi", [P, 4, C], F32R)
        mw_lo = core.sb(st, f"{tag}_mwlo", [P, 4, C], F32R)
        kv = core.sb(st, f"{tag}_kv", [P, NB, MT, C])
        grow = core.sb(st, f"{tag}_grow", [P, C])
        stat = core.sb(st, f"{tag}_stat", [P, MT, 3, H + 1])
        names = ("mem_in grow_in raw_in0 raw_in1 raw_in2 raw_in3 squared rooted inverted scaled turned "
                 "hi_done lo_done w_hi_done w_lo_done multiplied ksquared krooted kinverted kv_done v_hi_done "
                 "kturned khi_done klo_done v_lo_done kv_out")
        (mem_in, grow_in, raw_in0, raw_in1, raw_in2, raw_in3, squared, rooted, inverted, scaled, turned,
         hi_done, lo_done, w_hi_done, w_lo_done, multiplied, ksquared, krooted, kinverted, kv_done, v_hi_done,
         kturned, khi_done, klo_done, v_lo_done, kv_out) = core.sems(st, tag, names)
        raw_in = (raw_in0, raw_in1, raw_in2, raw_in3)
        block = st.enter_context(nc.Block())
        MEMC = KD * NB
        TOTAL = MEMC + 2 * wo_chunks

        def chunk_source(c):
            if c < MEMC:
                k, b = c // NB, c % NB
                return w_mem[k * P:(k + 1) * P, b * C:(b + 1) * C]
            k, half = (c - MEMC) // 2, (c - MEMC) % 2
            return wo_src[k * P:(k + 1) * P, half * C:(half + 1) * C]

        def chunk_split(c):
            if c < MEMC:
                return mw_hi[:, c % 4, :], mw_lo[:, c % 4, :]
            k, half = (c - MEMC) // 2, (c - MEMC) % 2
            cols = slice(half * C, (half + 1) * C)
            return wo_hi[:, k, cols], wo_lo[:, k, cols]

        @block.sync
        def _(sp):
            sp.dma_start(mem[:, :, :], io["mem_prompt"].rearrange("(m p) d -> p m d", p=P)).then_inc(mem_in, 16)
            sp.dma_start(grow[:, :], io["gain_rows"][norm_row:norm_row + 1, :].to_broadcast([P, C])
                         ).then_inc(grow_in, 16)
            for c in range(TOTAL):
                if c >= 4:
                    sp.wait_ge(w_lo_done, c - 3)
                sp.dma_start(raw[:, c % 4, :], chunk_source(c)).then_inc(raw_in[c % 4], 16)

        @block.gpsimd
        def _(pool):
            for b in range(NB):
                for m in range(MT):
                    pool.wait_ge(kv_done, b * MT + m + 1)
                    pool.dma_start(out_kv[m * P:(m + 1) * P, b * C:(b + 1) * C], kv[:, b, m, :]
                                   ).then_inc(kv_out, 16)
            pool.wait_ge(kv_out, 16 * NB * MT)

        @block.scalar
        def _(act):
            act.wait_ge(mem_in, 16)
            for m in range(MT):
                act.activation(mn[:, m, :], mem[:, m, :], ACT.Square,
                               accum_out=stat[:, m, 0, H:H + 1]).then_inc(squared, 1)
            for m in range(MT):
                act.wait_ge(squared, m + 1)
                act.activation(stat[:, m, 1, H:H + 1], stat[:, m, 0, H:H + 1], ACT.Sqrt, scale=1.0 / D,
                               bias=EPS).then_inc(rooted, 1)
            for m in range(MT):
                act.wait_ge(turned, m + 1)
                act.activation(mt_hi[:, :, m * P:(m + 1) * P],
                               ps[:, 2 * m:2 * m + 2, :].rearrange("p a (b t) -> p (a b) t", t=P),
                               ACT.Copy).then_inc(hi_done, 1)

            def split(c):
                act.wait_ge(raw_in[c % 4], 16 * (c // 4 + 1))
                if 4 <= c < MEMC:
                    act.wait_ge(multiplied, c - 3)
                scale = mem_gain[:, c // NB:c // NB + 1] if c < MEMC else 1.0
                split_weight_chunk_act(act, raw[:, c % 4, :], chunk_split(c)[0], scale).then_inc(w_hi_done, 1)
            for c in range(MEMC):
                split(c)
            act.wait_ge(multiplied, MEMC)
            for m in range(MT):
                for h in range(H):
                    sq = act.activation(kv[:, 0, m, h * HD:(h + 1) * HD], ps[:, 4 + m, h * HD:(h + 1) * HD],
                                        ACT.Square, accum_out=stat[:, m, 0, h:h + 1])
                sq.then_inc(ksquared, 1)
            for m in range(MT):
                act.wait_ge(ksquared, m + 1)
                act.activation(stat[:, m, 1, 0:H], stat[:, m, 0, 0:H], ACT.Sqrt, scale=1.0 / HD,
                               bias=EPS).then_inc(krooted, 1)
            for m in range(MT):
                act.activation(v_hi[:, m, :], ps[:, 6 + m, :], ACT.Copy).then_inc(v_hi_done, 1)
            act.wait_ge(kturned, 1)
            act.activation(kt_hi[:, :, :].rearrange("p h m -> p (h m)"),
                           ps[:, 0:2, :].rearrange("p a b -> p (a b)"), ACT.Copy).then_inc(khi_done, 1)
            for c in range(MEMC, TOTAL):
                split(c)

        @block.vector
        def _(dve):
            for m in range(MT):
                dve.wait_ge(rooted, m + 1)
                dve.reciprocal(stat[:, m, 2, H:H + 1], stat[:, m, 1, H:H + 1]).then_inc(inverted, 1)
                dve.wait_ge(inverted, m + 1)
                dve.tensor_scalar(mn[:, m, :], mem[:, m, :], stat[:, m, 2, H:H + 1], None, ALU.mult
                                  ).then_inc(scaled, 1)
            for m in range(MT):
                dve.wait_ge(hi_done, m + 1)
                dve.tensor_tensor(mt_lo[:, :, m * P:(m + 1) * P],
                                  ps[:, 2 * m:2 * m + 2, :].rearrange("p a (b t) -> p (a b) t", t=P),
                                  mt_hi[:, :, m * P:(m + 1) * P], ALU.subtract).then_inc(lo_done, 1)

            def split(c):
                dve.wait_ge(w_hi_done, c + 1)
                scale = mem_gain[:, c // NB:c // NB + 1] if c < MEMC else 1.0
                split_weight_chunk_dve(dve, raw[:, c % 4, :], *chunk_split(c), scale).then_inc(w_lo_done, 1)
            for c in range(MEMC):
                split(c)
            dve.wait_ge(grow_in, 16)
            for m in range(MT):
                dve.wait_ge(krooted, m + 1)
                dve.reciprocal(stat[:, m, 2, 0:H], stat[:, m, 1, 0:H]).then_inc(kinverted, 1)
                dve.wait_ge(kinverted, m + 1)
                for h in range(H):
                    cols = slice(h * HD, (h + 1) * HD)
                    k = dve.scalar_tensor_tensor(out=kv[:, 0, m, cols], in0=ps[:, 4 + m, cols],
                                                 scalar=stat[:, m, 2, h:h + 1], in1=grow[:, cols],
                                                 op0=ALU.mult, op1=ALU.mult)
                k.then_inc(kv_done, 1)
            for m in range(MT):
                dve.wait_ge(v_hi_done, m + 1)
                dve.tensor_copy(kv[:, 1, m, :], ps[:, 6 + m, :]).then_inc(kv_done, 1)
                dve.tensor_tensor(v_lo[:, m, :], ps[:, 6 + m, :], v_hi[:, m, :], ALU.subtract).then_inc(v_lo_done, 1)
            dve.wait_ge(khi_done, 1)
            dve.tensor_tensor(kt_lo[:, :, :].rearrange("p h m -> p (h m)"),
                              ps[:, 0:2, :].rearrange("p a b -> p (a b)"),
                              kt_hi[:, :, :].rearrange("p h m -> p (h m)"), ALU.subtract).then_inc(klo_done, 1)
            for c in range(MEMC, TOTAL):
                split(c)
            dve.wait_ge(w_lo_done, TOTAL)

        @block.tensor
        def _(pe):
            for m in range(MT):
                pe.wait_ge(scaled, m + 1)
                for k in range(KD):
                    at = (k % 4) * P
                    t = pe.transpose(ps[:, 2 * m + k // 4, at:at + P], mn[:, m, k * P:(k + 1) * P], ident[:, :])
                t.then_inc(turned, 1)
            pe.wait_ge(lo_done, MT)
            for c in range(MEMC):
                k, b = c // NB, c % NB
                pe.wait_ge(w_lo_done, c + 1)
                for m in range(MT):
                    acc = ps[:, 4 + 2 * b + m, :]
                    x_hi, x_lo = mt_hi[:, k, m * P:(m + 1) * P], mt_lo[:, k, m * P:(m + 1) * P]
                    pe.matmul(acc, x_hi, mw_hi[:, c % 4, :], start=(k == 0), stop=False)
                    pe.matmul(acc, x_hi, mw_lo[:, c % 4, :], start=False, stop=False)
                    mm = pe.matmul(acc, x_lo, mw_hi[:, c % 4, :], start=False, stop=(k == KD - 1))
                mm.then_inc(multiplied, 1)
            pe.wait_ge(kv_done, MT)
            for h in range(H):
                for m in range(MT):
                    at = (h % 2) * MEM + m * P
                    t = pe.transpose(ps[:, h // 2, at:at + P], kv[:, 0, m, h * HD:(h + 1) * HD], ident[:, :])
            t.then_inc(kturned, 1)


def out_stage(core, layer, src, x, y, wo_hi, wo_lo, kt_hi, kt_lo, v_hi, v_lo):
    nc, ps, ident = core.nc, core.ps, core.ident
    tag = f"out{layer}"
    conv = layer == 0
    MIX = KD if conv else H
    KO = MIX + H
    with ExitStack() as st:
        q_b = core.sb(st, f"{tag}_q", [P, 2, C])
        g_b = core.sb(st, f"{tag}_g", [P, 2, C])
        x_b = core.sb(st, f"{tag}_x", [P, 2, D])
        qt_hi = core.sb(st, f"{tag}_qthi", [P, C], F32R)
        qt_lo = core.sb(st, f"{tag}_qtlo", [P, C], F32R)
        prob = core.sb(st, f"{tag}_prob", [P, H, MEM])
        pt_hi = core.sb(st, f"{tag}_pthi", [P, H * MT, P], F32R)
        pt_lo = core.sb(st, f"{tag}_ptlo", [P, H * MT, P], F32R)
        og = core.sb(st, f"{tag}_og", [P, C])
        cat_hi = core.sb(st, f"{tag}_cathi", [P, 2, KO, P], F32R)
        cat_lo = core.sb(st, f"{tag}_catlo", [P, 2, KO, P], F32R)
        y_b = core.sb(st, f"{tag}_y", [P, 2, D])
        stat = core.sb(st, f"{tag}_stat", [P, 4, H])
        if conv:
            c_b = core.sb(st, f"{tag}_c", [P, 2, KD, P])
        else:
            grp = core.sb(st, f"{tag}_grp", [P, 2, 3, OW])
            gd_b = core.sb(st, f"{tag}_gd", [P, 2, C])
            od = core.sb(st, f"{tag}_od", [P, C])
            cstat = core.sb(st, f"{tag}_cstat", [P, 6, 3 * H])
        names = ("q_in0 q_in1 g_in0 g_in1 x_in0 x_in1 m_in0 m_in1 y_out0 y_out1 qturned qhi_done qlo_done "
                 "scored maxed biased exped inverted pturned phi_done plo_done summed og_done oturned ohi_done "
                 "olo_done mhi_done mlo_done left_done right_done left_added right_added mturned ops cexp")
        (q_in0, q_in1, g_in0, g_in1, x_in0, x_in1, m_in0, m_in1, y_out0, y_out1, qturned, qhi_done, qlo_done,
         scored, maxed, biased, exped, inverted, pturned, phi_done, plo_done, summed, og_done, oturned, ohi_done,
         olo_done, mhi_done, mlo_done, left_done, right_done, left_added, right_added, mturned, ops, cexp
         ) = core.sems(st, tag, names)
        q_in, g_in, x_in, m_in, y_out = (q_in0, q_in1), (g_in0, g_in1), (x_in0, x_in1), (m_in0, m_in1), (y_out0, y_out1)
        MLOADS = 1 if conv else 4
        COPS = 10
        block = st.enter_context(nc.Block())
        LAST = (NT // 2 - 1, 1)

        def before(q, u):
            return (q, 0) if u else (q - 1, 1)

        def count(q, u, extra=1):
            return q * 2 + (u + extra)

        @block.sync
        def _(sp):
            def load(q, u, first, second=False):
                n = q * (2 * P) + u * P
                if second and u == 0:
                    sp.wait_ge(og_done, 1)
                elif not first:
                    sp.wait_ge(right_added, count(q, u, -2))
                sp.dma_start(q_b[:, u, :], src["q"][ds(n, P), :]).then_inc(q_in[u], 16)
                if conv:
                    sp.dma_start(c_b[:, u, :, :], src["conv_t"].rearrange("(k p) t -> p k t", p=P)[:, :, ds(n, P)]
                                 ).then_inc(m_in[u], 16)
                else:
                    sp.dma_start(gd_b[:, u, :], src["gd"][ds(n, P), :]).then_inc(m_in[u], 16)
                    for g in range(3):
                        sp.dma_start(grp[:, u, g, :], src["grp"][ds(n + g * T, P), :]).then_inc(m_in[u], 16)
                sp.dma_start(g_b[:, u, :], src["mg"][ds(n, P), :]).then_inc(g_in[u], 16)
                if not (first and u == 0):
                    sp.dma_start(x_b[:, 1 - u, :], x[ds(q * (2 * P) + (u - 1) * P, P), :]).then_inc(x_in[1 - u], 16)
            for u in range(2):
                load(0, u, True)
            for u in range(2):
                load(1, u, False, second=True)
            with sp.Fori(2, NT // 2) as q:
                for u in range(2):
                    load(q, u, False)
            sp.wait_ge(right_added, NT - 2)
            sp.dma_start(x_b[:, 1, :], x[T - P:T, :]).then_inc(x_in[1], 16)

        @block.gpsimd
        def _(pool):
            def store(q, u, first):
                pool.wait_ge(left_added, count(q, u))
                pool.wait_ge(right_added, count(q, u))
                pool.dma_start(y[ds(q * (2 * P) + u * P, P), :], y_b[:, u, :]).then_inc(y_out[u], 16)
            pairs(pool, NT, store)
            for u in range(2):
                pool.wait_ge(y_out[u], 16 * (NT // 2))

        @block.scalar
        def _(act):
            def high_o(q, u):
                act.wait_ge(oturned, count(q, u))
                act.activation(cat_hi[:, u, MIX:KO, :].rearrange("p a b -> p (a b)"), ps[:, 5, :], ACT.Copy
                               ).then_inc(ohi_done, 1)

            def step(q, u, first):
                if not conv:
                    act.wait_ge(ops, q * (2 * COPS) + (u * COPS + 2))
                    act.activation(cstat[:, 2, :], cstat[:, 1, :], ACT.Exp, scale=SCALE).then_inc(cexp, 1)
                act.wait_ge(qturned, count(q, u))
                act.activation(qt_hi[:, :], ps[:, 0, :], ACT.Copy).then_inc(qhi_done, 1)
                if not (first and u == 0):
                    high_o(*before(q, u))
                if conv:
                    act.wait_ge(m_in[u], q * 16 + 16)
                    act.activation(cat_hi[:, u, 0:KD, :], c_b[:, u, :, :], ACT.Copy).then_inc(mhi_done, 1)
                act.wait_ge(biased, count(q, u))
                for h in range(H):
                    e = act.activation(prob[:, h, :], ps[:, 1 + h // 2, (h % 2) * MEM:(h % 2 + 1) * MEM], ACT.Exp,
                                       scale=SCALE, bias=stat[:, 1, h:h + 1], accum_out=stat[:, 2, h:h + 1])
                e.then_inc(exped, 1)
                act.wait_ge(pturned, count(q, u))
                act.activation(pt_hi[:, :, :].rearrange("p a b -> p (a b)"),
                               ps[:, 3:5, :].rearrange("p a b -> p (a b)"), ACT.Copy).then_inc(phi_done, 1)
                if not conv:
                    act.wait_ge(mturned, count(q, u))
                    act.activation(cat_hi[:, u, 0:H, :].rearrange("p a b -> p (a b)"), ps[:, 0, :], ACT.Copy
                                   ).then_inc(mhi_done, 1)
            pairs(act, NT, step)
            high_o(*LAST)

        @block.vector
        def _(dve):
            def joint_max(q, u):
                dve.wait_ge(m_in[u], q * (16 * MLOADS) + 16 * MLOADS)
                mx = grp[:, u, :, C:C + H]
                dve.tensor_reduce(cstat[:, 0, 0:H], mx.rearrange("p g h -> p h g"), AX.X, ALU.max).then_inc(ops, 1)
                dve.wait_ge(ops, q * (2 * COPS) + (u * COPS + 1))
                dve.tensor_tensor(cstat[:, 1, :].rearrange("p (g h) -> p g h", h=H), mx,
                                  cstat[:, 0:1, 0:H].to_broadcast([P, 3, H]), ALU.subtract).then_inc(ops, 1)

            def combine(q, u):
                def sync_to(k):
                    dve.wait_ge(ops, q * (2 * COPS) + (u * COPS + k))
                sums = grp[:, u, :, C + H:C + 2 * H]
                dve.wait_ge(cexp, count(q, u))
                dve.tensor_tensor(cstat[:, 3, :].rearrange("p (g h) -> p g h", h=H), sums,
                                  cstat[:, 2, :].rearrange("p (g h) -> p g h", h=H), ALU.mult).then_inc(ops, 1)
                sync_to(3)
                dve.tensor_reduce(cstat[:, 0, H:2 * H], cstat[:, 3, :].rearrange("p (g h) -> p h g", h=H), AX.X,
                                  ALU.add).then_inc(ops, 1)
                sync_to(4)
                dve.reciprocal(cstat[:, 4, 0:H], cstat[:, 0, H:2 * H]).then_inc(ops, 1)
                sync_to(5)
                dve.tensor_tensor(cstat[:, 5, :].rearrange("p (g h) -> p g h", h=H),
                                  cstat[:, 2, :].rearrange("p (g h) -> p g h", h=H),
                                  cstat[:, 4:5, 0:H].to_broadcast([P, 3, H]), ALU.mult).then_inc(ops, 1)
                sync_to(6)
                for g in range(3):
                    for h in range(H):
                        cols = slice(h * HD, (h + 1) * HD)
                        w = cstat[:, 5, g * H + h:g * H + h + 1]
                        if g == 0:
                            m = dve.tensor_scalar(od[:, cols], grp[:, u, g, cols], w, None, ALU.mult)
                        else:
                            m = dve.scalar_tensor_tensor(out=od[:, cols], in0=grp[:, u, g, cols], scalar=w,
                                                         in1=od[:, cols], op0=ALU.mult, op1=ALU.add)
                    m.then_inc(ops, 1)
                    sync_to(7 + g)
                dve.tensor_tensor(od[:, :], od[:, :], gd_b[:, u, :], ALU.mult).then_inc(ops, 1)

            def gate(q, u):
                dve.wait_ge(inverted, count(q, u))
                dve.wait_ge(g_in[u], q * 16 + 16)
                dve.wait_ge(summed, count(q, u))
                for h in range(H):
                    cols = slice(h * HD, (h + 1) * HD)
                    m = dve.scalar_tensor_tensor(out=og[:, cols], in0=ps[:, 5, cols], scalar=stat[:, 3, h:h + 1],
                                                 in1=g_b[:, u, cols], op0=ALU.mult, op1=ALU.mult)
                m.then_inc(og_done, 1)

            def low_o(q, u):
                dve.wait_ge(ohi_done, count(q, u))
                dve.tensor_tensor(cat_lo[:, u, MIX:KO, :].rearrange("p a b -> p (a b)"), ps[:, 5, :],
                                  cat_hi[:, u, MIX:KO, :].rearrange("p a b -> p (a b)"), ALU.subtract
                                  ).then_inc(olo_done, 1)

            def add_left(q, u, first):
                dve.wait_ge(left_done, count(q, u))
                dve.wait_ge(x_in[u], q * 16 + 16)
                if not first:
                    dve.wait_ge(y_out[u], q * 16)
                dve.tensor_tensor(y_b[:, u, 0:C], ps[:, 6, :], x_b[:, u, 0:C], ALU.add).then_inc(left_added, 1)

            def add_right(q, u):
                dve.wait_ge(right_done, count(q, u))
                dve.tensor_tensor(y_b[:, u, C:D], ps[:, 7, :], x_b[:, u, C:D], ALU.add).then_inc(right_added, 1)

            def step(q, u, first, second=False):
                if not conv:
                    joint_max(q, u)
                if not (first and u == 0):
                    gate(*before(q, u))
                dve.wait_ge(qhi_done, count(q, u))
                dve.tensor_tensor(qt_lo[:, :], ps[:, 0, :], qt_hi[:, :], ALU.subtract).then_inc(qlo_done, 1)
                if not (first and u == 0):
                    low_o(*before(q, u))
                if not first:
                    add_right(q - 1, u)
                dve.wait_ge(scored, count(q, u))
                dve.tensor_reduce(stat[:, 0, :], ps[:, 1:3, :].rearrange("p a (b m) -> p (a b) m", m=MEM), AX.X,
                                  ALU.max).then_inc(maxed, 1)
                dve.wait_ge(maxed, count(q, u))
                dve.tensor_scalar(stat[:, 1, :], stat[:, 0, :], -SCALE, None, ALU.mult).then_inc(biased, 1)
                if conv:
                    dve.wait_ge(mhi_done, count(q, u))
                    dve.tensor_tensor(cat_lo[:, u, 0:KD, :], c_b[:, u, :, :], cat_hi[:, u, 0:KD, :], ALU.subtract
                                      ).then_inc(mlo_done, 1)
                else:
                    combine(q, u)
                dve.wait_ge(exped, count(q, u))
                dve.reciprocal(stat[:, 3, :], stat[:, 2, :]).then_inc(inverted, 1)
                if not (first and u == 0):
                    add_left(*before(q, u), first or (second and u == 0))
                dve.wait_ge(phi_done, count(q, u))
                dve.tensor_tensor(pt_lo[:, :, :].rearrange("p a b -> p (a b)"),
                                  ps[:, 3:5, :].rearrange("p a b -> p (a b)"),
                                  pt_hi[:, :, :].rearrange("p a b -> p (a b)"), ALU.subtract).then_inc(plo_done, 1)
                if not conv:
                    dve.wait_ge(mhi_done, count(q, u))
                    dve.tensor_tensor(cat_lo[:, u, 0:H, :].rearrange("p a b -> p (a b)"), ps[:, 0, :],
                                      cat_hi[:, u, 0:H, :].rearrange("p a b -> p (a b)"), ALU.subtract
                                      ).then_inc(mlo_done, 1)
            for u in range(2):
                step(0, u, True)
            for u in range(2):
                step(1, u, False, second=True)
            with dve.Fori(2, NT // 2) as q:
                for u in range(2):
                    step(q, u, False)
            gate(*LAST)
            low_o(*LAST)
            add_right(NT // 2 - 1, 0)
            add_left(*LAST, False)
            add_right(*LAST)

        @block.tensor
        def _(pe):
            def turn(bank, rows):
                for h in range(H):
                    t = pe.transpose(ps[:, bank, h * HD:(h + 1) * HD], rows[:, h * HD:(h + 1) * HD], ident[:, :])
                return t

            def project(u, half, chunks):
                cols = slice(half * C, (half + 1) * C)
                for k in chunks:
                    m = split3(pe, ps[:, 6 + half, :], cat_hi[:, u, k, :], cat_lo[:, u, k, :],
                               wo_hi[:, k, cols], wo_lo[:, k, cols], k == 0, k == KO - 1)
                return m

            def values(q, u, first):
                pe.wait_ge(plo_done, count(q, u))
                if not first:
                    pe.wait_ge(olo_done, count(q, u, 0))
                for h in range(H):
                    cols = slice(h * HD, (h + 1) * HD)
                    for mt in range(MT):
                        m = split3(pe, ps[:, 5, cols], pt_hi[:, h * MT + mt, :], pt_lo[:, h * MT + mt, :],
                                   v_hi[:, mt, cols], v_lo[:, mt, cols], mt == 0, mt == MT - 1)
                m.then_inc(summed, 1)

            def right_end(q, u):
                project(u, 1, range(MIX, KO)).then_inc(right_done, 1)

            def turn_o(q, u):
                pe.wait_ge(og_done, count(q, u))
                turn(5, og).then_inc(oturned, 1)

            def left(q, u, first):
                pe.wait_ge(mlo_done, count(q, u))
                if not first:
                    pe.wait_ge(left_added, count(q, u, 0))
                project(u, 0, range(MIX))
                pe.wait_ge(olo_done, count(q, u))
                project(u, 0, range(MIX, KO)).then_inc(left_done, 1)

            def right_begin(q, u, first):
                if not first:
                    pe.wait_ge(right_added, count(q, u, 0))
                project(u, 1, range(MIX))

            def step(q, u, first):
                started = not (first and u == 0)
                third = first and u == 1
                if started:
                    values(*before(q, u), third)
                pe.wait_ge(q_in[u], q * 16 + 16)
                if started:
                    pe.wait_ge(qlo_done if conv else mlo_done, count(q, u, 0))
                turn(0, q_b[:, u, :]).then_inc(qturned, 1)
                if not first:
                    right_end(q - 1, u)
                if started:
                    turn_o(*before(q, u))
                pe.wait_ge(qlo_done, count(q, u))
                for h in range(H):
                    at = (h % 2) * MEM
                    cols = slice(h * HD, (h + 1) * HD)
                    m = split3(pe, ps[:, 1 + h // 2, at:at + MEM], qt_hi[:, cols], qt_lo[:, cols],
                               kt_hi[:, h, :], kt_lo[:, h, :], True, True)
                m.then_inc(scored, 1)
                if started:
                    left(*before(q, u), third)
                pe.wait_ge(exped, count(q, u))
                for h in range(H):
                    for mt in range(MT):
                        at = ((h * MT + mt) % 4) * P
                        t = pe.transpose(ps[:, 3 + h // 2, at:at + P], prob[:, h, mt * P:(mt + 1) * P], ident[:, :])
                t.then_inc(pturned, 1)
                if not conv:
                    pe.wait_ge(ops, q * (2 * COPS) + (u + 1) * COPS)
                    turn(0, od).then_inc(mturned, 1)
                if started:
                    right_begin(*before(q, u), third)
            pairs(pe, NT, step)
            values(*LAST, False)
            right_end(NT // 2 - 1, 0)
            turn_o(*LAST)
            left(*LAST, False)
            right_begin(*LAST, False)
            right_end(*LAST)


def dil_stage(core, g, q_src, kv_src, dst, masks_r, ident_r, zeros):
    nc, ps, ident = core.nc, core.ps, core.ident
    d = DIL[g][1]
    per_stream = NT // d
    U = 4
    TURNS = NT // U
    tag = f"dil{g}"

    def has_prev(q, u):
        if per_stream == 1:
            return False
        if d > 1:
            return u > 0
        return not (isinstance(q, int) and q == 0 and u == 0)

    def rows(ap, q, u):
        view = ap.rearrange("(m d) c -> d m c", d=d)
        if per_stream == 1:
            return view[ds(q * U + u, 1), :, :].rearrange("o m c -> (o m) c")
        if d > 1:
            return view[ds(q, 1), u * P:(u + 1) * P, :].rearrange("o m c -> (o m) c")
        return view[:, ds(q * (U * P) + u * P, P), :].rearrange("o m c -> (o m) c")

    def turns(eng, body, tail=()):
        for u in range(U):
            body(0, u)
        with eng.Fori(1, TURNS) as q:
            for u in range(U):
                body(q, u)

    def back(q, u, k):
        if u >= k:
            return q, u - k
        if isinstance(q, int) and q == 0:
            return None
        return q - 1, u - k + U

    def cnt(s, extra=1):
        return s[0] * U + (s[1] + extra)

    def use(s, per=16):
        return s[0] * (U // 2 * per) + (s[1] // 2 + 1) * per

    with ExitStack() as st:
        q_b = core.sb(st, f"{tag}_q", [P, 2, C])
        k_b = core.sb(st, f"{tag}_k", [P, 2, C])
        v_b = core.sb(st, f"{tag}_v", [P, 2, C])
        qt_hi = core.sb(st, f"{tag}_qthi", [P, C], F32R)
        qt_lo = core.sb(st, f"{tag}_qtlo", [P, C], F32R)
        kt_hi = core.sb(st, f"{tag}_kthi", [P, H, 2, P], F32R)
        kt_lo = core.sb(st, f"{tag}_ktlo", [P, H, 2, P], F32R)
        v_hi = core.sb(st, f"{tag}_vhi", [P, 2, C], F32R)
        v_lo = core.sb(st, f"{tag}_vlo", [P, 2, C], F32R)
        prob = core.sb(st, f"{tag}_prob", [P, H, 2, P])
        pt_hi = core.sb(st, f"{tag}_pthi", [P, H, 2, P], F32R)
        pt_lo = core.sb(st, f"{tag}_ptlo", [P, H, 2, P], F32R)
        o_b = core.sb(st, f"{tag}_o", [P, U, OW])
        bias = core.sb(st, f"{tag}_bias", [P, H])
        names = ("qk_in0 qk_in1 v_in0 v_in1 o_out0 o_out1 o_out2 o_out3 turned qhi_done khi_done qlo_done klo_done vhi_done "
                 "vlo_done scored maxed biased exped pturned phi_done plo_done summed o_done")
        (qk_in0, qk_in1, v_in0, v_in1, o_out0, o_out1, o_out2, o_out3, turned, qhi_done, khi_done, qlo_done, klo_done, vhi_done,
         vlo_done, scored, maxed, biased, exped, pturned, phi_done, plo_done, summed, o_done) = core.sems(
            st, tag, names)
        qk_in, v_in, o_out = (qk_in0, qk_in1), (v_in0, v_in1), (o_out0, o_out1, o_out2, o_out3)
        block = st.enter_context(nc.Block())

        def keys(s):
            return (1 - s[1] % 2, s[1] % 2) if has_prev(*s) else (s[1] % 2,)

        def span(s):
            ks = sorted(keys(s))
            return ks[0], ks[-1] + 1

        scores = ps[:, 1:3, :].rearrange("p a (b s k) -> p (a b) s k", b=2, s=2)
        turned_p = ps[:, 3:5, :].rearrange("p a (b s k) -> p (a b) s k", b=2, s=2)

        @block.sync
        def _(sp):
            def store(s):
                sp.wait_ge(o_done, cnt(s))
                sp.dma_start(rows(dst, *s), o_b[:, s[1], :]).then_inc(o_out[s[1]], 16)

            def body(q, u):
                slot = u % 2
                if back(q, u, 2):
                    sp.wait_ge(turned, cnt(back(q, u, 2)))
                sp.dma_start(q_b[:, slot, :], rows(q_src, q, u)).then_inc(qk_in[slot], 16)
                sp.dma_start(k_b[:, slot, :], rows(kv_src[:, 0:C], q, u)).then_inc(qk_in[slot], 16)
                if back(q, u, 2):
                    sp.wait_ge(vlo_done, cnt(back(q, u, 2)))
                sp.dma_start(v_b[:, slot, :], rows(kv_src[:, C:2 * C], q, u)).then_inc(v_in[slot], 16)
                if back(q, u, 3):
                    store(back(q, u, 3))
            turns(sp, body)
            for u in (U - 3, U - 2, U - 1):
                store(back(TURNS, 0, U - u))
            for s in o_out:
                sp.wait_ge(s, 16 * TURNS)

        @block.gpsimd
        def _(pool):
            def body(q, u):
                slot = u % 2
                pool.wait_ge(v_in[slot], use((q, u)))
                if back(q, u, 1):
                    pool.wait_ge(summed, cnt(back(q, u, 1)))
                pool.tensor_tensor(v_hi[:, slot, :], v_b[:, slot, :], zeros[:, :], ALU.add).then_inc(vhi_done, 1)
                pool.wait_ge(vhi_done, cnt((q, u)))
                pool.tensor_tensor(v_lo[:, slot, :], v_b[:, slot, :], v_hi[:, slot, :], ALU.subtract
                                   ).then_inc(vlo_done, 1)
            turns(pool, body)

        @block.scalar
        def _(act):
            def exps(s):
                a, b = span(s)
                act.wait_ge(biased, cnt(s))
                for h in range(H):
                    e = act.activation(prob[:, h, a:b, :], scores[:, h, a:b, :], ACT.Exp, scale=SCALE,
                                       bias=bias[:, h:h + 1],
                                       accum_out=o_b[:, s[1], C + H + h:C + H + h + 1])
                e.then_inc(exped, 1)

            def copy_sums(s):
                act.wait_ge(summed, cnt(s))
                act.activation(o_b[:, s[1], 0:C], ps[:, 5, :], ACT.Copy).then_inc(o_done, 1)

            def probs_high(s):
                a, b = span(s)
                act.wait_ge(pturned, cnt(s))
                act.activation(pt_hi[:, :, a:b, :], turned_p[:, :, a:b, :], ACT.Copy).then_inc(phi_done, 1)

            def body(q, u):
                act.wait_ge(turned, cnt((q, u)))
                act.activation(qt_hi[:, :], ps[:, 0, :], ACT.Copy).then_inc(qhi_done, 1)
                act.activation(kt_hi[:, :, u % 2, :], ps[:, 6, :].rearrange("p (h k) -> p h k", h=H), ACT.Copy
                               ).then_inc(khi_done, 1)
                if back(q, u, 1):
                    exps(back(q, u, 1))
                if back(q, u, 2):
                    copy_sums(back(q, u, 2))
                if back(q, u, 1):
                    probs_high(back(q, u, 1))
            turns(act, body)
            last, before = back(TURNS, 0, 1), back(TURNS, 0, 2)
            exps(last)
            copy_sums(before)
            probs_high(last)
            copy_sums(last)

        @block.vector
        def _(dve):
            def maxima(s):
                a, b = span(s)
                slot = s[1]
                dve.wait_ge(scored, cnt(s))
                if back(*s, U):
                    dve.wait_ge(o_out[slot], s[0] * 16)
                dve.tensor_reduce(o_b[:, slot, C:C + H], scores[:, :, a:b, :].rearrange("p h s k -> p h (s k)"),
                                  AX.X, ALU.max).then_inc(maxed, 1)
                dve.wait_ge(maxed, cnt(s))
                dve.tensor_scalar(bias[:, :], o_b[:, slot, C:C + H], -SCALE, None, ALU.mult).then_inc(biased, 1)

            def probs_low(s):
                a, b = span(s)
                dve.wait_ge(phi_done, cnt(s))
                dve.tensor_tensor(pt_lo[:, :, a:b, :].rearrange("p h s k -> p h (s k)"),
                                  turned_p[:, :, a:b, :].rearrange("p h s k -> p h (s k)"),
                                  pt_hi[:, :, a:b, :].rearrange("p h s k -> p h (s k)"), ALU.subtract
                                  ).then_inc(plo_done, 1)

            def body(q, u):
                if back(q, u, 1):
                    maxima(back(q, u, 1))
                dve.wait_ge(qhi_done, cnt((q, u)))
                dve.tensor_tensor(qt_lo[:, :], ps[:, 0, :], qt_hi[:, :], ALU.subtract).then_inc(qlo_done, 1)
                dve.wait_ge(khi_done, cnt((q, u)))
                dve.tensor_tensor(kt_lo[:, :, u % 2, :], ps[:, 6, :].rearrange("p (h k) -> p h k", h=H),
                                  kt_hi[:, :, u % 2, :], ALU.subtract).then_inc(klo_done, 1)
                if back(q, u, 1):
                    probs_low(back(q, u, 1))
            turns(dve, body)
            last = back(TURNS, 0, 1)
            maxima(last)
            probs_low(last)

        @block.tensor
        def _(pe):
            def score(s):
                a, b = span(s)
                own = s[1] % 2
                if has_prev(*s):
                    mask = masks_r[:, 0:2 * P] if own else masks_r[:, P:3 * P]
                else:
                    mask = masks_r[:, P:2 * P]
                pe.wait_ge(qlo_done, cnt(s))
                pe.wait_ge(klo_done, cnt(s))
                for h in range(H):
                    cols = slice(h * HD, (h + 1) * HD)
                    acc = scores[:, h, a:b, :].rearrange("p s k -> p (s k)")
                    pe.matmul(acc, ident_r[:, :], mask, start=True, stop=False)
                    m = split3(pe, acc, qt_hi[:, cols], qt_lo[:, cols],
                               kt_hi[:, h, a:b, :].rearrange("p s k -> p (s k)"),
                               kt_lo[:, h, a:b, :].rearrange("p s k -> p (s k)"), False, True)
                m.then_inc(scored, 1)

            def turn(q, u):
                pe.wait_ge(qk_in[u % 2], use((q, u), 32))
                for h in range(H):
                    cols = slice(h * HD, (h + 1) * HD)
                    pe.transpose(ps[:, 0, cols], q_b[:, u % 2, cols], ident[:, :])
                for h in range(H):
                    cols = slice(h * HD, (h + 1) * HD)
                    t = pe.transpose(ps[:, 6, cols], k_b[:, u % 2, cols], ident[:, :])
                t.then_inc(turned, 1)

            def sums(s):
                pe.wait_ge(plo_done, cnt(s))
                pe.wait_ge(vlo_done, cnt(s))
                if back(*s, 1):
                    pe.wait_ge(o_done, cnt(back(*s, 1)))
                ks = keys(s)
                for h in range(H):
                    cols = slice(h * HD, (h + 1) * HD)
                    for j, key in enumerate(ks):
                        m = split3(pe, ps[:, 5, cols], pt_hi[:, h, key, :], pt_lo[:, h, key, :],
                                   v_hi[:, key, cols], v_lo[:, key, cols], j == 0, j == len(ks) - 1)
                m.then_inc(summed, 1)

            def turn_probs(s):
                pe.wait_ge(exped, cnt(s))
                for h in range(H):
                    for key in keys(s):
                        t = pe.transpose(turned_p[:, h, key, :], prob[:, h, key, :], ident[:, :])
                t.then_inc(pturned, 1)

            def body(q, u):
                if back(q, u, 1):
                    score(back(q, u, 1))
                turn(q, u)
                if back(q, u, 2):
                    sums(back(q, u, 2))
                if back(q, u, 1):
                    turn_probs(back(q, u, 1))
            turns(pe, body)
            last, before = back(TURNS, 0, 1), back(TURNS, 0, 2)
            score(last)
            sums(before)
            turn_probs(last)
            sums(last)


def masks_stage(core, masks, masks_r, ident_r, zeros):
    nc, ident = core.nc, core.ident
    with ExitStack() as st:
        zeroed, made, = core.sems(st, "masks", "zeroed made")
        block = st.enter_context(nc.Block())

        @block.gpsimd
        def _(pool):
            pool.memset(masks[:, :], 0.0).then_inc(zeroed, 1)
            pool.wait_ge(zeroed, 1)
            for at, sign in ((0, -1), (1, 1), (2, -1)):
                cols = masks[:, at * P:(at + 1) * P]
                pool.affine_select(out=cols, in_=cols, compare_op=ALU.is_ge, fill=NEG, base=0,
                                   pattern=[[-sign, P]], channel_multiplier=sign).then_inc(made, 1)

        @block.vector
        def _(dve):
            dve.wait_ge(made, 3)
            dve.tensor_copy(masks_r[:, :], masks[:, :])
            dve.tensor_copy(ident_r[:, :], ident[:, :])
            dve.memset(zeros[:, :], 0.0)


def dec_stage(core, layer, src, x_s, y_s, wo_hi, wo_lo):
    nc, ps, ident, io = core.nc, core.ps, core.ident, core.io
    tag = f"dec{layer}"
    conv = layer == 0
    MIX = KD if conv else H
    KO = MIX + H
    HS = H * S
    NG = len(DIL)
    GW = P + S
    R = 2 if conv else 3
    NP = 4
    SP = S // NP
    with ExitStack() as st:
        rows_in = core.sb(st, f"{tag}_rows", [S, R, C])
        mk = core.sb(st, f"{tag}_mk", [P, S, H, MEM])
        mv = core.sb(st, f"{tag}_mv", [P, S, MT, C]) if conv else None
        cols_t = core.sb(st, f"{tag}_cols", [P, R, HS])
        scr = core.sb(st, f"{tag}_scr", [P, MT, HS])
        pr = core.sb(st, f"{tag}_pr", [HS, MEM])
        pt = core.sb(st, f"{tag}_pt", [P, MT, HS])
        stat = core.sb(st, f"{tag}_stat", [HS, 8])
        cat = core.sb(st, f"{tag}_cat", [P, KO, S])
        cat_hi = core.sb(st, f"{tag}_cathi", [P, KO, S], F32R)
        cat_lo = core.sb(st, f"{tag}_catlo", [P, KO, S], F32R)
        xs = core.sb(st, f"{tag}_xs", [S, D])
        ys = core.sb(st, f"{tag}_ys", [S, D])
        if conv:
            conv_in = core.sb(st, f"{tag}_conv", [S, D])
        else:
            mv = mk.rearrange("p s h m -> p s (h m)").rearrange("p s (m c) -> p s m c", m=MT)
            qd = core.sb(st, f"{tag}_qd", [S, NG, C])
            kvn = core.sb(st, f"{tag}_kvn", [S, NG, 2, C])
            kd = core.sb(st, f"{tag}_kd", [P, NG, S, C])
            qkt = core.sb(st, f"{tag}_qkt", [P, 2, NG, HS])
            dscr = core.sb(st, f"{tag}_dscr", [P, NG, HS])
            nscr = core.sb(st, f"{tag}_nscr", [S, NG, HS])
            other = core.sb(st, f"{tag}_other", [S, NG * H, S])
            dpr = core.sb(st, f"{tag}_dpr", [HS, NG * GW])
            dpt = core.sb(st, f"{tag}_dpt", [P, NG, HS])
            npt = core.sb(st, f"{tag}_npt", [S, NG, HS])
            dsum = core.sb(st, f"{tag}_dsum", [P, HS])
        names = ("in_done mk_in0 mk_in1 mk_in2 mk_in3 mv_in0 mv_in1 mv_in2 mv_in3 kd_in0 kd_in1 kd_in2 vd_in0 "
                 "vd_in1 vd_in2 rows_turned rows_copied m_scored m_copied m_turned m_maxed m_biased m_exped "
                 "m_inverted m_divided m_pturned m_pcopied m_summed d_scored d_copied d_turned d_maxed "
                 "d_biased d_exped d_inverted d_divided d_pturned d_pcopied d_summed d_reduced mk_used kd_used "
                 "gated hi_done lo_done projected y_done y_out other_made")
        sems = dict(zip(names.split(), core.sems(st, tag, names)))
        mk_in, mv_in = ([sems[f"{n}_in{i}"] for i in range(NP)] for n in ("mk", "mv"))
        kd_in, vd_in = ([sems[f"{n}_in{g}"] for g in range(NG)] for n in ("kd", "vd"))
        in_done, rows_turned, rows_copied = (sems[n] for n in ("in_done", "rows_turned", "rows_copied"))
        (m_scored, m_copied, m_turned, m_maxed, m_biased, m_exped, m_inverted, m_divided, m_pturned, m_pcopied,
         m_summed) = (sems[n] for n in names.split() if n.startswith("m_"))
        (d_scored, d_copied, d_turned, d_maxed, d_biased, d_exped, d_inverted, d_divided, d_pturned, d_pcopied,
         d_summed, d_reduced) = (sems[n] for n in names.split() if n.startswith("d_"))
        mk_used, kd_used, gated, hi_done, lo_done, projected, y_done, y_out, other_made = (
            sems[n] for n in names.split()[-9:])
        LOADS = 4 if conv else 6
        block = st.enter_context(nc.Block())

        def load_mk(eng, i):
            at = (layer * S + i * SP) * P
            eng.dma_start(mk[:, i * SP:(i + 1) * SP, :, :].rearrange("p s h m -> p s (h m)"),
                          io["cache_kt"][at:at + SP * P, :].rearrange("(s p) c -> p s c", p=P)).then_inc(mk_in[i], 16)

        def load_mv(eng, i):
            for m in range(MT):
                eng.dma_start(mv[:, i * SP:(i + 1) * SP, m, :],
                              io["cache_v"][layer, i * SP:(i + 1) * SP, m * P:(m + 1) * P, :].rearrange(
                                  "s p c -> p s c")).then_inc(mv_in[i], 16)

        def load_dil(eng, g, cache, sem):
            eng.dma_start(kd[:, g, :, :], cache[g * S * P:(g + 1) * S * P, :].rearrange("(s p) c -> p s c", p=P)
                          ).then_inc(sem[g], 16)

        @block.sync
        def _(sp):
            sp.dma_start(rows_in[:, 0, :], src["q"][T:TS, :]).then_inc(in_done, 16)
            sp.dma_start(rows_in[:, 1, :], src["mg"][T:TS, :]).then_inc(in_done, 16)
            sp.dma_start(xs[:, :], x_s).then_inc(in_done, 16)
            if conv:
                sp.dma_start(conv_in[:, :], src["conv_s"]).then_inc(in_done, 16)
                for i in range(NP):
                    load_mk(sp, i)
            else:
                sp.dma_start(rows_in[:, 2, :], src["gd"][T:TS, :]).then_inc(in_done, 16)
                sp.dma_start(qd[:, :, :], src["qd"].rearrange("g t c -> t g c")[T:TS, :, :]).then_inc(in_done, 16)
                sp.dma_start(kvn[:, :, :, :].rearrange("s g a c -> s g (a c)"),
                             src["kv"].rearrange("g t c -> t g c")[T:TS, :, :]).then_inc(in_done, 16)
                load_dil(sp, 0, io["dil_kt"], kd_in)
                load_dil(sp, 2, io["dil_kt"], kd_in)
                load_mk(sp, 1)
                load_mk(sp, 3)
                sp.wait_ge(kd_used, 1)
                load_dil(sp, 0, io["dil_v"], vd_in)
                sp.wait_ge(kd_used, 3)
                load_dil(sp, 2, io["dil_v"], vd_in)
                for i in (1, 3):
                    sp.wait_ge(mk_used, i + 1)
                    load_mv(sp, i)
            sp.wait_ge(y_done, 1)
            sp.dma_start(y_s, ys[:, :]).then_inc(y_out, 16)
            sp.wait_ge(y_out, 16)

        @block.gpsimd
        def _(pool):
            if not conv:
                pool.memset(other[:, :, :], NEG).then_inc(other_made, 1)
                pool.wait_ge(other_made, 1)
                pool.affine_select(out=other[:, :, :], in_=other[:, :, :], compare_op=ALU.not_equal, fill=0.0,
                                   base=0, pattern=[[0, NG * H], [-1, S]], channel_multiplier=1
                                   ).then_inc(other_made, 1)

        @block.scalar
        def _(act):
            if conv:
                for i in range(NP):
                    load_mv(act, i)
            else:
                load_dil(act, 1, io["dil_kt"], kd_in)
                load_mk(act, 0)
                load_mk(act, 2)
                act.wait_ge(kd_used, 2)
                load_dil(act, 1, io["dil_v"], vd_in)
                for i in (0, 2):
                    act.wait_ge(mk_used, i + 1)
                    load_mv(act, i)
                act.wait_ge(d_biased, 1)
                act.activation(dpr[:, :], ps[0:HS, 1, 0:NG * GW], ACT.Exp, scale=SCALE, bias=stat[:, 5:6],
                               accum_out=stat[:, 6:7]).then_inc(d_exped, 1)
            act.wait_ge(m_biased, 1)
            act.activation(pr[:, :], ps[0:HS, 2, 0:MEM], ACT.Exp, scale=SCALE, bias=stat[:, 1:2],
                           accum_out=stat[:, 2:3]).then_inc(m_exped, 1)

        @block.tensor
        def _(pe):
            id_s = ident[0:S, 0:S]
            pe.wait_ge(in_done, 16 * LOADS)
            for r in range(R):
                for h in range(H):
                    at = r * HS + h * S
                    t = pe.transpose(ps[:, 0, at:at + S], rows_in[:, r, h * HD:(h + 1) * HD], id_s)
            if conv:
                for k in range(KD):
                    at = R * HS + k * S
                    t = pe.transpose(ps[:, 0, at:at + S], conv_in[:, k * P:(k + 1) * P], id_s)
            else:
                for g in range(NG):
                    for h in range(H):
                        at = g * HS + h * S
                        pe.transpose(ps[:, 5, at:at + S], qd[:, g, h * HD:(h + 1) * HD], id_s)
                        at += NG * HS
                        t = pe.transpose(ps[:, 5, at:at + S], kvn[:, g, 0, h * HD:(h + 1) * HD], id_s)
            t.then_inc(rows_turned, 1)
            pe.wait_ge(rows_copied, 1)
            if not conv:
                for g in range(NG):
                    for h in range(H):
                        hs = slice(h * S, (h + 1) * S)
                        pe.matmul(ps[0:S, 6, g * HS + h * S:g * HS + (h + 1) * S], qkt[:, 1, g, hs],
                                  qkt[:, 0, g, hs], start=True, stop=True)
                for g in range(NG):
                    pe.wait_ge(kd_in[g], 16)
                    for b in range(S):
                        for h in range(H):
                            c = h * S + b
                            mm = pe.matmul(ps[:, 7, g * HS + c:g * HS + c + 1], kd[:, g, b, h * P:(h + 1) * P],
                                           qkt[:, 0, g, c:c + 1], start=True, stop=True)
                    mm.then_inc(kd_used, 1)
            for i in range(NP):
                pe.wait_ge(mk_in[i], 16)
                for b in range(i * SP, (i + 1) * SP):
                    for h in range(H):
                        for m in range(MT):
                            c = h * S + b
                            mm = pe.matmul(ps[:, 4, m * HS + c:m * HS + c + 1], mk[:, b, h, m * P:(m + 1) * P],
                                           cols_t[:, 0, c:c + 1], start=True, stop=True)
                mm.then_inc(mk_used, 1)
            if not conv:
                pe.wait_ge(d_copied, 1)
                for g in range(NG):
                    pe.transpose(ps[0:HS, 1, g * GW:g * GW + P], dscr[:, g, :], ident[:, :])
                    t = pe.transpose(ps[0:HS, 1, g * GW + P:(g + 1) * GW], nscr[:, g, :], id_s)
                t.then_inc(d_turned, 1)
            pe.wait_ge(m_copied, 1)
            for m in range(MT):
                t = pe.transpose(ps[0:HS, 2, m * P:(m + 1) * P], scr[:, m, :], ident[:, :])
            t.then_inc(m_turned, 1)
            if not conv:
                pe.wait_ge(d_divided, 1)
                for g in range(NG):
                    pe.transpose(ps[:, 7, g * HS:(g + 1) * HS], dpr[:, g * GW:g * GW + P], ident[0:HS, 0:HS])
                    t = pe.transpose(ps[0:S, 0, g * HS:(g + 1) * HS], dpr[:, g * GW + P:(g + 1) * GW],
                                     ident[0:HS, 0:HS])
                t.then_inc(d_pturned, 1)
            pe.wait_ge(m_divided, 1)
            for m in range(MT):
                t = pe.transpose(ps[:, 3, m * HS:(m + 1) * HS], pr[:, m * P:(m + 1) * P], ident[0:HS, 0:HS])
            t.then_inc(m_pturned, 1)
            if not conv:
                pe.wait_ge(d_pcopied, 1)
                for g in range(NG):
                    pe.wait_ge(vd_in[g], 16)
                    for b in range(S):
                        for h in range(H):
                            c = h * S + b
                            acc, cols = ps[:, 5, g * HS + c:g * HS + c + 1], slice(h * HD, (h + 1) * HD)
                            pe.matmul(acc, kd[:, g, b, cols], dpt[:, g, c:c + 1], start=True, stop=False)
                            mm = pe.matmul(acc, kvn[:, g, 1, cols], npt[:, g, c:c + 1], start=False, stop=True)
                mm.then_inc(d_summed, 1)
            pe.wait_ge(m_pcopied, 1)
            for i in range(NP):
                pe.wait_ge(mv_in[i], 16 * MT)
                for b in range(i * SP, (i + 1) * SP):
                    for h in range(H):
                        c = h * S + b
                        for m in range(MT):
                            mm = pe.matmul(ps[:, 4, c:c + 1], mv[:, b, m, h * HD:(h + 1) * HD], pt[:, m, c:c + 1],
                                           start=(m == 0), stop=(m == MT - 1))
            mm.then_inc(m_summed, 1)
            pe.wait_ge(lo_done, 1)
            for half in range(2):
                cols = slice(half * C, (half + 1) * C)
                for k in range(KO):
                    mm = split3(pe, ps[0:S, 6 + half, :], cat_hi[:, k, :], cat_lo[:, k, :], wo_hi[:, k, cols],
                                wo_lo[:, k, cols], k == 0, k == KO - 1)
            mm.then_inc(projected, 1)

        @block.vector
        def _(dve):
            dve.wait_ge(rows_turned, 1)
            if conv:
                dve.tensor_copy(cat[:, 0:KD, :].rearrange("p k s -> p (k s)"), ps[:, 0, R * HS:R * HS + KD * S])
            else:
                dve.tensor_copy(qkt[:, :, :, :].rearrange("p a g c -> p (a g c)"), ps[:, 5, 0:2 * NG * HS])
            dve.tensor_copy(cols_t[:, :, :].rearrange("p r c -> p (r c)"), ps[:, 0, 0:R * HS]
                            ).then_inc(rows_copied, 1)
            if not conv:
                dve.wait_ge(kd_used, NG)
                dve.wait_ge(other_made, 2)
                dve.tensor_tensor(nscr[:, :, :].rearrange("p g c -> p (g c)"), ps[0:S, 6, 0:NG * HS],
                                  other[:, :, :].rearrange("p a b -> p (a b)"), ALU.add)
                dve.tensor_copy(dscr[:, :, :].rearrange("p g c -> p (g c)"), ps[:, 7, 0:NG * HS]
                                ).then_inc(d_copied, 1)
            dve.wait_ge(mk_used, NP)
            dve.tensor_copy(scr[:, :, :].rearrange("p m c -> p (m c)"), ps[:, 4, 0:MT * HS]).then_inc(m_copied, 1)
            if not conv:
                dve.wait_ge(d_turned, 1)
                dve.tensor_reduce(stat[:, 4:5], ps[0:HS, 1, 0:NG * GW], AX.X, ALU.max).then_inc(d_maxed, 1)
                dve.wait_ge(d_maxed, 1)
                dve.tensor_scalar(stat[:, 5:6], stat[:, 4:5], -SCALE, None, ALU.mult).then_inc(d_biased, 1)
            dve.wait_ge(m_turned, 1)
            dve.tensor_reduce(stat[:, 0:1], ps[0:HS, 2, 0:MEM], AX.X, ALU.max).then_inc(m_maxed, 1)
            dve.wait_ge(m_maxed, 1)
            dve.tensor_scalar(stat[:, 1:2], stat[:, 0:1], -SCALE, None, ALU.mult).then_inc(m_biased, 1)
            if not conv:
                dve.wait_ge(d_exped, 1)
                dve.reciprocal(stat[:, 7:8], stat[:, 6:7]).then_inc(d_inverted, 1)
                dve.wait_ge(d_inverted, 1)
                dve.tensor_scalar(dpr[:, :], dpr[:, :], stat[:, 7:8], None, ALU.mult).then_inc(d_divided, 1)
            dve.wait_ge(m_exped, 1)
            dve.reciprocal(stat[:, 3:4], stat[:, 2:3]).then_inc(m_inverted, 1)
            dve.wait_ge(m_inverted, 1)
            dve.tensor_scalar(pr[:, :], pr[:, :], stat[:, 3:4], None, ALU.mult).then_inc(m_divided, 1)
            if not conv:
                dve.wait_ge(d_pturned, 1)
                dve.tensor_copy(npt[:, :, :].rearrange("p g c -> p (g c)"), ps[0:S, 0, 0:NG * HS])
                dve.tensor_copy(dpt[:, :, :].rearrange("p g c -> p (g c)"), ps[:, 7, 0:NG * HS]
                                ).then_inc(d_pcopied, 1)
            dve.wait_ge(m_pturned, 1)
            dve.tensor_copy(pt[:, :, :].rearrange("p m c -> p (m c)"), ps[:, 3, 0:MT * HS]).then_inc(m_pcopied, 1)
            if not conv:
                dve.wait_ge(d_summed, 1)
                dve.tensor_reduce(dsum[:, :], ps[:, 5, 0:NG * HS].rearrange("p (g c) -> p c g", c=HS), AX.X, ALU.add
                                  ).then_inc(d_reduced, 1)
                dve.wait_ge(d_reduced, 1)
                dve.tensor_tensor(cat[:, 0:H, :].rearrange("p h b -> p (h b)"), dsum[:, :], cols_t[:, 2, :],
                                  ALU.mult)
            dve.wait_ge(m_summed, 1)
            dve.tensor_tensor(cat[:, MIX:KO, :].rearrange("p h b -> p (h b)"), ps[:, 4, 0:HS], cols_t[:, 1, :],
                              ALU.mult).then_inc(gated, 1)
            dve.wait_ge(gated, 1)
            dve.tensor_copy(cat_hi[:, :, :], cat[:, :, :]).then_inc(hi_done, 1)
            dve.wait_ge(hi_done, 1)
            dve.tensor_tensor(cat_lo[:, :, :], cat[:, :, :], cat_hi[:, :, :], ALU.subtract).then_inc(lo_done, 1)
            dve.wait_ge(projected, 1)
            dve.tensor_tensor(ys[:, 0:C], ps[0:S, 6, :], xs[:, 0:C], ALU.add)
            dve.tensor_tensor(ys[:, C:D], ps[0:S, 7, :], xs[:, C:D], ALU.add).then_inc(y_done, 1)


def build(nc, io):
    with ExitStack() as ctx:
        core = Core(nc, ctx, io)
        gains = core.sb(ctx, "gains", [P, 5 * KD])
        norm_a, kv_norm, norm_b, mem_norm_0, mem_norm_1 = (gains[:, n * KD:(n + 1) * KD] for n in range(5))
        setup_stage(core, gains)

        def wide(stack, name):
            return [core.sb(stack, f"{name}_{n}", shape, F32R)
                    for n, shape in (("xthi", [P, KD, TS]), ("xtlo", [P, KD, TS]),
                                     ("wh0", [P, KD, C]), ("wl0", [P, KD, C]))]

        def output_side(layer, w_mem, w_out, chunks, mem_norm, src, x, x_s, y, y_s):
            with ExitStack() as st:
                wo_hi = core.sb(st, f"wohi{layer}", [P, chunks, D], F32R)
                wo_lo = core.sb(st, f"wolo{layer}", [P, chunks, D], F32R)
                with ExitStack() as kvs:
                    kt_hi, kt_lo = (core.sb(kvs, f"mk{n}{layer}", [P, H, MEM], F32R) for n in ("hi", "lo"))
                    v_hi, v_lo = (core.sb(kvs, f"mv{n}{layer}", [P, MT, C], F32R) for n in ("hi", "lo"))
                    memkv_stage(core, layer, w_mem, io["mem_kv"][layer * MEM:(layer + 1) * MEM, :], w_out, chunks,
                                wo_hi, wo_lo, kt_hi, kt_lo, v_hi, v_lo, mem_norm, 8 + layer)
                    out_stage(core, layer, src, x, y, wo_hi, wo_lo, kt_hi, kt_lo, v_hi, v_lo)
                dec_stage(core, layer, src, x_s, y_s, wo_hi, wo_lo)

        with ExitStack() as st:
            xt_hi, xt_lo, wh0, wl0 = wide(st, "a")
            prep_stage(core, "prepa", io["x_prompt"], io["x_sample"], xt_hi, xt_lo, io["w_a"], wh0, wl0, norm_a)
            wh, wl = (wh0, core.sb(st, "a_wh1", [P, KD, C], F32R)), (wl0, core.sb(st, "a_wl1", [P, KD, C], F32R))
            conv_stage(core, io["w_a"], xt_hi, xt_lo, wh, wl, norm_a)
            tokens_stage(core, "toka", io["w_a"][(NCONV + 1) * D:, :],
                         [("norm", io["tok_a"][0], norm_a, 6), ("silu", io["tok_a"][1], None, None)],
                         xt_hi, xt_lo, wh, wl)
        src = {"q": io["tok_a"][0], "mg": io["tok_a"][1], "conv_t": io["conv_t"], "conv_s": io["conv_s"]}
        output_side(0, io["w_mem"][0:D, :], io["w_out_a"], KD + H, mem_norm_0, src, io["x_prompt"],
                    io["x_sample"], io["x1"][0:T, :], io["x1"][T:TS, :])
        with ExitStack() as st:
            xt_hi, xt_lo, wh0, wl0 = wide(st, "b")
            prep_stage(core, "prepb", io["x1"][0:T, :], io["x1"][T:TS, :], xt_hi, xt_lo, io["w_b"], wh0, wl0,
                       kv_norm)
            wh, wl = (wh0, core.sb(st, "b_wh1", [P, KD, C], F32R)), (wl0, core.sb(st, "b_wl1", [P, KD, C], F32R))
            kv = lambda g, part: io["kv"][g][:, part * C:(part + 1) * C]
            blocks = []
            for g in range(len(DIL)):
                blocks.append(("norm", kv(g, 0), kv_norm, g))
                blocks.append(("copy", kv(g, 1), kv_norm if g < 2 else norm_b, None))
            for g in range(len(DIL)):
                blocks.append(("norm", io["tok_b"][g], norm_b, 3 + g))
            blocks.append(("norm", io["tok_b"][3], norm_b, 7))
            blocks.append(("silu", io["tok_b"][4], norm_b, None))
            blocks.append(("silu", io["tok_b"][5], None, None))
            tokens_stage(core, "tokb", io["w_b"][D:, :], blocks, xt_hi, xt_lo, wh, wl)
        with ExitStack() as st:
            masks = core.sb(st, "masks", [P, 3 * P])
            masks_r = core.sb(st, "masks_r", [P, 3 * P], F32R)
            ident_r = core.sb(st, "ident_r", [P, P], F32R)
            zeros = core.sb(st, "zeros", [P, C])
            masks_stage(core, masks, masks_r, ident_r, zeros)
            for g in range(len(DIL)):
                dil_stage(core, g, io["tok_b"][g][0:T, :], io["kv"][g][0:T, :], io["grp"][g * T:(g + 1) * T, :],
                          masks_r, ident_r, zeros)
        src = {"q": io["tok_b"][3], "mg": io["tok_b"][5], "gd": io["tok_b"][4], "grp": io["grp"],
               "qd": io["tok_b"][0:3], "kv": io["kv"]}
        output_side(1, io["w_mem"][D:2 * D, :], io["w_out_b"], 2 * H, mem_norm_1, src, io["x1"][0:T, :],
                    io["x1"][T:TS, :], io["y"][0:T, :], io["y"][T:TS, :])


def kernel(**inputs):
    import concourse.bacc as bacc
    from concourse.bass_utils import run_bass_kernel_spmd

    a = {k: np.asarray(v) for k, v in inputs.items()}
    layout = np.ascontiguousarray
    w_in_a, w_in_b = a["w_in_a"][0], a["w_in_b"][0]
    part = lambda w, n: w[:, n * D:(n + 1) * D].reshape(D, NCONV, P)
    conv_w = np.stack([part(w_in_a, n) for n in (1, 0, 3, 2)], axis=2)
    w_a = np.concatenate([conv_w.transpose(1, 0, 2, 3).reshape(NCONV * D, C),
                          w_in_a[:, 4 * D:].reshape(D, 2, C).transpose(1, 0, 2).reshape(2 * D, C)])
    b_cols = w_in_b.reshape(D, 6, C)[:, [0, 1, 2, 4, 3, 5], :]
    w_b = np.concatenate([a["w_kv"].reshape(D, 6, C).transpose(1, 0, 2).reshape(6 * D, C),
                          b_cols.transpose(1, 0, 2).reshape(6 * D, C)])
    columns = np.stack([a["norm_a"][0], a["kv_norm"], a["norm_b"][0], a["mem_norm"][0], a["mem_norm"][1]])
    rows = np.concatenate([a["k_norm_dil"], a["q_norm_b"][0], a["mem_q_norm"], a["mem_k_norm"]])
    caches = [a["cache_dil0_kv"], a["cache_dil1_kv"], a["cache_dil2_kv"]]
    dil = np.stack([c[:, ::d] for c, (_, d) in zip(caches, DIL)])
    mem = a["cache_mem_kv"]
    conv_rows = np.concatenate([np.broadcast_to(a["conv_w_a"], (S, 3, D)), a["state_conv"][0]], axis=1)
    arrays = {
        "x_prompt": a["x_prompt"][0],
        "x_sample": a["x_sample"][:, 0],
        "mem_prompt": a["mem_prompt"][0],
        "w_a": w_a,
        "w_b": w_b,
        "w_mem": a["w_mem_kv"].reshape(2 * D, 2 * C),
        "w_out_a": a["w_out_a"][0],
        "w_out_b": a["w_out_b"][0],
        "gain_cols": columns.reshape(5, KD, P).transpose(2, 0, 1).reshape(P, 5 * KD),
        "gain_rows": np.tile(rows, (1, H)),
        "conv_taps": a["conv_w_a"][0].T,
        "conv_rows": conv_rows.reshape(S, 5, NCONV, P).transpose(2, 0, 1, 3).reshape(NCONV * S, 5 * P),
        "cache_kt": mem[:, :, :, 0].transpose(0, 1, 4, 3, 2).reshape(2 * S * P, H * MEM),
        "cache_v": mem[:, :, :, 1].reshape(2, S, MEM, C),
        "dil_kt": dil[:, :, :, 0].transpose(0, 1, 4, 3, 2).reshape(3 * S * P, H * P),
        "dil_v": dil[:, :, :, 1].reshape(3 * S * P, C),
    }
    arrays = {k: layout(v) for k, v in arrays.items()}
    outs = {"y": (TS, D), "mem_kv": (2 * MEM, 2 * C), "tail": (D, 2), "tail_s": (S, 2 * D), "kv": (3, TS, 2 * C)}
    scratch = {"conv_t": (D, T), "conv_s": (S, D), "tok_a": (2, TS, C), "tok_b": (6, TS, C), "grp": (3 * T, OW), "x1": (TS, D)}
    nc = bacc.Bacc("TRN2", target_bir_lowering=False, num_devices=1)
    io = {}
    for name, v in arrays.items():
        io[name] = nc.dram_tensor(f"{name}_dram", v.shape, F32, kind="ExternalInput").ap()
    for name, shape in outs.items():
        io[name] = nc.dram_tensor(f"{name}_dram", shape, F32, kind="ExternalOutput").ap()
    for name, shape in scratch.items():
        io[name] = nc.dram_tensor(f"{name}_dram", shape, F32, kind="Internal").ap()
    build(nc, io)
    r = run_bass_kernel_spmd(nc, [{f"{k}_dram": v for k, v in arrays.items()}], core_ids=[0]).results[0]
    y, kv = r["y_dram"], r["kv_dram"].reshape(3, TS, 2, H, HD)
    heads = (2, H, HD)
    prompt = [kv[g, T - w:T][None] for g, (w, _) in enumerate(DIL)]
    sample = [kv[g, T:TS][:, None] for g in range(3)]
    return (
        y[0:T][None],
        y[T:TS][:, None],
        r["mem_kv_dram"].reshape(2, 1, MEM, *heads),
        layout(r["tail_dram"].T)[None, None],
        r["tail_s_dram"].reshape(1, S, 2, D),
        *(layout(p) for p in prompt),
        *(layout(s) for s in sample),
    )
```

```python
from contextlib import ExitStack

import concourse.bass as bass
import numpy as np
from concourse import mybir

F32 = mybir.dt.float32
F32R = mybir.dt.float32r
ACT = mybir.ActivationFunctionType
ALU = mybir.AluOpType
AX = mybir.AxisListType

P = 128
D = 1024
KD = D // P
T = 2048
NT = T // P
S = 8
TS = T + S
HD = 128
H = 4
C = H * HD
MEM = 256
MT = MEM // P
TB = 4
NW = TB * C // T * 512
EPS = 1e-6
NEG = -1e30
SCALE = HD ** -0.5
DIL = ((128, 1), (512, 4), (2048, 16))
OW = C + 2 * H
NCONV = KD


def ds(start, n):
    return bass.ds(start, n)


def pairs(eng, n, body):
    for u in range(2):
        body(0, u, True)
    if n > 2:
        with eng.Fori(1, n // 2) as q:
            for u in range(2):
                body(q, u, False)


class Core:

    def __init__(self, nc, ctx, io):
        self.nc, self.ctx, self.io = nc, ctx, io
        self.ps = ctx.enter_context(nc.psum_tensor("ps", [P, 8, 512], F32))
        self.ident = ctx.enter_context(nc.sbuf_tensor("ident", [P, P], F32))

    def sems(self, stack, tag, names):
        sems = [self.nc.alloc_semaphore(f"{tag}_{n}") for n in names.split()]
        stack.callback(self.nc.all_engine_barrier)
        stack.callback(self.nc.clear_and_free_semaphores, sems)
        return sems

    def sb(self, stack, name, shape, dt=F32):
        return stack.enter_context(self.nc.sbuf_tensor(name, shape, dt))


def setup_stage(core, gains):
    nc = core.nc
    with ExitStack() as st:
        zeroed, made, loaded = core.sems(st, "setup", "zeroed made loaded")
        block = st.enter_context(nc.Block())

        @block.gpsimd
        def _(pool):
            pool.memset(core.ident[:, :], 0.0).then_inc(zeroed, 1)
            pool.wait_ge(zeroed, 1)
            pool.affine_select(out=core.ident[:, :], in_=core.ident[:, :], compare_op=ALU.not_equal,
                               fill=1.0, base=0, pattern=[[-1, P]], channel_multiplier=1).then_inc(made, 1)
            pool.wait_ge(made, 1)

        @block.sync
        def _(sp):
            sp.dma_start(gains[:, :], core.io["gain_cols"]).then_inc(loaded, 16)
            sp.wait_ge(loaded, 16)


def split_weight_chunk_act(act, raw, w_hi, gain):
    return act.activation(w_hi, raw, ACT.Copy, scale=gain)


def split_weight_chunk_dve(dve, raw, w_hi, w_lo, gain):
    return dve.scalar_tensor_tensor(out=w_lo, in0=raw, scalar=gain, in1=w_hi,
                                    op0=ALU.mult, op1=ALU.subtract)


def split3(pe, acc, a_hi, a_lo, b_hi, b_lo, first, last):
    pe.matmul(acc, a_hi, b_hi, start=first, stop=False)
    pe.matmul(acc, a_hi, b_lo, start=False, stop=False)
    return pe.matmul(acc, a_lo, b_hi, start=False, stop=last)


class Prep:
    TILES = NT + 1
    RING = 4

    def __init__(self, core, tag, x, x_s, xt_hi, xt_lo, w_src, w_hi, w_lo, gain):
        self.core, self.tag, self.x, self.x_s, self.xt_hi, self.xt_lo = core, tag, x, x_s, xt_hi, xt_lo
        self.w_src, self.w_hi, self.w_lo, self.gain = w_src, w_hi, w_lo, gain

    def buffers(self, stack):
        core, tag = self.core, self.tag
        with ExitStack() as early:
            self.xb = core.sb(early, f"{tag}_x", [P, self.RING, D])
            self.xn = core.sb(early, f"{tag}_xn", [P, 2, D])
            self.raw = core.sb(early, f"{tag}_raw", [P, self.RING, C])
        return (core.sb(stack, f"{tag}_wh1", [P, KD, C], F32R), core.sb(stack, f"{tag}_wl1", [P, KD, C], F32R))

    def open(self, stack, bank):
        self.bank = bank
        self.stat = self.core.sb(stack, f"{self.tag}_stat", [P, 2, 4])
        sems = self.core.sems(stack, self.tag, "x_in0 x_in1 x_in2 x_in3 raw_in0 raw_in1 raw_in2 raw_in3 squared "
                                               "rooted inverted scaled turned hi_done lo_done w_hi_done w_lo_done")
        self.x_in, self.raw_in = sems[0:4], sems[4:8]
        (self.squared, self.rooted, self.inverted, self.scaled, self.turned, self.hi_done, self.lo_done,
         self.w_hi_done, self.w_lo_done) = sems[8:]

    def rows(self, t):
        return P if t < NT else S

    def transposed(self, t):
        b = self.bank(t)
        return self.core.ps[:, b:b + 2, :].rearrange("p a (b t) -> p (a b) t", t=P)[:, :, 0:self.rows(t)]

    def load_x(self, sp, t):
        n, slot = self.rows(t), t % self.RING
        if t >= self.RING:
            sp.wait_ge(self.scaled, t - self.RING + 1)
        sp.dma_start(self.xb[0:n, slot, :], self.x[t * P:t * P + n, :] if t < NT else self.x_s
                     ).then_inc(self.x_in[slot], 16)

    def load_w(self, sp, k):
        if k >= self.RING:
            sp.wait_ge(self.w_lo_done, k - self.RING + 1)
        sp.dma_start(self.raw[:, k % self.RING, :], self.w_src[k * P:(k + 1) * P, :]
                     ).then_inc(self.raw_in[k % self.RING], 16)

    def loads(self, sp):
        for n in range(self.RING):
            self.load_x(sp, n)
            self.load_w(sp, n)
        for k in range(self.RING, KD):
            self.load_w(sp, k)
        for t in range(self.RING, self.TILES):
            self.load_x(sp, t)

    def square(self, act, t):
        n, slot, u = self.rows(t), t % self.RING, t % 2
        act.wait_ge(self.x_in[slot], 16 * (t // self.RING + 1))
        if t >= 2:
            act.wait_ge(self.turned, t - 1)
        act.activation(self.xn[0:n, u, :], self.xb[0:n, slot, :], ACT.Square,
                       accum_out=self.stat[0:n, u, 0:1]).then_inc(self.squared, 1)
        act.wait_ge(self.squared, t + 1)
        act.activation(self.stat[0:n, u, 1:2], self.stat[0:n, u, 0:1], ACT.Sqrt, scale=1.0 / D,
                       bias=EPS).then_inc(self.rooted, 1)

    def scale(self, dve, t):
        n, u = self.rows(t), t % 2
        dve.wait_ge(self.rooted, t + 1)
        dve.reciprocal(self.stat[0:n, u, 2:3], self.stat[0:n, u, 1:2]).then_inc(self.inverted, 1)
        dve.wait_ge(self.inverted, t + 1)
        dve.tensor_scalar(self.xn[0:n, u, :], self.xb[0:n, t % self.RING, :], self.stat[0:n, u, 2:3], None,
                          ALU.mult).then_inc(self.scaled, 1)

    def turn(self, pe, t):
        n, u = self.rows(t), t % 2
        pe.wait_ge(self.scaled, t + 1)
        if t >= 2:
            pe.wait_ge(self.lo_done, t - 1)
        for k in range(KD):
            at = (k % 4) * P
            m = pe.transpose(self.core.ps[:, self.bank(t) + k // 4, at:at + n], self.xn[0:n, u, k * P:(k + 1) * P],
                             self.core.ident[0:n, 0:n])
        m.then_inc(self.turned, 1)

    def high(self, act, t):
        act.wait_ge(self.turned, t + 1)
        act.activation(self.xt_hi[:, :, t * P:t * P + self.rows(t)], self.transposed(t), ACT.Copy
                       ).then_inc(self.hi_done, 1)

    def low(self, dve, t):
        cols = slice(t * P, t * P + self.rows(t))
        dve.wait_ge(self.hi_done, t + 1)
        dve.tensor_tensor(self.xt_lo[:, :, cols], self.transposed(t), self.xt_hi[:, :, cols], ALU.subtract
                          ).then_inc(self.lo_done, 1)

    def split_high(self, act, k):
        act.wait_ge(self.raw_in[k % self.RING], 16 * (k // self.RING + 1))
        split_weight_chunk_act(act, self.raw[:, k % self.RING, :], self.w_hi[:, k, :], self.gain[:, k:k + 1]
                               ).then_inc(self.w_hi_done, 1)

    def split_low(self, dve, k):
        dve.wait_ge(self.w_hi_done, k + 1)
        split_weight_chunk_dve(dve, self.raw[:, k % self.RING, :], self.w_hi[:, k, :], self.w_lo[:, k, :],
                               self.gain[:, k:k + 1]).then_inc(self.w_lo_done, 1)

    def over(self, eng):
        eng.wait_ge(self.scaled, self.TILES)
        eng.wait_ge(self.turned, self.TILES)

    def begin_act(self, act, tiles):
        k = 0
        for t in range(tiles + 2):
            self.square(act, t)
            if t >= 1 and t - 1 < tiles:
                self.high(act, t - 1)
            for _ in range(2 if k < KD else 0):
                self.split_high(act, k)
                k += 1

    def begin_dve(self, dve, tiles):
        k = 0
        for t in range(tiles + 2):
            self.scale(dve, t)
            if t >= 1 and t - 1 < tiles:
                self.low(dve, t - 1)
            for _ in range(2 if k < KD else 0):
                self.split_low(dve, k)
                k += 1

    def begin_pe(self, pe, tiles):
        for t in range(tiles):
            self.turn(pe, t)


def conv_stage(core, prep, w_all, xt_hi, xt_lo, wh, wl, gain):
    nc, ps, io = core.nc, core.ps, core.io
    tail_s = io["tail_s"].rearrange("s (a c) -> s a c", a=2)
    OPS = 7
    BOPS = TB * OPS + 9
    BMUL = TB * 4 + 1
    W0, W1, W2, S0, S1 = range(5)
    with ExitStack() as st:
        raw = core.sb(st, "conv_raw", [P, 2, C])
        u = core.sb(st, "conv_u", [P, 2, 2 + 512])
        t = core.sb(st, "conv_gate", [P, 512])
        o = core.sb(st, "conv_o", [P, 512])
        taps = core.sb(st, "conv_taps", [P, 2, 3])
        rows = core.sb(st, "conv_rows", [S, 5, P])
        u_s = u[0:S, 0, 2:2 + P]
        (raw_in0, raw_in1, taps_in0, taps_in1, rows_in, w_hi_done, w_lo_done, multiplied, c_copied, tapped,
         gated, ops, o_out, block_out) = core.sems(
            st, "conv", "raw_in0 raw_in1 taps_in0 taps_in1 rows_in w_hi_done w_lo_done multiplied c_copied "
                        "tapped gated ops o_out block_out")
        raw_in, taps_in = (raw_in0, raw_in1), (taps_in0, taps_in1)
        prep.open(st, lambda t: 4 * (max(t // 4, 1) % 2) + 2 * (t % 2))
        block = st.enter_context(nc.Block())
        BOUT = 4 * 16

        def ahead(b):
            return list(range(4 * b + 4, min(4 * b + 8, Prep.TILES)))

        def loop(eng, body):
            body(0, True)
            with eng.Fori(1, NCONV // 2) as q:
                body(q, False)

        @block.sync
        def _(sp):
            def body(q, first):
                for j in range(2):
                    if not first:
                        sp.wait_ge(ops, (q * 2 + (j - 1)) * BOPS)
                    sp.dma_start(taps[:, j, :], io["conv_taps"][ds((q * 2 + j) * P, P), :]).then_inc(taps_in[j], 16)
                    if first and j == 0:
                        prep.loads(sp)
                    for k in range(KD):
                        if not (first and j == 0 and k < 2):
                            sp.wait_ge(w_lo_done, q * (2 * KD) + (j * KD + k - 1))
                        sp.dma_start(raw[:, k % 2, :],
                                     w_all[ds((q * 2 + (j + 1)) * D + k * P, P), :]).then_inc(raw_in[k % 2], 16)
                        if k == 3:
                            if not (first and j == 0):
                                sp.wait_ge(block_out, (q * 2 + j) * BOUT)
                            sp.dma_start(rows[:, :, :].rearrange("s a c -> s (a c)"),
                                         io["conv_rows"][ds((q * 2 + j) * S, S), :]).then_inc(rows_in, 16)
            loop(sp, body)

        @block.gpsimd
        def _(pool):
            def body(q, first):
                for j in range(2):
                    blk = q * 2 + j
                    for b in range(TB):
                        pool.wait_ge(ops, blk * BOPS + (b + 1) * OPS)
                        pool.dma_start(io["conv_t"][ds(blk * P, P), b * 512:(b + 1) * 512], o[:, :]
                                       ).then_inc(o_out, 16)
                    pool.dma_start(io["tail"][ds(blk * P, P), :], u[:, 1, 512:514]).then_inc(block_out, 16)
                    pool.wait_ge(ops, (blk + 1) * BOPS)
                    pool.dma_start(io["conv_s"][:, ds(blk * P, P)], rows[:, W0, :]).then_inc(block_out, 16)
                    pool.dma_start(tail_s[:, 0, ds(blk * P, P)], rows[:, S1, :]).then_inc(block_out, 16)
                    pool.dma_start(tail_s[:, 1, ds(blk * P, P)], u_s).then_inc(block_out, 16)
            loop(pool, body)
            pool.wait_ge(o_out, 16 * NCONV * TB)
            pool.wait_ge(block_out, BOUT * NCONV)

        @block.scalar
        def _(act):
            def split(q, j, k):
                act.wait_ge(raw_in[k % 2], q * (KD * 16) + (j * (KD // 2) + k // 2 + 1) * 16)
                split_weight_chunk_act(act, raw[:, k % 2, :], wh[1 - j][:, k, :], gain[:, k:k + 1]
                                       ).then_inc(w_hi_done, 1)

            def body(q, first):
                for j in range(2):
                    blk = q * 2 + j
                    begun = not (first and j == 0)
                    for b in range(TB):
                        slot = (j * (TB + 1) + b) % 2
                        step = blk * TB + b
                        tiles = [] if begun else ahead(b)
                        more = [] if begun or b + 1 == TB else ahead(b + 1)

                        def high(n):
                            if n < len(tiles):
                                prep.high(act, tiles[n])

                        def square(n, of):
                            if n < len(of):
                                prep.square(act, of[n])
                        u_new = u[:, b % 2, 2:514]
                        act.wait_ge(multiplied, blk * BMUL + b * 4 + 1)
                        if begun or b:
                            act.wait_ge(ops, blk * BOPS + b * OPS)
                        if b == 0 and begun:
                            act.wait_ge(block_out, blk * BOUT)
                        act.activation(u_new, ps[:, slot * 4, :], ACT.Copy).then_inc(c_copied, 1)
                        high(0)
                        square(2, tiles)
                        high(1)
                        square(3, tiles)
                        if not begun and b == TB - 1:
                            prep.over(act)
                            for k in range(KD // 2):
                                split(q, j, k)
                        act.wait_ge(ops, blk * BOPS + (b * OPS + 2))
                        if begun or b:
                            act.wait_ge(o_out, step * 16)
                        if b == 0:
                            act.wait_ge(taps_in[j], q * 16 + 16)
                        act.activation(o[:, :], u_new, ACT.Copy, scale=taps[:, j, 2:3]).then_inc(tapped, 1)
                        high(2)
                        square(0, more)
                        act.wait_ge(multiplied, blk * BMUL + b * 4 + 3)
                        act.activation(t[:, :], ps[:, slot * 4 + 2, :], ACT.Sigmoid).then_inc(gated, 1)
                        high(3)
                        square(1, more)
                        if begun:
                            split(q, j, 2 * b)
                            split(q, j, 2 * b + 1)
                        elif b == TB - 1:
                            for k in range(KD // 2, KD):
                                split(q, j, k)
                    slot = (j * (TB + 1) + TB) % 2
                    act.wait_ge(multiplied, (blk + 1) * BMUL)
                    act.wait_ge(ops, blk * BOPS + TB * OPS)
                    act.activation(u_s, ps[0:S, slot * 4, 0:P], ACT.Copy).then_inc(c_copied, 1)
                    act.activation(t[0:S, 0:P], ps[0:S, slot * 4, 2 * P:3 * P], ACT.Sigmoid).then_inc(gated, 1)
            prep.begin_act(act, 4)
            loop(act, body)

        @block.vector
        def _(dve):
            def split(q, j, k):
                dve.wait_ge(w_hi_done, q * (2 * KD) + (j * KD + k + 1))
                split_weight_chunk_dve(dve, raw[:, k % 2, :], wh[1 - j][:, k, :], wl[1 - j][:, k, :],
                                       gain[:, k:k + 1]).then_inc(w_lo_done, 1)

            def body(q, first):
                for j in range(2):
                    blk = q * 2 + j
                    begun = not (first and j == 0)
                    for b in range(TB):
                        slot = (j * (TB + 1) + b) % 2
                        at = blk * BOPS + b * OPS
                        tiles = [] if begun else ahead(b)
                        more = [] if begun or b + 1 == TB else ahead(b + 1)

                        def low(n):
                            if n < len(tiles):
                                prep.low(dve, tiles[n])

                        def scale(n, of):
                            if n < len(of):
                                prep.scale(dve, of[n])
                        low(0)
                        scale(2, tiles)
                        low(1)
                        scale(3, tiles)
                        if not begun and b == TB - 1:
                            for k in range(KD // 2):
                                split(q, j, k)
                        u_new, u_one, u_two = (u[:, b % 2, n:n + 512] for n in (2, 1, 0))
                        if b == 0:
                            dve.wait_ge(taps_in[j], q * 16 + 16)
                        if b == 0:
                            dve.memset(u[:, 0, 0:2], 0.0).then_inc(ops, 1)
                        else:
                            dve.tensor_copy(u[:, b % 2, 0:2], u[:, 1 - b % 2, 512:514]).then_inc(ops, 1)
                        dve.wait_ge(c_copied, blk * (TB + 1) + (b + 1))
                        dve.wait_ge(multiplied, blk * BMUL + b * 4 + 2)
                        dve.tensor_tensor(u_new, ps[:, slot * 4 + 1, :], u_new, ALU.mult).then_inc(ops, 1)
                        dve.wait_ge(tapped, blk * TB + (b + 1))
                        dve.wait_ge(ops, at + 2)
                        dve.scalar_tensor_tensor(out=o[:, :], in0=u_one, scalar=taps[:, j, 1:2], in1=o[:, :],
                                                 op0=ALU.mult, op1=ALU.add).then_inc(ops, 1)
                        dve.wait_ge(ops, at + 3)
                        dve.scalar_tensor_tensor(out=o[:, :], in0=u_two, scalar=taps[:, j, 0:1], in1=o[:, :],
                                                 op0=ALU.mult, op1=ALU.add).then_inc(ops, 1)
                        low(2)
                        scale(0, more)
                        dve.wait_ge(gated, blk * (TB + 1) + (b + 1))
                        dve.tensor_tensor(t[:, :], ps[:, slot * 4 + 2, :], t[:, :], ALU.mult).then_inc(ops, 1)
                        low(3)
                        scale(1, more)
                        dve.wait_ge(multiplied, blk * BMUL + b * 4 + 4)
                        dve.wait_ge(ops, at + 5)
                        dve.tensor_tensor(t[:, :], ps[:, slot * 4 + 3, :], t[:, :], ALU.mult).then_inc(ops, 1)
                        dve.wait_ge(ops, at + 6)
                        dve.tensor_tensor(o[:, :], o[:, :], t[:, :], ALU.mult).then_inc(ops, 1)
                        if begun:
                            split(q, j, 2 * b)
                            split(q, j, 2 * b + 1)
                        elif b == TB - 1:
                            for k in range(KD // 2, KD):
                                split(q, j, k)
                    slot = (j * (TB + 1) + TB) % 2
                    at = blk * BOPS + TB * OPS
                    row = lambda n: rows[:, n, :]
                    z = lambda n: ps[0:S, slot * 4, n * P:(n + 1) * P]
                    dve.wait_ge(rows_in, (blk + 1) * 16)
                    dve.tensor_tensor(row(W0), row(S0), row(W0), ALU.mult).then_inc(ops, 1)
                    dve.tensor_tensor(row(W1), row(S1), row(W1), ALU.mult).then_inc(ops, 1)
                    dve.wait_ge(c_copied, (blk + 1) * (TB + 1))
                    dve.wait_ge(gated, (blk + 1) * (TB + 1))
                    dve.wait_ge(ops, at + 2)
                    dve.tensor_tensor(row(W0), row(W0), row(W1), ALU.add).then_inc(ops, 1)
                    dve.tensor_tensor(u_s, z(1), u_s, ALU.mult).then_inc(ops, 1)
                    dve.wait_ge(ops, at + 4)
                    dve.tensor_tensor(row(W2), u_s, row(W2), ALU.mult).then_inc(ops, 1)
                    dve.tensor_tensor(t[0:S, 0:P], z(2), t[0:S, 0:P], ALU.mult).then_inc(ops, 1)
                    dve.wait_ge(ops, at + 6)
                    dve.tensor_tensor(row(W0), row(W0), row(W2), ALU.add).then_inc(ops, 1)
                    dve.tensor_tensor(t[0:S, 0:P], z(3), t[0:S, 0:P], ALU.mult).then_inc(ops, 1)
                    dve.wait_ge(ops, at + 8)
                    dve.tensor_tensor(row(W0), row(W0), t[0:S, 0:P], ALU.mult).then_inc(ops, 1)
            prep.begin_dve(dve, 4)
            loop(dve, body)
            dve.wait_ge(w_lo_done, NCONV * KD)

        @block.tensor
        def _(pe):
            def body(q, first):
                for j in range(2):
                    blk = q * 2 + j
                    begun = not (first and j == 0)
                    if begun:
                        pe.wait_ge(w_lo_done, blk * KD)
                    for b in range(TB):
                        slot = (j * (TB + 1) + b) % 2
                        if b >= 1 and (begun or b >= 2):
                            pe.wait_ge(ops, blk * BOPS + (b - 1) * OPS)
                        elif b == 0 and begun:
                            pe.wait_ge(ops, (blk - 1) * BOPS + TB * OPS)
                        tiles = [] if begun else ahead(b)
                        if not begun:
                            pe.wait_ge(prep.lo_done, 4 * b + 4)
                        for part in range(4):
                            for k in range(KD):
                                if not begun and b == 0 and part == 0:
                                    pe.wait_ge(prep.w_lo_done, k + 1)
                                cols, toks = slice(part * P, (part + 1) * P), slice(b * 512, (b + 1) * 512)
                                m = split3(pe, ps[:, slot * 4 + part, :], wh[j][:, k, cols], wl[j][:, k, cols],
                                           xt_hi[:, k, toks], xt_lo[:, k, toks], k == 0, k == KD - 1)
                            m.then_inc(multiplied, 1)
                            for n in ((0, 1), (2,), (3,), ())[part]:
                                if n < len(tiles):
                                    if n == 0 and b:
                                        pe.wait_ge(ops, b * OPS)
                                    prep.turn(pe, tiles[n])
                    if not begun:
                        pe.wait_ge(prep.lo_done, Prep.TILES)
                    slot = (j * (TB + 1) + TB) % 2
                    pe.wait_ge(ops, blk * BOPS + (TB - 1) * OPS)
                    for k in range(KD):
                        m = split3(pe, ps[0:S, slot * 4, :], xt_hi[:, k, T:TS], xt_lo[:, k, T:TS],
                                   wh[j][:, k, :], wl[j][:, k, :], k == 0, k == KD - 1)
                    m.then_inc(multiplied, 1)
            prep.begin_pe(pe, 4)
            loop(pe, body)


def tokens_stage(core, tag, w_all, blocks, xt_hi, xt_lo, wh, wl, prep=None):
    nc, ps, io = core.nc, core.ps, core.io
    N = NT + 1
    LOW = 32
    count = lambda b, kind: sum(blk[0] == kind for blk in blocks[:b])
    with ExitStack() as st:
        raw = core.sb(st, f"{tag}_raw", [P, 2, C])
        o = core.sb(st, f"{tag}_o", [P, 2, C])
        xs_hl = core.sb(st, f"{tag}_xshl", [P, KD, LOW + S], F32R)
        low_rows = core.sb(st, f"{tag}_lowrows", [S, C])
        grow = core.sb(st, f"{tag}_grow", [P, C])
        stat = core.sb(st, f"{tag}_stat", [P, 2, 3, H])
        (raw_in0, raw_in1, grow_in, w_hi_done, w_lo_done, multiplied, squared, acted, inverted, o_done,
         o_out0, o_out1, xs_made, low_copied, folded) = core.sems(
            st, tag, "raw_in0 raw_in1 grow_in w_hi_done w_lo_done multiplied squared acted inverted "
                     "o_done o_out0 o_out1 xs_made low_copied folded")
        raw_in, o_out = (raw_in0, raw_in1), (o_out0, o_out1)
        if prep:
            prep.open(st, lambda t: 4 + 2 * (t % 2))

        def chunks_at(b, i):
            if b or not prep:
                return [i // 2] if i % 2 else []
            return range(KD)[3 * (i - N + 3):3 * (i - N + 4)] if i >= N - 3 else []
        block = st.enter_context(nc.Block())
        rows = lambda i: P if i < NT else S

        @block.sync
        def _(sp):
            for b, (kind, dst, gain, g) in enumerate(blocks):
                if kind == "norm":
                    if b:
                        sp.wait_ge(o_done, b * N)
                    sp.dma_start(grow[:, :], io["gain_rows"][g:g + 1, :].to_broadcast([P, C])).then_inc(grow_in, 16)
                if prep and b == 0:
                    prep.loads(sp)
                if gain is not None:
                    for k in range(KD):
                        if b * KD + k >= 2:
                            sp.wait_ge(w_lo_done, b * KD + k - 1)
                        sp.dma_start(raw[:, k % 2, :], w_all[b * D + k * P:b * D + (k + 1) * P, :]
                                     ).then_inc(raw_in[k % 2], 16)

        @block.gpsimd
        def _(pool):
            for b, (kind, dst, gain, g) in enumerate(blocks):
                for i in range(N):
                    n, tile = rows(i), b * N + i
                    pool.wait_ge(o_done, tile + 1)
                    pool.dma_start(dst[i * P:i * P + n, :], o[0:n, tile % 2, :]).then_inc(o_out[tile % 2], 16)
            for slot in range(2):
                pool.wait_ge(o_out[slot], 16 * ((len(blocks) * N + 1 - slot) // 2))

        @block.scalar
        def _(act):
            if prep:
                prep.begin_act(act, 2)
            for b, (kind, dst, gain, g) in enumerate(blocks):
                for i in range(N):
                    if prep and b == 0:
                        if i + 2 < N:
                            prep.high(act, i + 2)
                        if i + 4 < N:
                            prep.square(act, i + 4)
                    n, tile = rows(i), b * N + i
                    slot = tile % 2
                    act.wait_ge(multiplied, tile + 1)
                    if i == NT:
                        act.activation(low_rows[:, :], ps[LOW:LOW + S, slot, :], ACT.Copy).then_inc(low_copied, 1)
                        act.wait_ge(folded, b + 1)
                    if kind != "copy" and tile >= 2:
                        act.wait_ge(o_out[slot], 16 * (tile // 2))
                    if kind == "norm":
                        for h in range(H):
                            cols = slice(h * HD, (h + 1) * HD)
                            sq = act.activation(o[0:n, slot, cols], ps[0:n, slot, cols], ACT.Square,
                                                accum_out=stat[0:n, slot, 0, h:h + 1])
                        sq.then_inc(squared, 1)
                        act.wait_ge(squared, count(b, "norm") * N + i + 1)
                        act.activation(stat[0:n, slot, 1, :], stat[0:n, slot, 0, :], ACT.Sqrt, scale=1.0 / HD,
                                       bias=EPS).then_inc(acted, 1)
                    if kind == "silu":
                        act.activation(o[0:n, slot, :], ps[0:n, slot, :], ACT.Sigmoid).then_inc(acted, 1)
                    for k in chunks_at(b, i) if gain is not None else ():
                        if prep and b == 0 and k == 0:
                            prep.over(act)
                        act.wait_ge(raw_in[k % 2], 16 * (b * KD // 2 + k // 2 + 1))
                        split_weight_chunk_act(act, raw[:, k % 2, :], wh[1 - b % 2][:, k, :],
                                               gain[:, k:k + 1]).then_inc(w_hi_done, 1)

        @block.vector
        def _(dve):
            if prep:
                prep.begin_dve(dve, 2)
            for b, (kind, dst, gain, g) in enumerate(blocks):
                if kind == "norm":
                    dve.wait_ge(grow_in, 16 * (count(b, "norm") + 1))
                for i in range(N):
                    n, tile = rows(i), b * N + i
                    slot = tile % 2
                    if prep and b == 0:
                        if i + 2 < N:
                            prep.low(dve, i + 2)
                        if i + 4 < N:
                            prep.scale(dve, i + 4)
                    if b == 0 and i == NT - 1:
                        if prep:
                            dve.wait_ge(prep.lo_done, Prep.TILES)
                        dve.tensor_copy(xs_hl[:, :, 0:S], xt_hi[:, :, T:TS])
                        dve.tensor_copy(xs_hl[:, :, S:LOW], xt_hi[:, :, 0:LOW - S])
                        dve.tensor_copy(xs_hl[:, :, LOW:LOW + S], xt_lo[:, :, T:TS]).then_inc(xs_made, 1)
                    if i == NT:
                        dve.wait_ge(low_copied, b + 1)
                        dve.tensor_tensor(ps[0:S, slot, :], ps[0:S, slot, :], low_rows[:, :], ALU.add
                                          ).then_inc(folded, 1)
                        dve.wait_ge(folded, b + 1)
                    if kind == "copy":
                        dve.wait_ge(multiplied, tile + 1)
                        if tile >= 2:
                            dve.wait_ge(o_out[slot], 16 * (tile // 2))
                        dve.tensor_copy(o[0:n, slot, :], ps[0:n, slot, :]).then_inc(o_done, 1)
                    else:
                        dve.wait_ge(acted, (b - count(b, "copy")) * N + i + 1)
                    if kind == "silu":
                        dve.tensor_tensor(o[0:n, slot, :], ps[0:n, slot, :], o[0:n, slot, :],
                                          ALU.mult).then_inc(o_done, 1)
                    if kind == "norm":
                        dve.reciprocal(stat[0:n, slot, 2, :], stat[0:n, slot, 1, :]).then_inc(inverted, 1)
                        dve.wait_ge(inverted, count(b, "norm") * N + i + 1)
                        for h in range(H):
                            cols = slice(h * HD, (h + 1) * HD)
                            m = dve.scalar_tensor_tensor(out=o[0:n, slot, cols], in0=ps[0:n, slot, cols],
                                                         scalar=stat[0:n, slot, 2, h:h + 1], in1=grow[0:n, cols],
                                                         op0=ALU.mult, op1=ALU.mult)
                        m.then_inc(o_done, 1)
                    for k in chunks_at(b, i) if gain is not None else ():
                        dve.wait_ge(w_hi_done, b * KD + k + 1)
                        split_weight_chunk_dve(dve, raw[:, k % 2, :], wh[1 - b % 2][:, k, :],
                                               wl[1 - b % 2][:, k, :], gain[:, k:k + 1]).then_inc(w_lo_done, 1)

        @block.tensor
        def _(pe):
            if prep:
                prep.begin_pe(pe, 2)
            for b in range(len(blocks)):
                if b:
                    pe.wait_ge(w_lo_done, b * KD)
                for i in range(N):
                    n, tile = rows(i), b * N + i
                    if tile >= 2:
                        pe.wait_ge(o_done, tile - 1)
                    acc = ps[0:n, tile % 2, :]
                    if prep and b == 0:
                        if i + 2 < N:
                            prep.turn(pe, i + 2)
                        pe.wait_ge(prep.lo_done, i + 1)
                    if i == NT:
                        pe.wait_ge(xs_made, 1)
                    for k in range(KD):
                        if i == NT:
                            acc = ps[0:LOW + S, tile % 2, :]
                            pe.matmul(acc, xs_hl[:, k, :], wh[b % 2][:, k, :], start=(k == 0), stop=False)
                            m = pe.matmul(acc, xs_hl[:, k, :], wl[b % 2][:, k, :], start=False, stop=(k == KD - 1))
                            continue
                        if prep and tile == 0:
                            pe.wait_ge(prep.w_lo_done, k + 1)
                        x_hi = xt_hi[:, k, i * P:i * P + n]
                        x_lo = xt_lo[:, k, i * P:i * P + n]
                        pe.matmul(acc, x_hi, wh[b % 2][:, k, :], start=(k == 0), stop=False)
                        pe.matmul(acc, x_hi, wl[b % 2][:, k, :], start=False, stop=False)
                        m = pe.matmul(acc, x_lo, wh[b % 2][:, k, :], start=False, stop=(k == KD - 1))
                    m.then_inc(multiplied, 1)


def memkv_stage(core, layer, w_mem, out_kv, wo_src, wo_chunks, wo_hi, wo_lo, kt_hi, kt_lo, v_hl,
                mem_gain, norm_row):
    nc, ps, io, ident = core.nc, core.ps, core.io, core.ident
    tag = f"memkv{layer}"
    NB = 2
    RING = 8
    SLOTS = 4
    with ExitStack() as st:
        mem = core.sb(st, f"{tag}_mem", [P, MT, D])
        mn = core.sb(st, f"{tag}_mn", [P, MT, D])
        mt_hi = core.sb(st, f"{tag}_mthi", [P, KD, MEM], F32R)
        mt_lo = core.sb(st, f"{tag}_mtlo", [P, KD, MEM], F32R)
        raw = core.sb(st, f"{tag}_raw", [P, RING, C])
        mw_hi = core.sb(st, f"{tag}_mwhi", [P, SLOTS, C], F32R)
        mw_lo = core.sb(st, f"{tag}_mwlo", [P, SLOTS, C], F32R)
        kv = core.sb(st, f"{tag}_kv", [P, NB, MT, C])
        grow = core.sb(st, f"{tag}_grow", [P, C])
        stat = core.sb(st, f"{tag}_stat", [P, MT, 3, H + 1])
        names = ("mem_in0 mem_in1 grow_in raw_in0 raw_in1 raw_in2 raw_in3 raw_in4 raw_in5 raw_in6 raw_in7 "
                 "squared rooted inverted scaled turned "
                 "hi_done lo_done w_hi_done w_lo_done multiplied ksquared krooted kinverted kv_done v_hi_done "
                 "kturned khi_done klo_done v_lo_done kv_out")
        sems = core.sems(st, tag, names)
        mem_in, grow_in, raw_in = sems[0:2], sems[2], sems[3:3 + RING]
        (squared, rooted, inverted, scaled, turned, hi_done, lo_done, w_hi_done, w_lo_done, multiplied, ksquared,
         krooted, kinverted, kv_done, v_hi_done, kturned, khi_done, klo_done, v_lo_done, kv_out) = sems[3 + RING:]
        block = st.enter_context(nc.Block())
        MEMC = KD * NB
        OUTC = 2 * wo_chunks
        order, w = [(True, c) for c in range(SLOTS)] + [(False, c) for c in range(RING)], RING
        for c in range(SLOTS, MEMC):
            order.append((True, c))
            if (c - SLOTS + 1) * (OUTC - RING) // (MEMC - SLOTS) > w - RING and w - RING < c - SLOTS + 1:
                order.append((False, w))
                w += 1
        order += [(False, c) for c in range(w, OUTC)]
        TOTAL = len(order)
        place = {chunk: n for n, chunk in enumerate(order)}
        LEFT = OUTC - w

        def chunk_source(n):
            mem_chunk, c = order[n]
            k, b = c // 2, c % 2
            return (w_mem if mem_chunk else wo_src)[k * P:(k + 1) * P, b * C:(b + 1) * C]

        def chunk_split(n):
            mem_chunk, c = order[n]
            if mem_chunk:
                return mw_hi[:, c % SLOTS, :], mw_lo[:, c % SLOTS, :]
            k, half = c // 2, c % 2
            cols = slice(half * C, (half + 1) * C)
            return wo_hi[:, k, cols], wo_lo[:, k, cols]

        def chunk_gain(n):
            mem_chunk, c = order[n]
            return mem_gain[:, c // NB:c // NB + 1] if mem_chunk else 1.0

        @block.sync
        def _(sp):
            for m in range(MT):
                sp.dma_start(mem[:, m, :], io["mem_prompt"][m * P:(m + 1) * P, :]).then_inc(mem_in[m], 16)
            sp.dma_start(grow[:, :], io["gain_rows"][norm_row:norm_row + 1, :].to_broadcast([P, C])
                         ).then_inc(grow_in, 16)
            for c in range(TOTAL):
                if c >= RING:
                    sp.wait_ge(w_lo_done, c - RING + 1)
                sp.dma_start(raw[:, c % RING, :], chunk_source(c)).then_inc(raw_in[c % RING], 16)

        @block.gpsimd
        def _(pool):
            for b in range(NB):
                for m in range(MT):
                    pool.wait_ge(kv_done, b * MT + m + 1)
                    pool.dma_start(out_kv[m * P:(m + 1) * P, b * C:(b + 1) * C], kv[:, b, m, :]
                                   ).then_inc(kv_out, 16)
            pool.wait_ge(kv_out, 16 * NB * MT)

        @block.scalar
        def _(act):
            for m in range(MT):
                act.wait_ge(mem_in[m], 16)
                act.activation(mn[:, m, :], mem[:, m, :], ACT.Square,
                               accum_out=stat[:, m, 0, H:H + 1]).then_inc(squared, 1)
            for m in range(MT):
                act.wait_ge(squared, m + 1)
                act.activation(stat[:, m, 1, H:H + 1], stat[:, m, 0, H:H + 1], ACT.Sqrt, scale=1.0 / D,
                               bias=EPS).then_inc(rooted, 1)
            def split(c):
                act.wait_ge(raw_in[c % RING], 16 * (c // RING + 1))
                mem_chunk, m = order[c]
                if mem_chunk and m >= SLOTS:
                    act.wait_ge(multiplied, m - SLOTS + 1)
                split_weight_chunk_act(act, raw[:, c % RING, :], chunk_split(c)[0], chunk_gain(c)).then_inc(w_hi_done, 1)
            for c in range(SLOTS):
                split(c)
            for m in range(MT):
                act.wait_ge(turned, m + 1)
                act.activation(mt_hi[:, :, m * P:(m + 1) * P],
                               ps[:, 2 * m:2 * m + 2, :].rearrange("p a (b t) -> p (a b) t", t=P),
                               ACT.Copy).then_inc(hi_done, 1)
            for c in range(SLOTS, TOTAL - LEFT):
                split(c)
            act.wait_ge(multiplied, MEMC)
            for m in range(MT):
                for h in range(H):
                    sq = act.activation(kv[:, 0, m, h * HD:(h + 1) * HD], ps[:, 4 + m, h * HD:(h + 1) * HD],
                                        ACT.Square, accum_out=stat[:, m, 0, h:h + 1])
                sq.then_inc(ksquared, 1)
            for m in range(MT):
                act.wait_ge(ksquared, m + 1)
                act.activation(stat[:, m, 1, 0:H], stat[:, m, 0, 0:H], ACT.Sqrt, scale=1.0 / HD,
                               bias=EPS).then_inc(krooted, 1)
            for m in range(MT):
                act.activation(v_hl[:, m, :, 0, :], ps[:, 6 + m, :].rearrange("p (h e) -> p h e", h=H), ACT.Copy
                               ).then_inc(v_hi_done, 1)
            act.wait_ge(kturned, 1)
            act.activation(kt_hi[:, :, :].rearrange("p h m -> p (h m)"),
                           ps[:, 0:2, :].rearrange("p a b -> p (a b)"), ACT.Copy).then_inc(khi_done, 1)
            for c in range(TOTAL - LEFT, TOTAL):
                split(c)

        @block.vector
        def _(dve):
            for m in range(MT):
                dve.wait_ge(rooted, m + 1)
                dve.reciprocal(stat[:, m, 2, H:H + 1], stat[:, m, 1, H:H + 1]).then_inc(inverted, 1)
                dve.wait_ge(inverted, m + 1)
                dve.tensor_scalar(mn[:, m, :], mem[:, m, :], stat[:, m, 2, H:H + 1], None, ALU.mult
                                  ).then_inc(scaled, 1)
            def split(c):
                dve.wait_ge(w_hi_done, c + 1)
                split_weight_chunk_dve(dve, raw[:, c % RING, :], *chunk_split(c), chunk_gain(c)).then_inc(w_lo_done, 1)
            for c in range(SLOTS):
                split(c)
            for m in range(MT):
                dve.wait_ge(hi_done, m + 1)
                dve.tensor_tensor(mt_lo[:, :, m * P:(m + 1) * P],
                                  ps[:, 2 * m:2 * m + 2, :].rearrange("p a (b t) -> p (a b) t", t=P),
                                  mt_hi[:, :, m * P:(m + 1) * P], ALU.subtract).then_inc(lo_done, 1)
            for c in range(SLOTS, TOTAL - LEFT):
                split(c)
            dve.wait_ge(grow_in, 16)
            for m in range(MT):
                dve.wait_ge(krooted, m + 1)
                dve.reciprocal(stat[:, m, 2, 0:H], stat[:, m, 1, 0:H]).then_inc(kinverted, 1)
                dve.wait_ge(kinverted, m + 1)
                for h in range(H):
                    cols = slice(h * HD, (h + 1) * HD)
                    k = dve.scalar_tensor_tensor(out=kv[:, 0, m, cols], in0=ps[:, 4 + m, cols],
                                                 scalar=stat[:, m, 2, h:h + 1], in1=grow[:, cols],
                                                 op0=ALU.mult, op1=ALU.mult)
                k.then_inc(kv_done, 1)
            for m in range(MT):
                dve.wait_ge(v_hi_done, m + 1)
                dve.tensor_copy(kv[:, 1, m, :], ps[:, 6 + m, :]).then_inc(kv_done, 1)
                dve.tensor_tensor(v_hl[:, m, :, 1, :], ps[:, 6 + m, :].rearrange("p (h e) -> p h e", h=H),
                                  v_hl[:, m, :, 0, :], ALU.subtract).then_inc(v_lo_done, 1)
            dve.wait_ge(khi_done, 1)
            dve.tensor_tensor(kt_lo[:, :, :].rearrange("p h m -> p (h m)"),
                              ps[:, 0:2, :].rearrange("p a b -> p (a b)"),
                              kt_hi[:, :, :].rearrange("p h m -> p (h m)"), ALU.subtract).then_inc(klo_done, 1)
            for c in range(TOTAL - LEFT, TOTAL):
                split(c)
            dve.wait_ge(w_lo_done, TOTAL)

        @block.tensor
        def _(pe):
            for m in range(MT):
                pe.wait_ge(scaled, m + 1)
                for k in range(KD):
                    at = (k % 4) * P
                    t = pe.transpose(ps[:, 2 * m + k // 4, at:at + P], mn[:, m, k * P:(k + 1) * P], ident[:, :])
                t.then_inc(turned, 1)
            pe.wait_ge(lo_done, MT)
            for c in range(MEMC):
                k, b = c // NB, c % NB
                pe.wait_ge(w_lo_done, place[True, c] + 1)
                for m in range(MT):
                    acc = ps[:, 4 + 2 * b + m, :]
                    x_hi, x_lo = mt_hi[:, k, m * P:(m + 1) * P], mt_lo[:, k, m * P:(m + 1) * P]
                    pe.matmul(acc, x_hi, mw_hi[:, c % SLOTS, :], start=(k == 0), stop=False)
                    pe.matmul(acc, x_hi, mw_lo[:, c % SLOTS, :], start=False, stop=False)
                    mm = pe.matmul(acc, x_lo, mw_hi[:, c % SLOTS, :], start=False, stop=(k == KD - 1))
                mm.then_inc(multiplied, 1)
            pe.wait_ge(kv_done, MT)
            for h in range(H):
                for m in range(MT):
                    at = (h % 2) * MEM + m * P
                    t = pe.transpose(ps[:, h // 2, at:at + P], kv[:, 0, m, h * HD:(h + 1) * HD], ident[:, :])
            t.then_inc(kturned, 1)


def out_stage(core, layer, src, x, y, wo_hi, wo_lo, kt_hi, kt_lo, v_hl):
    nc, ps, ident = core.nc, core.ps, core.ident
    tag = f"out{layer}"
    conv = layer == 0
    MIX = KD if conv else H
    KO = MIX + H
    with ExitStack() as st:
        q_b = core.sb(st, f"{tag}_q", [P, 2, C])
        g_b = core.sb(st, f"{tag}_g", [P, 2, C])
        x_b = core.sb(st, f"{tag}_x", [P, 2, D])
        qt_hi = core.sb(st, f"{tag}_qthi", [P, C], F32R)
        qt_lo = core.sb(st, f"{tag}_qtlo", [P, C], F32R)
        prob = core.sb(st, f"{tag}_prob", [P, H, MEM])
        pt_hi = core.sb(st, f"{tag}_pthi", [P, H * MT, P], F32R)
        pt_lo = core.sb(st, f"{tag}_ptlo", [P, H * MT, P], F32R)
        og = core.sb(st, f"{tag}_og", [P, C])
        cat_hi = core.sb(st, f"{tag}_cathi", [P, 2, KO, P], F32R)
        cat_lo = core.sb(st, f"{tag}_catlo", [P, 2, KO, P], F32R)
        y_b = core.sb(st, f"{tag}_y", [P, 2, D])
        stat = core.sb(st, f"{tag}_stat", [P, 4, H])
        if conv:
            c_b = core.sb(st, f"{tag}_c", [P, 2, KD, P])
        else:
            grp = core.sb(st, f"{tag}_grp", [P, 2, 3, OW])
            gd_b = core.sb(st, f"{tag}_gd", [P, 2, C])
            od = core.sb(st, f"{tag}_od", [P, C])
            cstat = core.sb(st, f"{tag}_cstat", [P, 6, 3 * H])
        names = ("q_in0 q_in1 g_in0 g_in1 x_in0 x_in1 m_in0 m_in1 y_out0 y_out1 qturned qhi_done qlo_done "
                 "scored maxed biased exped inverted pturned phi_done plo_done summed og_done oturned ohi_done "
                 "olo_done mhi_done mlo_done left_done right_done left_added right_added mturned ops cexp "
                 "o_begun o_added")
        (q_in0, q_in1, g_in0, g_in1, x_in0, x_in1, m_in0, m_in1, y_out0, y_out1, qturned, qhi_done, qlo_done,
         scored, maxed, biased, exped, inverted, pturned, phi_done, plo_done, summed, og_done, oturned, ohi_done,
         olo_done, mhi_done, mlo_done, left_done, right_done, left_added, right_added, mturned, ops, cexp,
         o_begun, o_added
         ) = core.sems(st, tag, names)
        q_in, g_in, x_in, m_in, y_out = (q_in0, q_in1), (g_in0, g_in1), (x_in0, x_in1), (m_in0, m_in1), (y_out0, y_out1)
        MLOADS = 1 if conv else 4
        COPS = 10
        block = st.enter_context(nc.Block())
        LAST = (NT // 2 - 1, 1)

        sums_hl = ps[:, 3:5, :].rearrange("p a (b x e) -> p (a b) x e", b=2, x=2)
        og_heads = og[:, :].rearrange("p (h e) -> p h e", h=H)

        def before(q, u):
            return (q, 0) if u else (q - 1, 1)

        def count(q, u, extra=1):
            return q * 2 + (u + extra)

        @block.sync
        def _(sp):
            def load(q, u, first, second=False):
                n = q * (2 * P) + u * P
                if second and u == 0:
                    sp.wait_ge(og_done, 1)
                elif not first:
                    sp.wait_ge(right_added, count(q, u, -2))
                sp.dma_start(q_b[:, u, :], src["q"][ds(n, P), :]).then_inc(q_in[u], 16)
                if conv:
                    sp.dma_start(c_b[:, u, :, :], src["conv_t"].rearrange("(k p) t -> p k t", p=P)[:, :, ds(n, P)]
                                 ).then_inc(m_in[u], 16)
                else:
                    sp.dma_start(gd_b[:, u, :], src["gd"][ds(n, P), :]).then_inc(m_in[u], 16)
                    for g in range(3):
                        sp.dma_start(grp[:, u, g, :], src["grp"][ds(n + g * T, P), :]).then_inc(m_in[u], 16)
                sp.dma_start(g_b[:, u, :], src["mg"][ds(n, P), :]).then_inc(g_in[u], 16)
                if not (first and u == 0):
                    sp.dma_start(x_b[:, 1 - u, :], x[ds(q * (2 * P) + (u - 1) * P, P), :]).then_inc(x_in[1 - u], 16)
            for u in range(2):
                load(0, u, True)
            for u in range(2):
                load(1, u, False, second=True)
            with sp.Fori(2, NT // 2) as q:
                for u in range(2):
                    load(q, u, False)
            sp.wait_ge(right_added, NT - 2)
            sp.dma_start(x_b[:, 1, :], x[T - P:T, :]).then_inc(x_in[1], 16)

        @block.gpsimd
        def _(pool):
            def store(q, u, first):
                pool.wait_ge(left_added, count(q, u))
                pool.wait_ge(right_added, count(q, u))
                pool.dma_start(y[ds(q * (2 * P) + u * P, P), :], y_b[:, u, :]).then_inc(y_out[u], 16)
            pairs(pool, NT, store)
            for u in range(2):
                pool.wait_ge(y_out[u], 16 * (NT // 2))

        @block.scalar
        def _(act):
            def copy_sums(q, u):
                act.wait_ge(summed, count(q, u))
                act.activation(og_heads, sums_hl[:, :, 0, :], ACT.Copy).then_inc(o_begun, 1)

            def high_o(q, u):
                act.wait_ge(oturned, count(q, u))
                act.activation(cat_hi[:, u, MIX:KO, :].rearrange("p a b -> p (a b)"), ps[:, 5, :], ACT.Copy
                               ).then_inc(ohi_done, 1)

            def step(q, u, first):
                if not conv:
                    act.wait_ge(ops, q * (2 * COPS) + (u * COPS + 2))
                    act.activation(cstat[:, 2, :], cstat[:, 1, :], ACT.Exp, scale=SCALE).then_inc(cexp, 1)
                if not (first and u == 0):
                    copy_sums(*before(q, u))
                act.wait_ge(qturned, count(q, u))
                act.activation(qt_hi[:, :], ps[:, 0, :], ACT.Copy).then_inc(qhi_done, 1)
                if not (first and u == 0):
                    high_o(*before(q, u))
                if conv:
                    act.wait_ge(m_in[u], q * 16 + 16)
                    act.activation(cat_hi[:, u, 0:KD, :], c_b[:, u, :, :], ACT.Copy).then_inc(mhi_done, 1)
                act.wait_ge(biased, count(q, u))
                for h in range(H):
                    e = act.activation(prob[:, h, :], ps[:, 1 + h // 2, (h % 2) * MEM:(h % 2 + 1) * MEM], ACT.Exp,
                                       scale=SCALE, bias=stat[:, 1, h:h + 1], accum_out=stat[:, 2, h:h + 1])
                e.then_inc(exped, 1)
                act.wait_ge(pturned, count(q, u))
                act.activation(pt_hi[:, :, :].rearrange("p a b -> p (a b)"),
                               ps[:, 3:5, :].rearrange("p a b -> p (a b)"), ACT.Copy).then_inc(phi_done, 1)
                if not conv:
                    act.wait_ge(mturned, count(q, u))
                    act.activation(cat_hi[:, u, 0:H, :].rearrange("p a b -> p (a b)"), ps[:, 0, :], ACT.Copy
                                   ).then_inc(mhi_done, 1)
            pairs(act, NT, step)
            copy_sums(*LAST)
            high_o(*LAST)

        @block.vector
        def _(dve):
            def joint_max(q, u):
                dve.wait_ge(m_in[u], q * (16 * MLOADS) + 16 * MLOADS)
                mx = grp[:, u, :, C:C + H]
                dve.tensor_reduce(cstat[:, 0, 0:H], mx.rearrange("p g h -> p h g"), AX.X, ALU.max).then_inc(ops, 1)
                dve.wait_ge(ops, q * (2 * COPS) + (u * COPS + 1))
                dve.tensor_tensor(cstat[:, 1, :].rearrange("p (g h) -> p g h", h=H), mx,
                                  cstat[:, 0:1, 0:H].to_broadcast([P, 3, H]), ALU.subtract).then_inc(ops, 1)

            def combine(q, u):
                def sync_to(k):
                    dve.wait_ge(ops, q * (2 * COPS) + (u * COPS + k))
                sums = grp[:, u, :, C + H:C + 2 * H]
                dve.wait_ge(cexp, count(q, u))
                dve.tensor_tensor(cstat[:, 3, :].rearrange("p (g h) -> p g h", h=H), sums,
                                  cstat[:, 2, :].rearrange("p (g h) -> p g h", h=H), ALU.mult).then_inc(ops, 1)
                sync_to(3)
                dve.tensor_reduce(cstat[:, 0, H:2 * H], cstat[:, 3, :].rearrange("p (g h) -> p h g", h=H), AX.X,
                                  ALU.add).then_inc(ops, 1)
                sync_to(4)
                dve.reciprocal(cstat[:, 4, 0:H], cstat[:, 0, H:2 * H]).then_inc(ops, 1)
                sync_to(5)
                dve.tensor_tensor(cstat[:, 5, :].rearrange("p (g h) -> p g h", h=H),
                                  cstat[:, 2, :].rearrange("p (g h) -> p g h", h=H),
                                  cstat[:, 4:5, 0:H].to_broadcast([P, 3, H]), ALU.mult).then_inc(ops, 1)
                sync_to(6)
                for g in range(3):
                    for h in range(H):
                        cols = slice(h * HD, (h + 1) * HD)
                        w = cstat[:, 5, g * H + h:g * H + h + 1]
                        if g == 0:
                            m = dve.tensor_scalar(od[:, cols], grp[:, u, g, cols], w, None, ALU.mult)
                        else:
                            m = dve.scalar_tensor_tensor(out=od[:, cols], in0=grp[:, u, g, cols], scalar=w,
                                                         in1=od[:, cols], op0=ALU.mult, op1=ALU.add)
                    m.then_inc(ops, 1)
                    sync_to(7 + g)
                dve.tensor_tensor(od[:, :], od[:, :], gd_b[:, u, :], ALU.mult).then_inc(ops, 1)

            def gate(q, u):
                dve.wait_ge(o_begun, count(q, u))
                dve.tensor_tensor(og_heads, sums_hl[:, :, 1, :], og_heads, ALU.add).then_inc(o_added, 1)
                dve.wait_ge(inverted, count(q, u))
                dve.wait_ge(g_in[u], q * 16 + 16)
                dve.wait_ge(o_added, count(q, u))
                for h in range(H):
                    cols = slice(h * HD, (h + 1) * HD)
                    m = dve.scalar_tensor_tensor(out=og[:, cols], in0=og[:, cols], scalar=stat[:, 3, h:h + 1],
                                                 in1=g_b[:, u, cols], op0=ALU.mult, op1=ALU.mult)
                m.then_inc(og_done, 1)

            def low_o(q, u):
                dve.wait_ge(ohi_done, count(q, u))
                dve.tensor_tensor(cat_lo[:, u, MIX:KO, :].rearrange("p a b -> p (a b)"), ps[:, 5, :],
                                  cat_hi[:, u, MIX:KO, :].rearrange("p a b -> p (a b)"), ALU.subtract
                                  ).then_inc(olo_done, 1)

            def add_left(q, u, first):
                dve.wait_ge(left_done, count(q, u))
                dve.wait_ge(x_in[u], q * 16 + 16)
                if not first:
                    dve.wait_ge(y_out[u], q * 16)
                dve.tensor_tensor(y_b[:, u, 0:C], ps[:, 6, :], x_b[:, u, 0:C], ALU.add).then_inc(left_added, 1)

            def add_right(q, u):
                dve.wait_ge(right_done, count(q, u))
                dve.tensor_tensor(y_b[:, u, C:D], ps[:, 7, :], x_b[:, u, C:D], ALU.add).then_inc(right_added, 1)

            def step(q, u, first, second=False):
                if not conv:
                    joint_max(q, u)
                if not (first and u == 0):
                    gate(*before(q, u))
                dve.wait_ge(qhi_done, count(q, u))
                dve.tensor_tensor(qt_lo[:, :], ps[:, 0, :], qt_hi[:, :], ALU.subtract).then_inc(qlo_done, 1)
                if not (first and u == 0):
                    low_o(*before(q, u))
                if not first:
                    add_right(q - 1, u)
                dve.wait_ge(scored, count(q, u))
                dve.tensor_reduce(stat[:, 0, :], ps[:, 1:3, :].rearrange("p a (b m) -> p (a b) m", m=MEM), AX.X,
                                  ALU.max).then_inc(maxed, 1)
                dve.wait_ge(maxed, count(q, u))
                dve.tensor_scalar(stat[:, 1, :], stat[:, 0, :], -SCALE, None, ALU.mult).then_inc(biased, 1)
                if conv:
                    dve.wait_ge(mhi_done, count(q, u))
                    dve.tensor_tensor(cat_lo[:, u, 0:KD, :], c_b[:, u, :, :], cat_hi[:, u, 0:KD, :], ALU.subtract
                                      ).then_inc(mlo_done, 1)
                else:
                    combine(q, u)
                dve.wait_ge(exped, count(q, u))
                dve.reciprocal(stat[:, 3, :], stat[:, 2, :]).then_inc(inverted, 1)
                if not (first and u == 0):
                    add_left(*before(q, u), first or (second and u == 0))
                dve.wait_ge(phi_done, count(q, u))
                dve.tensor_tensor(pt_lo[:, :, :].rearrange("p a b -> p (a b)"),
                                  ps[:, 3:5, :].rearrange("p a b -> p (a b)"),
                                  pt_hi[:, :, :].rearrange("p a b -> p (a b)"), ALU.subtract).then_inc(plo_done, 1)
                if not conv:
                    dve.wait_ge(mhi_done, count(q, u))
                    dve.tensor_tensor(cat_lo[:, u, 0:H, :].rearrange("p a b -> p (a b)"), ps[:, 0, :],
                                      cat_hi[:, u, 0:H, :].rearrange("p a b -> p (a b)"), ALU.subtract
                                      ).then_inc(mlo_done, 1)
            for u in range(2):
                step(0, u, True)
            for u in range(2):
                step(1, u, False, second=True)
            with dve.Fori(2, NT // 2) as q:
                for u in range(2):
                    step(q, u, False)
            gate(*LAST)
            low_o(*LAST)
            add_right(NT // 2 - 1, 0)
            add_left(*LAST, False)
            add_right(*LAST)

        @block.tensor
        def _(pe):
            def turn(bank, rows):
                for h in range(H):
                    t = pe.transpose(ps[:, bank, h * HD:(h + 1) * HD], rows[:, h * HD:(h + 1) * HD], ident[:, :])
                return t

            def project(u, half, chunks):
                cols = slice(half * C, (half + 1) * C)
                for k in chunks:
                    m = split3(pe, ps[:, 6 + half, :], cat_hi[:, u, k, :], cat_lo[:, u, k, :],
                               wo_hi[:, k, cols], wo_lo[:, k, cols], k == 0, k == KO - 1)
                return m

            def values(q, u):
                pe.wait_ge(plo_done, count(q, u))
                for h in range(H):
                    for mt in range(MT):
                        pe.matmul(sums_hl[:, h, :, :].rearrange("p x e -> p (x e)"), pt_hi[:, h * MT + mt, :],
                                  v_hl[:, mt, h, :, :].rearrange("p x e -> p (x e)"), start=(mt == 0), stop=False)
                        m = pe.matmul(sums_hl[:, h, 0, :], pt_lo[:, h * MT + mt, :], v_hl[:, mt, h, 0, :],
                                      start=False, stop=(mt == MT - 1))
                m.then_inc(summed, 1)

            def right_end(q, u):
                project(u, 1, range(MIX, KO)).then_inc(right_done, 1)

            def turn_o(q, u, first):
                pe.wait_ge(og_done, count(q, u))
                if not first:
                    pe.wait_ge(olo_done, count(q, u, 0))
                turn(5, og).then_inc(oturned, 1)

            def left(q, u, first):
                pe.wait_ge(mlo_done, count(q, u))
                if not first:
                    pe.wait_ge(left_added, count(q, u, 0))
                project(u, 0, range(MIX))
                pe.wait_ge(olo_done, count(q, u))
                project(u, 0, range(MIX, KO)).then_inc(left_done, 1)

            def right_begin(q, u, first):
                if not first:
                    pe.wait_ge(right_added, count(q, u, 0))
                project(u, 1, range(MIX))

            def step(q, u, first):
                started = not (first and u == 0)
                third = first and u == 1
                if started:
                    values(*before(q, u))
                pe.wait_ge(q_in[u], q * 16 + 16)
                if started:
                    pe.wait_ge(qlo_done if conv else mlo_done, count(q, u, 0))
                turn(0, q_b[:, u, :]).then_inc(qturned, 1)
                if not first:
                    right_end(q - 1, u)
                if started:
                    turn_o(*before(q, u), third)
                pe.wait_ge(qlo_done, count(q, u))
                for h in range(H):
                    at = (h % 2) * MEM
                    cols = slice(h * HD, (h + 1) * HD)
                    m = split3(pe, ps[:, 1 + h // 2, at:at + MEM], qt_hi[:, cols], qt_lo[:, cols],
                               kt_hi[:, h, :], kt_lo[:, h, :], True, True)
                m.then_inc(scored, 1)
                if started:
                    left(*before(q, u), third)
                pe.wait_ge(exped, count(q, u))
                for h in range(H):
                    for mt in range(MT):
                        at = ((h * MT + mt) % 4) * P
                        t = pe.transpose(ps[:, 3 + h // 2, at:at + P], prob[:, h, mt * P:(mt + 1) * P], ident[:, :])
                t.then_inc(pturned, 1)
                if not conv:
                    pe.wait_ge(ops, q * (2 * COPS) + (u + 1) * COPS)
                    turn(0, od).then_inc(mturned, 1)
                if started:
                    right_begin(*before(q, u), third)
            pairs(pe, NT, step)
            values(*LAST)
            right_end(NT // 2 - 1, 0)
            turn_o(*LAST, False)
            left(*LAST, False)
            right_begin(*LAST, False)
            right_end(*LAST)


def dil_stage(core, g, q_src, kv_src, dst, masks_r, ident_r, zeros):
    nc, ps, ident = core.nc, core.ps, core.ident
    d = DIL[g][1]
    per_stream = NT // d
    U = 4
    TURNS = NT // U
    tag = f"dil{g}"

    def has_prev(q, u):
        if per_stream == 1:
            return False
        if d > 1:
            return u > 0
        return not (isinstance(q, int) and q == 0 and u == 0)

    def rows(ap, q, u):
        view = ap.rearrange("(m d) c -> d m c", d=d)
        if per_stream == 1:
            return view[ds(q * U + u, 1), :, :].rearrange("o m c -> (o m) c")
        if d > 1:
            return view[ds(q, 1), u * P:(u + 1) * P, :].rearrange("o m c -> (o m) c")
        return view[:, ds(q * (U * P) + u * P, P), :].rearrange("o m c -> (o m) c")

    def turns(eng, body, tail=()):
        for u in range(U):
            body(0, u)
        with eng.Fori(1, TURNS) as q:
            for u in range(U):
                body(q, u)

    def back(q, u, k):
        if u >= k:
            return q, u - k
        if isinstance(q, int) and q == 0:
            return None
        return q - 1, u - k + U

    def cnt(s, extra=1):
        return s[0] * U + (s[1] + extra)

    def half_cnt(s, half):
        return s[0] * (2 * U) + (2 * s[1] + half + 1)

    def use(s, per=16):
        return s[0] * per + per

    with ExitStack() as st:
        q_b = core.sb(st, f"{tag}_q", [P, U, C])
        k_b = core.sb(st, f"{tag}_k", [P, U, C])
        v_b = core.sb(st, f"{tag}_v", [P, U, C])
        qt_hi = core.sb(st, f"{tag}_qthi", [P, C], F32R)
        qt_lo = core.sb(st, f"{tag}_qtlo", [P, C], F32R)
        kt_hi = core.sb(st, f"{tag}_kthi", [P, H, 2, P], F32R)
        kt_lo = core.sb(st, f"{tag}_ktlo", [P, H, 2, P], F32R)
        v_hl = core.sb(st, f"{tag}_vhl", [P, 2, H, 2, HD], F32R)
        prob = core.sb(st, f"{tag}_prob", [P, H, 2, P])
        pt_hi = core.sb(st, f"{tag}_pthi", [P, H, 2, P], F32R)
        pt_lo = core.sb(st, f"{tag}_ptlo", [P, H, 2, P], F32R)
        o_b = core.sb(st, f"{tag}_o", [P, U, OW])
        bias = core.sb(st, f"{tag}_bias", [P, H])
        names = ("qk_in0 qk_in1 qk_in2 qk_in3 v_in0 v_in1 v_in2 v_in3 o_out0 o_out1 o_out2 o_out3 "
                 "turned qhi_done khi_done qlo_done klo_done vhi_done "
                 "vlo_done scored maxed biased exped pturned phi_done plo_done summed o_begun o_done")
        sems = core.sems(st, tag, names)
        qk_in, v_in, o_out = sems[0:U], sems[U:2 * U], sems[2 * U:3 * U]
        (turned, qhi_done, khi_done, qlo_done, klo_done, vhi_done, vlo_done, scored, maxed, biased, exped, pturned,
         phi_done, plo_done, summed, o_begun, o_done) = sems[3 * U:]
        block = st.enter_context(nc.Block())

        def keys(s):
            return (1 - s[1] % 2, s[1] % 2) if has_prev(*s) else (s[1] % 2,)

        def span(s):
            ks = sorted(keys(s))
            return ks[0], ks[-1] + 1

        scores = ps[:, 1:3, :].rearrange("p a (b s k) -> p (a b) s k", b=2, s=2)
        sums_hl = ps[:, 6:8, :].rearrange("p a (b x e) -> p (a b) x e", b=2, x=2)
        turned_p = ps[:, 3:5, :].rearrange("p a (b s k) -> p (a b) s k", b=2, s=2)

        @block.sync
        def _(sp):
            def store(s):
                sp.wait_ge(o_done, cnt(s))
                sp.dma_start(rows(dst, *s), o_b[:, s[1], :]).then_inc(o_out[s[1]], 16)

            def body(q, u):
                if back(q, u, U):
                    sp.wait_ge(turned, cnt(back(q, u, U)))
                sp.dma_start(q_b[:, u, :], rows(q_src, q, u)).then_inc(qk_in[u], 16)
                sp.dma_start(k_b[:, u, :], rows(kv_src[:, 0:C], q, u)).then_inc(qk_in[u], 16)
                if back(q, u, U):
                    sp.wait_ge(vlo_done, cnt(back(q, u, U)))
                sp.dma_start(v_b[:, u, :], rows(kv_src[:, C:2 * C], q, u)).then_inc(v_in[u], 16)
                if back(q, u, 3):
                    store(back(q, u, 3))
            turns(sp, body)
            for u in (U - 3, U - 2, U - 1):
                store(back(TURNS, 0, U - u))
            for s in o_out:
                sp.wait_ge(s, 16 * TURNS)

        @block.gpsimd
        def _(pool):
            def body(q, u):
                slot = u % 2
                pool.wait_ge(v_in[u], use((q, u)))
                if back(q, u, 1):
                    pool.wait_ge(summed, cnt(back(q, u, 1)))
                v, zero = (t.rearrange("p (h e) -> p h e", h=H) for t in (v_b[:, u, :], zeros[:, :]))
                pool.tensor_tensor(v_hl[:, slot, :, 0, :], v, zero, ALU.add).then_inc(vhi_done, 1)
                pool.wait_ge(vhi_done, cnt((q, u)))
                pool.tensor_tensor(v_hl[:, slot, :, 1, :], v, v_hl[:, slot, :, 0, :], ALU.subtract
                                   ).then_inc(vlo_done, 1)
            turns(pool, body)

        @block.scalar
        def _(act):
            def exps(s, half):
                a, b = span(s)
                act.wait_ge(biased, half_cnt(s, half))
                for h in (2 * half, 2 * half + 1):
                    e = act.activation(prob[:, h, a:b, :], scores[:, h, a:b, :], ACT.Exp, scale=SCALE,
                                       bias=bias[:, h:h + 1],
                                       accum_out=o_b[:, s[1], C + H + h:C + H + h + 1])
                e.then_inc(exped, 1)

            def copy_sums(s):
                act.wait_ge(summed, cnt(s))
                act.activation(o_b[:, s[1], 0:C].rearrange("p (h e) -> p h e", h=H), sums_hl[:, :, 0, :], ACT.Copy
                               ).then_inc(o_begun, 1)

            def probs_high(s, half):
                a, b = span(s)
                heads = slice(2 * half, 2 * half + 2)
                act.wait_ge(pturned, half_cnt(s, half))
                act.activation(pt_hi[:, heads, a:b, :], turned_p[:, heads, a:b, :], ACT.Copy).then_inc(phi_done, 1)

            def body(q, u):
                if back(q, u, 1):
                    exps(back(q, u, 1), 0)
                act.wait_ge(turned, cnt((q, u)))
                act.activation(qt_hi[:, :], ps[:, 0, :], ACT.Copy).then_inc(qhi_done, 1)
                act.activation(kt_hi[:, :, u % 2, :], ps[:, 5, :].rearrange("p (h k) -> p h k", h=H), ACT.Copy
                               ).then_inc(khi_done, 1)
                if back(q, u, 1):
                    exps(back(q, u, 1), 1)
                    probs_high(back(q, u, 1), 0)
                    probs_high(back(q, u, 1), 1)
                if back(q, u, 2):
                    copy_sums(back(q, u, 2))
            turns(act, body)
            last, before = back(TURNS, 0, 1), back(TURNS, 0, 2)
            for half in range(2):
                exps(last, half)
            for half in range(2):
                probs_high(last, half)
            copy_sums(before)
            copy_sums(last)

        @block.vector
        def _(dve):
            def maxima(s, half):
                a, b = span(s)
                slot = s[1]
                heads, cols = slice(2 * half, 2 * half + 2), slice(C + 2 * half, C + 2 * half + 2)
                dve.wait_ge(scored, half_cnt(s, half))
                if half == 0 and back(*s, U):
                    dve.wait_ge(o_out[slot], s[0] * 16)
                dve.tensor_reduce(o_b[:, slot, cols], scores[:, heads, a:b, :].rearrange("p h s k -> p h (s k)"),
                                  AX.X, ALU.max).then_inc(maxed, 1)
                dve.wait_ge(maxed, half_cnt(s, half))
                dve.tensor_scalar(bias[:, heads], o_b[:, slot, cols], -SCALE, None, ALU.mult).then_inc(biased, 1)

            def probs_low(s, half):
                a, b = span(s)
                heads = slice(2 * half, 2 * half + 2)
                dve.wait_ge(phi_done, half_cnt(s, half))
                dve.tensor_tensor(pt_lo[:, heads, a:b, :].rearrange("p h s k -> p h (s k)"),
                                  turned_p[:, heads, a:b, :].rearrange("p h s k -> p h (s k)"),
                                  pt_hi[:, heads, a:b, :].rearrange("p h s k -> p h (s k)"), ALU.subtract
                                  ).then_inc(plo_done, 1)

            def add_sums(s):
                o = o_b[:, s[1], 0:C].rearrange("p (h e) -> p h e", h=H)
                dve.wait_ge(o_begun, cnt(s))
                dve.tensor_tensor(o, sums_hl[:, :, 1, :], o, ALU.add).then_inc(o_done, 1)

            def attend(q, u):
                one, two, three = (back(q, u, k) for k in (1, 2, 3))
                if two:
                    probs_low(two, 0)
                if one:
                    maxima(one, 0)
                if three:
                    add_sums(three)
                if two:
                    probs_low(two, 1)
                if one:
                    maxima(one, 1)

            def body(q, u):
                attend(q, u)
                dve.wait_ge(qhi_done, cnt((q, u)))
                dve.tensor_tensor(qt_lo[:, :], ps[:, 0, :], qt_hi[:, :], ALU.subtract).then_inc(qlo_done, 1)
                dve.wait_ge(khi_done, cnt((q, u)))
                dve.tensor_tensor(kt_lo[:, :, u % 2, :], ps[:, 5, :].rearrange("p (h k) -> p h k", h=H),
                                  kt_hi[:, :, u % 2, :], ALU.subtract).then_inc(klo_done, 1)
            turns(dve, body)
            attend(TURNS, 0)
            last = back(TURNS, 0, 1)
            for half in range(2):
                probs_low(last, half)
            add_sums(back(TURNS, 0, 2))
            add_sums(last)

        @block.tensor
        def _(pe):
            def score(s):
                a, b = span(s)
                own = s[1] % 2
                if has_prev(*s):
                    mask = masks_r[:, 0:2 * P] if own else masks_r[:, P:3 * P]
                else:
                    mask = masks_r[:, P:2 * P]
                pe.wait_ge(qlo_done, cnt(s))
                pe.wait_ge(klo_done, cnt(s))
                for h in range(H):
                    cols = slice(h * HD, (h + 1) * HD)
                    acc = scores[:, h, a:b, :].rearrange("p s k -> p (s k)")
                    pe.matmul(acc, ident_r[:, :], mask, start=True, stop=False)
                    m = split3(pe, acc, qt_hi[:, cols], qt_lo[:, cols],
                               kt_hi[:, h, a:b, :].rearrange("p s k -> p (s k)"),
                               kt_lo[:, h, a:b, :].rearrange("p s k -> p (s k)"), False, True)
                    if h % 2:
                        m.then_inc(scored, 1)

            def turn(q, u):
                pe.wait_ge(qk_in[u], use((q, u), 32))
                for h in range(H):
                    cols = slice(h * HD, (h + 1) * HD)
                    pe.transpose(ps[:, 0, cols], q_b[:, u, cols], ident[:, :])
                for h in range(H):
                    cols = slice(h * HD, (h + 1) * HD)
                    t = pe.transpose(ps[:, 5, cols], k_b[:, u, cols], ident[:, :])
                t.then_inc(turned, 1)

            def sums(s):
                pe.wait_ge(vlo_done, cnt(s))
                if back(*s, 1):
                    pe.wait_ge(o_done, cnt(back(*s, 1)))
                ks = keys(s)
                for h in range(H):
                    if h % 2 == 0:
                        pe.wait_ge(plo_done, half_cnt(s, h // 2))
                    for j, key in enumerate(ks):
                        last = j == len(ks) - 1
                        pe.matmul(sums_hl[:, h, :, :].rearrange("p x e -> p (x e)"), pt_hi[:, h, key, :],
                                  v_hl[:, key, h, :, :].rearrange("p x e -> p (x e)"), start=(j == 0), stop=False)
                        m = pe.matmul(sums_hl[:, h, 0, :], pt_lo[:, h, key, :], v_hl[:, key, h, 0, :],
                                      start=False, stop=last)
                m.then_inc(summed, 1)

            def turn_probs(s):
                for h in range(H):
                    if h % 2 == 0:
                        pe.wait_ge(exped, half_cnt(s, h // 2))
                    for key in keys(s):
                        t = pe.transpose(turned_p[:, h, key, :], prob[:, h, key, :], ident[:, :])
                    if h % 2:
                        t.then_inc(pturned, 1)

            def body(q, u):
                if back(q, u, 1):
                    score(back(q, u, 1))
                turn(q, u)
                if back(q, u, 2):
                    sums(back(q, u, 2))
                if back(q, u, 1):
                    turn_probs(back(q, u, 1))
            turns(pe, body)
            last, before = back(TURNS, 0, 1), back(TURNS, 0, 2)
            score(last)
            sums(before)
            turn_probs(last)
            sums(last)


def masks_stage(core, masks, masks_r, ident_r, zeros):
    nc, ident = core.nc, core.ident
    with ExitStack() as st:
        zeroed, made, = core.sems(st, "masks", "zeroed made")
        block = st.enter_context(nc.Block())

        @block.gpsimd
        def _(pool):
            pool.memset(masks[:, :], 0.0).then_inc(zeroed, 1)
            pool.wait_ge(zeroed, 1)
            for at, sign in ((0, -1), (1, 1), (2, -1)):
                cols = masks[:, at * P:(at + 1) * P]
                pool.affine_select(out=cols, in_=cols, compare_op=ALU.is_ge, fill=NEG, base=0,
                                   pattern=[[-sign, P]], channel_multiplier=sign).then_inc(made, 1)

        @block.vector
        def _(dve):
            dve.wait_ge(made, 3)
            dve.tensor_copy(masks_r[:, :], masks[:, :])
            dve.tensor_copy(ident_r[:, :], ident[:, :])
            dve.memset(zeros[:, :], 0.0)


def dec_stage(core, layer, src, x_s, y_s, wo_hi, wo_lo):
    nc, ps, ident, io = core.nc, core.ps, core.ident, core.io
    tag = f"dec{layer}"
    conv = layer == 0
    MIX = KD if conv else H
    KO = MIX + H
    HS = H * S
    NG = len(DIL)
    GW = P + S
    NZ = 3 if conv else 2 + NG
    NP = 4
    SP = S // NP
    WIN = HS + S
    with ExitStack() as st:
        q_rows = core.sb(st, f"{tag}_q", [S, C])
        mgate = core.sb(st, f"{tag}_mgate", [HS, HD])
        mk = core.sb(st, f"{tag}_mk", [P, S, H, MEM])
        zone = core.sb(st, f"{tag}_zone", [P, NZ, HS * HS])
        pr = core.sb(st, f"{tag}_pr", [HS, MEM])
        og = core.sb(st, f"{tag}_og", [HS, 2, HD])
        stat = core.sb(st, f"{tag}_stat", [HS, 8])
        cat_hi = core.sb(st, f"{tag}_cathi", [P, KO, S], F32R)
        cat_lo = core.sb(st, f"{tag}_catlo", [P, KO, S], F32R)
        xs = core.sb(st, f"{tag}_xs", [S, D])
        if conv:
            mv = core.sb(st, f"{tag}_mv", [P, S, MT, C])
            conv_in = core.sb(st, f"{tag}_conv", [S, D])
        else:
            mv = mk.rearrange("p s h m -> p s (h m)").rearrange("p s (m c) -> p s m c", m=MT)
            dgate = core.sb(st, f"{tag}_dgate", [HS, HD])
            qd = core.sb(st, f"{tag}_qd", [S, NG, C])
            kvn = core.sb(st, f"{tag}_kvn", [S, NG, 2, C])
            kd = core.sb(st, f"{tag}_kd", [P, NG, S, C])
            knt = core.sb(st, f"{tag}_knt", [P, NG, HS])
            qheads = core.sb(st, f"{tag}_qheads", [P, NG, H, WIN])
            pheads = core.sb(st, f"{tag}_pheads", [S, NG, H, WIN])
            other = core.sb(st, f"{tag}_other", [HS, 2, S])
            dpr = core.sb(st, f"{tag}_dpr", [HS, NG * GW])
        names = ("in_done gates_in mk_in0 mk_in1 mk_in2 mk_in3 mv_in0 mv_in1 mv_in2 mv_in3 kd_in0 kd_in1 kd_in2 "
                 "vd_in0 vd_in1 vd_in2 zeroed rows_turned q_copied m_scored m_maxed m_biased m_exped "
                 "m_inverted m_turned m_copied m_summed m_gated m_oturned m_ohi m_olo d_scored d_masked d_maxed "
                 "d_biased d_exped d_inverted d_turned d_copied d_summed d_gated d_oturned d_ohi d_olo mk_used "
                 "kd_used same_made other_made chi clo projected y_done y_out")
        sems = dict(zip(names.split(), core.sems(st, tag, names)))
        mk_in, mv_in = ([sems[f"{n}_in{i}"] for i in range(NP)] for n in ("mk", "mv"))
        kd_in, vd_in = ([sems[f"{n}_in{g}"] for g in range(NG)] for n in ("kd", "vd"))
        in_done, gates_in, zeroed, rows_turned, q_copied = (
            sems[n] for n in "in_done gates_in zeroed rows_turned q_copied".split())
        (m_scored, m_maxed, m_biased, m_exped, m_inverted, m_turned, m_copied, m_summed, m_gated, m_oturned,
         m_ohi, m_olo) = (sems[n] for n in names.split() if n.startswith("m_"))
        (d_scored, d_masked, d_maxed, d_biased, d_exped, d_inverted, d_turned, d_copied, d_summed, d_gated,
         d_oturned, d_ohi, d_olo) = (sems[n] for n in names.split() if n.startswith("d_"))
        mk_used, kd_used, same_made, other_made, chi, clo, projected, y_done, y_out = (
            sems[n] for n in names.split()[-9:])
        block = st.enter_context(nc.Block())
        LOADS = 2 if conv else 3
        TURNED, MSC, DSC, MPT, DPT, SUMS = 0, 1, 2, 3, 4, 5

        def diagonal(z):
            return zone[:, z, 0:HS * HS:HS + 1]

        def window(z, c):
            return zone[:, z, c * HS:(c + 1) * HS]

        def head_window(t, g, h):
            return t[:, g, :, :].rearrange("p h w -> p (h w)")[:, h * HS:(h + 1) * HS]

        def load_mk(eng, i):
            at = (layer * S + i * SP) * P
            eng.dma_start(mk[:, i * SP:(i + 1) * SP, :, :].rearrange("p s h m -> p s (h m)"),
                          io["cache_kt"][at:at + SP * P, :].rearrange("(s p) c -> p s c", p=P)).then_inc(mk_in[i], 16)

        def load_mv(eng, i):
            for m in range(MT):
                eng.dma_start(mv[:, i * SP:(i + 1) * SP, m, :],
                              io["cache_v"][layer, i * SP:(i + 1) * SP, m * P:(m + 1) * P, :].rearrange(
                                  "s p c -> p s c")).then_inc(mv_in[i], 16)

        def load_dil(eng, g, cache, sem):
            eng.dma_start(kd[:, g, :, :], cache[g * S * P:(g + 1) * S * P, :].rearrange("(s p) c -> p s c", p=P)
                          ).then_inc(sem[g], 16)

        @block.sync
        def _(sp):
            sp.dma_start(q_rows[:, :], src["q"][T:TS, :]).then_inc(in_done, 16)
            if conv:
                for i in range(NP):
                    load_mk(sp, i)
            else:
                sp.dma_start(kvn[:, :, :, :].rearrange("s g a c -> s g (a c)"),
                             src["kv"].rearrange("g t c -> t g c")[T:TS, :, :]).then_inc(in_done, 16)
                load_mk(sp, 1)
                load_mk(sp, 3)
                load_dil(sp, 0, io["dil_kt"], kd_in)
                load_dil(sp, 2, io["dil_kt"], kd_in)
                for i in (1, 3):
                    sp.wait_ge(mk_used, i + 1)
                    load_mv(sp, i)
                sp.wait_ge(kd_used, 1)
                load_dil(sp, 0, io["dil_v"], vd_in)
                sp.wait_ge(kd_used, 3)
                load_dil(sp, 2, io["dil_v"], vd_in)
            sp.wait_ge(y_done, 1)
            sp.dma_start(y_s, xs[:, :]).then_inc(y_out, 16)
            sp.wait_ge(y_out, 16)

        @block.gpsimd
        def _(pool):
            pool.memset(zone[:, 1:NZ, :], 0.0).then_inc(zeroed, 1)
            for h in range(H):
                pool.dma_start(mgate[h * S:(h + 1) * S, :], src["mg"][T:TS, h * HD:(h + 1) * HD]).then_inc(gates_in, 16)
                if not conv:
                    pool.dma_start(dgate[h * S:(h + 1) * S, :], src["gd"][T:TS, h * HD:(h + 1) * HD]
                                   ).then_inc(gates_in, 16)
            pool.dma_start(xs[:, :], x_s).then_inc(gates_in, 16)

        @block.scalar
        def _(act):
            if conv:
                act.dma_start(conv_in[:, :], src["conv_s"]).then_inc(in_done, 16)
                for i in range(NP):
                    load_mv(act, i)
            else:
                act.dma_start(qd[:, :, :], src["qd"].rearrange("g t c -> t g c")[T:TS, :, :]).then_inc(in_done, 16)
                load_mk(act, 0)
                load_mk(act, 2)
                load_dil(act, 1, io["dil_kt"], kd_in)
                for i in (0, 2):
                    act.wait_ge(mk_used, i + 1)
                    load_mv(act, i)
            act.wait_ge(m_biased, 1)
            act.activation(pr[:, :], ps[0:HS, MSC, 0:MEM], ACT.Exp, scale=SCALE, bias=stat[:, 1:2],
                           accum_out=stat[:, 2:3]).then_inc(m_exped, 1)
            if not conv:
                act.wait_ge(kd_used, 2)
                load_dil(act, 1, io["dil_v"], vd_in)
                act.wait_ge(d_biased, 1)
                act.activation(dpr[:, :], ps[0:HS, DSC, 0:NG * GW], ACT.Exp, scale=SCALE, bias=stat[:, 5:6],
                               accum_out=stat[:, 6:7]).then_inc(d_exped, 1)

        @block.tensor
        def _(pe):
            id_s = ident[0:S, 0:S]

            def turn_rows(at, rows, n=H):
                for h in range(n):
                    t = pe.transpose(ps[:, TURNED, at + h * S:at + (h + 1) * S], rows[:, h * P:(h + 1) * P], id_s)
                return t

            def project(chunks, start=False, stop=False):
                for half in range(2):
                    cols = slice(half * C, (half + 1) * C)
                    for k in chunks:
                        mm = split3(pe, ps[0:S, 6 + half, :], cat_hi[:, k, :], cat_lo[:, k, :], wo_hi[:, k, cols],
                                    wo_lo[:, k, cols], start and k == chunks[0], stop and k == chunks[-1])
                return mm
            pe.wait_ge(in_done, 16 * LOADS)
            t = turn_rows(0, q_rows)
            if conv:
                t = turn_rows(HS, conv_in, KD)
            else:
                for g in range(NG):
                    turn_rows((1 + g) * HS, qd[:, g, :])
                    t = turn_rows((1 + NG + g) * HS, kvn[:, g, 0, :])
            t.then_inc(rows_turned, 1)
            if conv:
                pe.wait_ge(clo, 1)
                project(range(MIX), start=True)
            pe.wait_ge(q_copied, 1)
            for i in range(NP):
                pe.wait_ge(mk_in[i], 16)
                for b in range(i * SP, (i + 1) * SP):
                    for h in range(H):
                        mm = pe.matmul(ps[0:HS, MSC, 0:MEM], window(0, h * S + b), mk[:, b, h, :],
                                       start=(b == 0 and h == 0), stop=(b == S - 1 and h == H - 1))
                mm.then_inc(mk_used, 1)
            if not conv:
                for g in range(NG):
                    for h in range(H):
                        pe.matmul(ps[0:HS, DSC, g * GW + P:(g + 1) * GW], head_window(qheads, g, h),
                                  knt[:, g, h * S:(h + 1) * S], start=(h == 0), stop=(h == H - 1))
                for g in range(NG):
                    pe.wait_ge(kd_in[g], 16)
                    for b in range(S):
                        for h in range(H):
                            mm = pe.matmul(ps[0:HS, DSC, g * GW:g * GW + P], window(1 + g, h * S + b),
                                           kd[:, g, b, h * P:(h + 1) * P],
                                           start=(b == 0 and h == 0), stop=(b == S - 1 and h == H - 1))
                    mm.then_inc(kd_used, 1)
            pe.wait_ge(m_exped, 1)
            for m in range(MT):
                t = pe.transpose(ps[:, MPT, m * HS:(m + 1) * HS], pr[:, m * P:(m + 1) * P], ident[0:HS, 0:HS])
            t.then_inc(m_turned, 1)
            pe.wait_ge(m_copied, 1)
            for i in range(NP):
                pe.wait_ge(mv_in[i], 16 * MT)
                for b in range(i * SP, (i + 1) * SP):
                    for h in range(H):
                        for m in range(MT):
                            mm = pe.matmul(ps[0:HS, SUMS, 0:HD], window((0, NZ - 1)[m], h * S + b),
                                           mv[:, b, m, h * HD:(h + 1) * HD], start=(b == 0 and h == 0 and m == 0),
                                           stop=(b == S - 1 and h == H - 1 and m == MT - 1))
            mm.then_inc(m_summed, 1)
            if not conv:
                pe.wait_ge(d_exped, 1)
                for g in range(NG):
                    pe.transpose(ps[:, DPT, g * HS:(g + 1) * HS], dpr[:, g * GW:g * GW + P], ident[0:HS, 0:HS])
                    at = (NG + g) * HS
                    t = pe.transpose(ps[0:S, DPT, at:at + HS], dpr[:, g * GW + P:(g + 1) * GW], ident[0:HS, 0:HS])
                t.then_inc(d_turned, 1)
                pe.wait_ge(d_copied, 1)
                for g in range(NG):
                    for h in range(H):
                        pe.matmul(ps[0:HS, MSC, 0:HD], head_window(pheads, g, h),
                                  kvn[:, g, 1, h * HD:(h + 1) * HD], start=(g == 0 and h == 0), stop=False)
                for g in range(NG):
                    pe.wait_ge(vd_in[g], 16)
                    for b in range(S):
                        for h in range(H):
                            last = g == NG - 1 and b == S - 1 and h == H - 1
                            mm = pe.matmul(ps[0:HS, MSC, 0:HD], window(1 + g, h * S + b),
                                           kd[:, g, b, h * HD:(h + 1) * HD], start=False, stop=last)
                mm.then_inc(d_summed, 1)
            pe.wait_ge(m_gated, 1)
            pe.transpose(ps[:, MPT, 0:HS], og[:, 0, :], ident[0:HS, 0:HS]).then_inc(m_oturned, 1)
            if not conv:
                pe.wait_ge(d_gated, 1)
                pe.transpose(ps[:, DPT, 0:HS], og[:, 1, :], ident[0:HS, 0:HS]).then_inc(d_oturned, 1)
            pe.wait_ge(m_olo, 1)
            mm = project(range(MIX, KO), start=not conv, stop=conv)
            if not conv:
                pe.wait_ge(d_olo, 1)
                mm = project(range(MIX), stop=True)
            mm.then_inc(projected, 1)

        @block.vector
        def _(dve):
            if not conv:
                dve.tensor_reduce(other[:, 0, :], ident[0:HS, 0:HS].rearrange("p (h b) -> p b h", b=S), AX.X,
                                  ALU.add).then_inc(same_made, 1)
                dve.wait_ge(same_made, 1)
                dve.tensor_scalar(other[:, 1, :], other[:, 0, :], -1.0, -NEG, ALU.add, ALU.mult
                                  ).then_inc(other_made, 1)
                dve.memset(qheads[:, :, :, :], 0.0).then_inc(zeroed, 1)
                dve.memset(pheads[:, :, :, :], 0.0).then_inc(zeroed, 1)
            dve.memset(zone[:, 0, :], 0.0).then_inc(zeroed, 1)
            dve.wait_ge(rows_turned, 1)
            if conv:
                turned = ps[:, TURNED, HS:HS + KD * S]
                dve.tensor_copy(cat_hi[:, 0:KD, :].rearrange("p k s -> p (k s)"), turned).then_inc(chi, 1)
                dve.wait_ge(chi, 1)
                dve.tensor_tensor(cat_lo[:, 0:KD, :].rearrange("p k s -> p (k s)"), turned,
                                  cat_hi[:, 0:KD, :].rearrange("p k s -> p (k s)"), ALU.subtract).then_inc(clo, 1)
            dve.wait_ge(zeroed, 2 if conv else 4)
            if not conv:
                for g in range(NG):
                    dve.tensor_copy(diagonal(1 + g), ps[:, TURNED, (1 + g) * HS:(2 + g) * HS])
                dve.tensor_copy(qheads[:, :, :, 0:S],
                                ps[:, TURNED, HS:(1 + NG) * HS].rearrange("p (g h b) -> p g h b", h=H, b=S))
                dve.tensor_copy(knt[:, :, :].rearrange("p g c -> p (g c)"),
                                ps[:, TURNED, (1 + NG) * HS:(1 + 2 * NG) * HS])
            dve.tensor_copy(diagonal(0), ps[:, TURNED, 0:HS]).then_inc(q_copied, 1)
            dve.wait_ge(mk_used, NP)
            dve.tensor_reduce(stat[:, 0:1], ps[0:HS, MSC, 0:MEM], AX.X, ALU.max).then_inc(m_maxed, 1)
            dve.wait_ge(m_maxed, 1)
            dve.tensor_scalar(stat[:, 1:2], stat[:, 0:1], -SCALE, None, ALU.mult).then_inc(m_biased, 1)
            if not conv:
                dve.wait_ge(kd_used, NG)
                dve.wait_ge(other_made, 1)
                new = ps[0:HS, DSC, 0:NG * GW].rearrange("p (g w) -> p g w", w=GW)[:, :, P:GW]
                dve.tensor_tensor(new, new, other[:, 1:2, :].to_broadcast([HS, NG, S]), ALU.add
                                  ).then_inc(d_masked, 1)
                dve.wait_ge(d_masked, 1)
                dve.tensor_reduce(stat[:, 4:5], ps[0:HS, DSC, 0:NG * GW], AX.X, ALU.max).then_inc(d_maxed, 1)
                dve.wait_ge(d_maxed, 1)
                dve.tensor_scalar(stat[:, 5:6], stat[:, 4:5], -SCALE, None, ALU.mult).then_inc(d_biased, 1)
            dve.wait_ge(m_exped, 1)
            dve.reciprocal(stat[:, 3:4], stat[:, 2:3]).then_inc(m_inverted, 1)
            dve.wait_ge(m_turned, 1)
            dve.tensor_copy(diagonal(NZ - 1), ps[:, MPT, HS:2 * HS])
            dve.tensor_copy(diagonal(0), ps[:, MPT, 0:HS]).then_inc(m_copied, 1)
            if not conv:
                dve.wait_ge(d_exped, 1)
                dve.reciprocal(stat[:, 7:8], stat[:, 6:7]).then_inc(d_inverted, 1)
                dve.wait_ge(d_turned, 1)
                for g in range(NG):
                    dve.tensor_copy(diagonal(1 + g), ps[:, DPT, g * HS:(g + 1) * HS])
                dve.tensor_copy(pheads[:, :, :, 0:S],
                                ps[0:S, DPT, NG * HS:2 * NG * HS].rearrange("p (g h b) -> p g h b", h=H, b=S)
                                ).then_inc(d_copied, 1)

            def gate(n, bank, inverse, gates, summed, gated, waits):
                dve.wait_ge(summed, 1)
                dve.wait_ge(gates_in, 16 * waits)
                dve.scalar_tensor_tensor(out=og[:, n, :], in0=ps[0:HS, bank, 0:HD], scalar=inverse,
                                         in1=gates, op0=ALU.mult, op1=ALU.mult).then_inc(gated, 1)

            def split(bank, chunks, oturned, ohi, olo):
                hi, lo = (c[:, chunks, :].rearrange("p h b -> p (h b)") for c in (cat_hi, cat_lo))
                dve.wait_ge(oturned, 1)
                dve.tensor_copy(hi, ps[:, bank, 0:HS]).then_inc(ohi, 1)
                dve.wait_ge(ohi, 1)
                dve.tensor_tensor(lo, ps[:, bank, 0:HS], hi, ALU.subtract).then_inc(olo, 1)
            gates = H + 1 if conv else 2 * H + 1
            dve.wait_ge(m_inverted, 1)
            gate(0, SUMS, stat[:, 3:4], mgate[:, :], m_summed, m_gated, gates)
            if not conv:
                dve.wait_ge(d_inverted, 1)
                gate(1, MSC, stat[:, 7:8], dgate[:, :], d_summed, d_gated, gates)
            split(MPT, slice(MIX, KO), m_oturned, m_ohi, m_olo)
            if not conv:
                split(DPT, slice(0, H), d_oturned, d_ohi, d_olo)
            dve.wait_ge(projected, 1)
            dve.tensor_tensor(xs[:, 0:C], ps[0:S, 6, :], xs[:, 0:C], ALU.add)
            dve.tensor_tensor(xs[:, C:D], ps[0:S, 7, :], xs[:, C:D], ALU.add).then_inc(y_done, 1)


def build(nc, io):
    with ExitStack() as ctx:
        core = Core(nc, ctx, io)
        gains = core.sb(ctx, "gains", [P, 5 * KD])
        norm_a, kv_norm, norm_b, mem_norm_0, mem_norm_1 = (gains[:, n * KD:(n + 1) * KD] for n in range(5))
        setup_stage(core, gains)

        def wide(stack, name):
            return [core.sb(stack, f"{name}_{n}", shape, F32R)
                    for n, shape in (("xthi", [P, KD, TS]), ("xtlo", [P, KD, TS]),
                                     ("wh0", [P, KD, C]), ("wl0", [P, KD, C]))]

        def output_side(layer, w_mem, w_out, chunks, mem_norm, src, x, x_s, y, y_s):
            with ExitStack() as st:
                wo_hi = core.sb(st, f"wohi{layer}", [P, chunks, D], F32R)
                wo_lo = core.sb(st, f"wolo{layer}", [P, chunks, D], F32R)
                with ExitStack() as kvs:
                    kt_hi, kt_lo = (core.sb(kvs, f"mk{n}{layer}", [P, H, MEM], F32R) for n in ("hi", "lo"))
                    v_hl = core.sb(kvs, f"mvhl{layer}", [P, MT, H, 2, HD], F32R)
                    memkv_stage(core, layer, w_mem, io["mem_kv"][layer * MEM:(layer + 1) * MEM, :], w_out, chunks,
                                wo_hi, wo_lo, kt_hi, kt_lo, v_hl, mem_norm, 8 + layer)
                    out_stage(core, layer, src, x, y, wo_hi, wo_lo, kt_hi, kt_lo, v_hl)
                dec_stage(core, layer, src, x_s, y_s, wo_hi, wo_lo)

        with ExitStack() as st:
            xt_hi, xt_lo, wh0, wl0 = wide(st, "a")
            prep = Prep(core, "prepa", io["x_prompt"], io["x_sample"], xt_hi, xt_lo, io["w_a"], wh0, wl0, norm_a)
            wh1, wl1 = prep.buffers(st)
            wh, wl = (wh0, wh1), (wl0, wl1)
            conv_stage(core, prep, io["w_a"], xt_hi, xt_lo, wh, wl, norm_a)
            tokens_stage(core, "toka", io["w_a"][(NCONV + 1) * D:, :],
                         [("norm", io["tok_a"][0], norm_a, 6), ("silu", io["tok_a"][1], None, None)],
                         xt_hi, xt_lo, wh, wl)
        src = {"q": io["tok_a"][0], "mg": io["tok_a"][1], "conv_t": io["conv_t"], "conv_s": io["conv_s"]}
        output_side(0, io["w_mem"][0:D, :], io["w_out_a"], KD + H, mem_norm_0, src, io["x_prompt"],
                    io["x_sample"], io["x1"][0:T, :], io["x1"][T:TS, :])
        with ExitStack() as st:
            xt_hi, xt_lo, wh0, wl0 = wide(st, "b")
            prep = Prep(core, "prepb", io["x1"][0:T, :], io["x1"][T:TS, :], xt_hi, xt_lo, io["w_b"], wh0, wl0,
                        kv_norm)
            wh1, wl1 = prep.buffers(st)
            wh, wl = (wh0, wh1), (wl0, wl1)
            kv = lambda g, part: io["kv"][g][:, part * C:(part + 1) * C]
            blocks = []
            for g in range(len(DIL)):
                blocks.append(("norm", kv(g, 0), kv_norm, g))
                blocks.append(("copy", kv(g, 1), kv_norm if g < 2 else norm_b, None))
            for g in range(len(DIL)):
                blocks.append(("norm", io["tok_b"][g], norm_b, 3 + g))
            blocks.append(("norm", io["tok_b"][3], norm_b, 7))
            blocks.append(("silu", io["tok_b"][4], norm_b, None))
            blocks.append(("silu", io["tok_b"][5], None, None))
            tokens_stage(core, "tokb", io["w_b"][D:, :], blocks, xt_hi, xt_lo, wh, wl, prep)
        with ExitStack() as st:
            masks = core.sb(st, "masks", [P, 3 * P])
            masks_r = core.sb(st, "masks_r", [P, 3 * P], F32R)
            ident_r = core.sb(st, "ident_r", [P, P], F32R)
            zeros = core.sb(st, "zeros", [P, C])
            masks_stage(core, masks, masks_r, ident_r, zeros)
            for g in range(len(DIL)):
                dil_stage(core, g, io["tok_b"][g][0:T, :], io["kv"][g][0:T, :], io["grp"][g * T:(g + 1) * T, :],
                          masks_r, ident_r, zeros)
        src = {"q": io["tok_b"][3], "mg": io["tok_b"][5], "gd": io["tok_b"][4], "grp": io["grp"],
               "qd": io["tok_b"][0:3], "kv": io["kv"]}
        output_side(1, io["w_mem"][D:2 * D, :], io["w_out_b"], 2 * H, mem_norm_1, src, io["x1"][0:T, :],
                    io["x1"][T:TS, :], io["y"][0:T, :], io["y"][T:TS, :])


def kernel(**inputs):
    import concourse.bacc as bacc
    from concourse.bass_utils import run_bass_kernel_spmd

    a = {k: np.asarray(v) for k, v in inputs.items()}
    layout = np.ascontiguousarray
    w_in_a, w_in_b = a["w_in_a"][0], a["w_in_b"][0]
    part = lambda w, n: w[:, n * D:(n + 1) * D].reshape(D, NCONV, P)
    conv_w = np.stack([part(w_in_a, n) for n in (1, 0, 3, 2)], axis=2)
    w_a = np.concatenate([conv_w.transpose(1, 0, 2, 3).reshape(NCONV * D, C),
                          w_in_a[:, 4 * D:].reshape(D, 2, C).transpose(1, 0, 2).reshape(2 * D, C)])
    b_cols = w_in_b.reshape(D, 6, C)[:, [0, 1, 2, 4, 3, 5], :]
    w_b = np.concatenate([a["w_kv"].reshape(D, 6, C).transpose(1, 0, 2).reshape(6 * D, C),
                          b_cols.transpose(1, 0, 2).reshape(6 * D, C)])
    columns = np.stack([a["norm_a"][0], a["kv_norm"], a["norm_b"][0], a["mem_norm"][0], a["mem_norm"][1]])
    rows = np.concatenate([a["k_norm_dil"], a["q_norm_b"][0], a["mem_q_norm"], a["mem_k_norm"]])
    caches = [a["cache_dil0_kv"], a["cache_dil1_kv"], a["cache_dil2_kv"]]
    dil = np.stack([c[:, ::d] for c, (_, d) in zip(caches, DIL)])
    mem = a["cache_mem_kv"]
    conv_rows = np.concatenate([np.broadcast_to(a["conv_w_a"], (S, 3, D)), a["state_conv"][0]], axis=1)
    arrays = {
        "x_prompt": a["x_prompt"][0],
        "x_sample": a["x_sample"][:, 0],
        "mem_prompt": a["mem_prompt"][0],
        "w_a": w_a,
        "w_b": w_b,
        "w_mem": a["w_mem_kv"].reshape(2 * D, 2 * C),
        "w_out_a": a["w_out_a"][0],
        "w_out_b": a["w_out_b"][0],
        "gain_cols": columns.reshape(5, KD, P).transpose(2, 0, 1).reshape(P, 5 * KD),
        "gain_rows": np.tile(rows, (1, H)),
        "conv_taps": a["conv_w_a"][0].T,
        "conv_rows": conv_rows.reshape(S, 5, NCONV, P).transpose(2, 0, 1, 3).reshape(NCONV * S, 5 * P),
        "cache_kt": mem[:, :, :, 0].transpose(0, 1, 4, 3, 2).reshape(2 * S * P, H * MEM),
        "cache_v": mem[:, :, :, 1].reshape(2, S, MEM, C),
        "dil_kt": dil[:, :, :, 0].transpose(0, 1, 4, 3, 2).reshape(3 * S * P, H * P),
        "dil_v": dil[:, :, :, 1].reshape(3 * S * P, C),
    }
    arrays = {k: layout(v) for k, v in arrays.items()}
    outs = {"y": (TS, D), "mem_kv": (2 * MEM, 2 * C), "tail": (D, 2), "tail_s": (S, 2 * D), "kv": (3, TS, 2 * C)}
    scratch = {"conv_t": (D, T), "conv_s": (S, D), "tok_a": (2, TS, C), "tok_b": (6, TS, C),
               "grp": (3 * T, OW), "x1": (TS, D)}
    nc = bacc.Bacc("TRN2", target_bir_lowering=False, num_devices=1)
    io = {}
    for name, v in arrays.items():
        io[name] = nc.dram_tensor(f"{name}_dram", v.shape, F32, kind="ExternalInput").ap()
    for name, shape in outs.items():
        io[name] = nc.dram_tensor(f"{name}_dram", shape, F32, kind="ExternalOutput").ap()
    for name, shape in scratch.items():
        io[name] = nc.dram_tensor(f"{name}_dram", shape, F32, kind="Internal").ap()
    build(nc, io)
    r = run_bass_kernel_spmd(nc, [{f"{k}_dram": v for k, v in arrays.items()}], core_ids=[0]).results[0]
    y, kv = r["y_dram"], r["kv_dram"].reshape(3, TS, 2, H, HD)
    heads = (2, H, HD)
    prompt = [kv[g, T - w:T][None] for g, (w, _) in enumerate(DIL)]
    sample = [kv[g, T:TS][:, None] for g in range(3)]
    return (
        y[0:T][None],
        y[T:TS][:, None],
        r["mem_kv_dram"].reshape(2, 1, MEM, *heads),
        layout(r["tail_dram"].T)[None, None],
        r["tail_s_dram"].reshape(1, S, 2, D),
        *(layout(p) for p in prompt),
        *(layout(s) for s in sample),
    )
```
